# Optimizing a Trainium2 kernel written in Bass

```python
import math
import jax, jax.numpy as jnp
from jax import lax
import numpy as np

D_MODEL = 1024
BATCH = 1
SEQ = 256
DEPTH = 1

MEM_LEN = 256
SSM_WIDTH = 512
SSM_GROUP = 16
SSM_GROUPS = SSM_WIDTH // SSM_GROUP
SSM_STATE = 64
DSA_HEADS = 8
DSA_HEAD_DIM = 64
IDX_HEADS = 4
IDX_DIM = 64
IDX_TOPK_MAX = 256
Q_BLOCK = 128
MEM_HEADS = 4
MEM_HEAD_DIM = 128
N_BRANCHES = 3
ROPE_THETA = 10000.0
N_GROUPS = 4
EXPERTS_PER_GROUP = 8
N_EXPERTS = N_GROUPS * EXPERTS_PER_GROUP
TOP_K_EXPERTS = 2
EXPERT_FF = 512
EPS = 1e-6
IN_SPLITS = (SSM_WIDTH, DSA_HEADS * DSA_HEAD_DIM, DSA_HEAD_DIM, DSA_HEAD_DIM, IDX_HEADS * IDX_DIM, IDX_DIM, IDX_HEADS, MEM_HEADS * MEM_HEAD_DIM, N_BRANCHES * D_MODEL)
IN_COLS = sum(IN_SPLITS)


F32 = jnp.float32

def rms_norm(x, g):
    xf = x.astype(F32)
    y = xf * lax.rsqrt(jnp.mean(xf * xf, axis=-1, keepdims=True) + EPS)
    return (y * g.astype(F32)).astype(x.dtype)

def rope_tables(positions, dim):
    inv = 1.0 / (ROPE_THETA ** (jnp.arange(0, dim, 2, dtype=F32) / dim))
    ang = positions.astype(F32)[..., None] * inv
    return jnp.cos(ang), jnp.sin(ang)

def apply_rope(x, cos, sin):
    extra = x.ndim - cos.ndim
    cos = cos.reshape(cos.shape[:2] + (1,) * extra + cos.shape[2:])
    sin = sin.reshape(sin.shape[:2] + (1,) * extra + sin.shape[2:])
    x1, x2 = jnp.split(x.astype(F32), 2, axis=-1)
    out = jnp.concatenate([x1 * cos - x2 * sin, x2 * cos + x1 * sin], axis=-1)
    return out.astype(x.dtype)

def _ssm_combine(e1, e2):
    a1, b1 = e1
    a2, b2 = e2
    return a1 * a2, a2 * b1 + b2

def s5_branch(u, lam_re, lam_im, log_dt, b_re, b_im, c_re, c_im, d_skip, w_glu):
    bsz, seq, _ = u.shape
    uf = u.astype(F32).reshape(bsz, seq, SSM_GROUPS, SSM_GROUP)
    lam = lax.complex(lam_re.astype(F32), lam_im.astype(F32))
    dt = jnp.exp(log_dt.astype(F32))[:, None]
    lam_bar = jnp.exp(lam * dt)
    b = lax.complex(b_re.astype(F32), b_im.astype(F32))
    b_bar = ((lam_bar - 1.0) / lam)[..., None] * b
    bu = jnp.einsum('bsgh,gph->bsgp', uf.astype(jnp.complex64), b_bar)
    a = jnp.broadcast_to(lam_bar, (1, seq) + lam_bar.shape)
    _, states = lax.associative_scan(_ssm_combine, (a, bu), axis=1)
    c = lax.complex(c_re.astype(F32), c_im.astype(F32))
    y = jnp.real(jnp.einsum('bsgp,ghp->bsgh', states, c))
    y = y + d_skip.astype(F32).reshape(SSM_GROUPS, SSM_GROUP) * uf
    y = jax.nn.gelu(y.reshape(bsz, seq, SSM_WIDTH))
    y = y * jax.nn.sigmoid(y @ w_glu.astype(F32))
    return y.astype(u.dtype)

def dsa_branch(q, k, v, qi, ki, wi, pos):
    bsz, seq = pos.shape
    topk = min(IDX_TOPK_MAX, seq // 4)
    nb = seq // Q_BLOCK
    kif = ki.astype(F32)
    gather = jax.vmap(lambda src, idx: src[idx])

    def to_blocks(t):
        t = t.reshape((bsz, nb, Q_BLOCK) + t.shape[2:])
        return jnp.moveaxis(t, 1, 0)

    def block_fn(args):
        qb, qib, wib, posb = args
        sc = jnp.einsum('bqhd,bsd->bqhs', qib.astype(F32), kif) * (IDX_DIM ** -0.5)
        iscore = jnp.einsum('bqh,bqhs->bqs', wib.astype(F32), jax.nn.relu(sc))
        causal = pos[:, None, :] <= posb[:, :, None]
        iscore = jnp.where(causal, iscore, -jnp.inf)
        _, idx = lax.top_k(iscore, topk)
        ks = gather(k, idx).astype(F32)
        vs = gather(v, idx).astype(F32)
        ps = gather(pos, idx)
        s = jnp.einsum('bqhd,bqkd->bqhk', qb.astype(F32), ks) * (DSA_HEAD_DIM ** -0.5)
        valid = (ps <= posb[..., None])[:, :, None, :]
        p = jax.nn.softmax(jnp.where(valid, s, -jnp.inf), axis=-1)
        o = jnp.einsum('bqhk,bqkd->bqhd', p, vs)
        return o.astype(qb.dtype)

    out = lax.map(block_fn, (to_blocks(q), to_blocks(qi), to_blocks(wi), to_blocks(pos)))
    out = jnp.moveaxis(out, 0, 1).reshape(bsz, seq, DSA_HEADS * DSA_HEAD_DIM)
    return out

def memory_branch(qm, km, vm):
    bsz, seq = qm.shape[:2]
    s = jnp.einsum('bshd,bmhd->bhsm', qm.astype(F32), km.astype(F32)) * (MEM_HEAD_DIM ** -0.5)
    p = jax.nn.softmax(s, axis=-1)
    o = jnp.einsum('bhsm,bmhd->bshd', p, vm.astype(F32))
    return o.reshape(bsz, seq, MEM_HEADS * MEM_HEAD_DIM).astype(qm.dtype)

def hier_moe(h, w_group, b_group, w_expert, b_expert, w_gate, w_up, w_down):
    bsz, seq, d = h.shape
    t = h.reshape(-1, d)
    hf = t.astype(F32)
    g_prob = jax.nn.softmax(hf @ w_group.astype(F32) + b_group.astype(F32), axis=-1)
    g_idx = jnp.argmax(g_prob, axis=-1)
    g_gate = jnp.take_along_axis(g_prob, g_idx[:, None], axis=-1)[:, 0]
    e_logits = (hf @ w_expert.astype(F32)).reshape(-1, N_GROUPS, EXPERTS_PER_GROUP) + b_expert.astype(F32)
    e_logits = jnp.take_along_axis(e_logits, g_idx[:, None, None], axis=1)[:, 0]
    e_prob = jax.nn.softmax(e_logits, axis=-1)
    top_p, top_i = lax.top_k(e_prob, TOP_K_EXPERTS)
    top_w = g_gate[:, None] * top_p / jnp.sum(top_p, axis=-1, keepdims=True)
    global_i = g_idx[:, None] * EXPERTS_PER_GROUP + top_i
    combine = jnp.sum(jax.nn.one_hot(global_i, N_EXPERTS, dtype=F32) * top_w[..., None], axis=1)
    out = jnp.zeros(hf.shape, F32)
    for e in range(N_EXPERTS):
        hid = jax.nn.silu(t @ w_gate[e]) * (t @ w_up[e])
        out = out + combine[:, e:e + 1] * (hid @ w_down[e]).astype(F32)
    return out.reshape(bsz, seq, d).astype(h.dtype)

def hybrid_layer(x, mem, positions, g_mix, g_mem, w_in, lam_re, lam_im, log_dt, b_re, b_im, c_re, c_im, d_skip, w_glu, g_q, g_k, g_qm, g_km, w_mem_kv, w_up_ssm, w_up_dsa, w_up_mem, w_out, g_ffn, w_group, b_group, w_expert, b_expert, w_gate, w_up, w_down):
    bsz, seq, _ = x.shape
    mlen = mem.shape[1]
    h = rms_norm(x, g_mix)
    proj = h @ w_in
    offs = [int(o) for o in np.cumsum(IN_SPLITS)[:-1]]
    u_ssm, q, k, v, qi, ki, wi, qm, gates = jnp.split(proj, offs, axis=-1)
    cos_a, sin_a = rope_tables(positions, DSA_HEAD_DIM)
    cos_i, sin_i = rope_tables(positions, IDX_DIM)
    q = apply_rope(rms_norm(q.reshape(bsz, seq, DSA_HEADS, DSA_HEAD_DIM), g_q), cos_a, sin_a)
    k = apply_rope(rms_norm(k, g_k), cos_a, sin_a)
    qi = apply_rope(qi.reshape(bsz, seq, IDX_HEADS, IDX_DIM), cos_i, sin_i)
    ki = apply_rope(ki, cos_i, sin_i)
    wi = wi * (IDX_HEADS ** -0.5)
    qm = rms_norm(qm.reshape(bsz, seq, MEM_HEADS, MEM_HEAD_DIM), g_qm)
    km, vm = jnp.split(rms_norm(mem, g_mem) @ w_mem_kv, 2, axis=-1)
    km = rms_norm(km.reshape(bsz, mlen, MEM_HEADS, MEM_HEAD_DIM), g_km)
    vm = vm.reshape(bsz, mlen, MEM_HEADS, MEM_HEAD_DIM)

    y_ssm = s5_branch(u_ssm, lam_re, lam_im, log_dt, b_re, b_im, c_re, c_im, d_skip, w_glu)
    y_dsa = dsa_branch(q, k, v, qi, ki, wi, positions)
    y_mem = memory_branch(qm, km, vm)

    g_s, g_d, g_m = jnp.split(jax.nn.sigmoid(gates), N_BRANCHES, axis=-1)
    merged = g_s * (y_ssm @ w_up_ssm) + g_d * (y_dsa @ w_up_dsa) + g_m * (y_mem @ w_up_mem)
    x = x + merged @ w_out
    x = x + hier_moe(rms_norm(x, g_ffn), w_group, b_group, w_expert, b_expert, w_gate, w_up, w_down)
    return x

def first_inputs(seed: int = 0) -> dict:
    key = jax.random.key(seed)
    ks = iter(jax.random.split(key, 48))
    L = DEPTH

    def nrm(shape, scale):
        return jax.random.normal(next(ks), shape, F32) * scale

    def gain(shape):
        return 1.0 + 0.02 * jax.random.normal(next(ks), shape, F32)

    x = nrm((BATCH, SEQ, D_MODEL), 1.0)
    mem = nrm((BATCH, MEM_LEN, D_MODEL), 1.0)
    offset = jax.random.randint(next(ks), (BATCH, 1), 0, 1024, dtype=jnp.int32)
    positions = offset + jnp.arange(SEQ, dtype=jnp.int32)[None, :]
    n = jnp.arange(SSM_STATE, dtype=F32)
    lam_re = -0.5 + nrm((L, SSM_GROUPS, SSM_STATE), 0.01)
    lam_im = jnp.pi * n + nrm((L, SSM_GROUPS, SSM_STATE), 0.01)
    log_dt = jax.random.uniform(next(ks), (L, SSM_GROUPS), F32, math.log(1e-3), math.log(1e-1))
    return {
        'x': x,
        'mem': mem,
        'positions': positions,
        'g_mix': gain((L, D_MODEL)),
        'g_mem': gain((L, D_MODEL)),
        'w_in': nrm((L, D_MODEL, IN_COLS), D_MODEL ** -0.5),
        'lam_re': lam_re,
        'lam_im': lam_im,
        'log_dt': log_dt,
        'b_re': nrm((L, SSM_GROUPS, SSM_STATE, SSM_GROUP), (2 * SSM_GROUP) ** -0.5),
        'b_im': nrm((L, SSM_GROUPS, SSM_STATE, SSM_GROUP), (2 * SSM_GROUP) ** -0.5),
        'c_re': nrm((L, SSM_GROUPS, SSM_GROUP, SSM_STATE), SSM_STATE ** -0.5),
        'c_im': nrm((L, SSM_GROUPS, SSM_GROUP, SSM_STATE), SSM_STATE ** -0.5),
        'd_skip': nrm((L, SSM_WIDTH), 1.0),
        'w_glu': nrm((L, SSM_WIDTH, SSM_WIDTH), SSM_WIDTH ** -0.5),
        'g_q': gain((L, DSA_HEAD_DIM)),
        'g_k': gain((L, DSA_HEAD_DIM)),
        'g_qm': gain((L, MEM_HEAD_DIM)),
        'g_km': gain((L, MEM_HEAD_DIM)),
        'w_mem_kv': nrm((L, D_MODEL, 2 * MEM_HEADS * MEM_HEAD_DIM), D_MODEL ** -0.5),
        'w_up_ssm': nrm((L, SSM_WIDTH, D_MODEL), SSM_WIDTH ** -0.5),
        'w_up_dsa': nrm((L, DSA_HEADS * DSA_HEAD_DIM, D_MODEL), (DSA_HEADS * DSA_HEAD_DIM) ** -0.5),
        'w_up_mem': nrm((L, MEM_HEADS * MEM_HEAD_DIM, D_MODEL), (MEM_HEADS * MEM_HEAD_DIM) ** -0.5),
        'w_out': nrm((L, D_MODEL, D_MODEL), D_MODEL ** -0.5),
        'g_ffn': gain((L, D_MODEL)),
        'w_group': nrm((L, D_MODEL, N_GROUPS), D_MODEL ** -0.5),
        'b_group': nrm((L, N_GROUPS), 0.01),
        'w_expert': nrm((L, D_MODEL, N_EXPERTS), D_MODEL ** -0.5),
        'b_expert': nrm((L, N_GROUPS, EXPERTS_PER_GROUP), 0.01),
        'w_gate': nrm((L, N_EXPERTS, D_MODEL, EXPERT_FF), D_MODEL ** -0.5),
        'w_up': nrm((L, N_EXPERTS, D_MODEL, EXPERT_FF), D_MODEL ** -0.5),
        'w_down': nrm((L, N_EXPERTS, EXPERT_FF, D_MODEL), EXPERT_FF ** -0.5),
    }

def first_block(x, mem, positions, g_mix, g_mem, w_in, lam_re, lam_im, log_dt, b_re, b_im, c_re, c_im, d_skip, w_glu, g_q, g_k, g_qm, g_km, w_mem_kv, w_up_ssm, w_up_dsa, w_up_mem, w_out, g_ffn, w_group, b_group, w_expert, b_expert, w_gate, w_up, w_down):
    for l in range(DEPTH):
        x = hybrid_layer(x, mem, positions, g_mix[l], g_mem[l], w_in[l], lam_re[l], lam_im[l], log_dt[l], b_re[l], b_im[l], c_re[l], c_im[l], d_skip[l], w_glu[l], g_q[l], g_k[l], g_qm[l], g_km[l], w_mem_kv[l], w_up_ssm[l], w_up_dsa[l], w_up_mem[l], w_out[l], g_ffn[l], w_group[l], b_group[l], w_expert[l], b_expert[l], w_gate[l], w_up[l], w_down[l])
    return x


DEPTH_2 = 2

SWA_HEADS = 8
SWA_KV_HEADS = 2
SWA_HEAD_DIM = 64
SWA_WINDOW = 128
SWA_BLOCK = 128
GLA_HEADS = 4
GLA_DK = D_MODEL // 2 // GLA_HEADS
GLA_DV = D_MODEL // GLA_HEADS
GLA_GATE_RANK = 16
GLA_TAU = 16.0
GLA_CHUNK = 64
D_FF = 2816

SWA_Q_W = SWA_HEADS * SWA_HEAD_DIM
SWA_KV_W = SWA_KV_HEADS * SWA_HEAD_DIM
GLA_K_W = GLA_HEADS * GLA_DK
GLA_V_W = GLA_HEADS * GLA_DV
IN_SPLITS_2 = (SWA_Q_W, SWA_KV_W, SWA_KV_W, GLA_K_W, GLA_K_W, GLA_V_W, GLA_V_W, GLA_GATE_RANK, D_MODEL, D_MODEL)
IN_COLS_2 = sum(IN_SPLITS_2)


def rmsnorm(x, g):
    xf = x.astype(jnp.float32)
    y = xf * lax.rsqrt(jnp.mean(xf * xf, axis=-1, keepdims=True) + EPS)
    return (y * g.astype(jnp.float32)).astype(x.dtype)

def swiglu(h, w_gate, w_up, w_down):
    return (jax.nn.silu(h @ w_gate) * (h @ w_up)) @ w_down

def split_cols(z, sizes):
    idx = np.cumsum(np.array(sizes))[:-1].tolist()
    return jnp.split(z, idx, axis=-1)

def rope_tables_2(T):
    inv_freq = ROPE_THETA ** (-jnp.arange(0, SWA_HEAD_DIM, 2, dtype=jnp.float32) / SWA_HEAD_DIM)
    ang = jnp.arange(T, dtype=jnp.float32)[:, None] * inv_freq[None, :]
    return jnp.cos(ang), jnp.sin(ang)

def apply_rope_2(x, cos, sin):
    x1, x2 = jnp.split(x, 2, axis=-1)
    c = cos[None, :, None, :]
    s = sin[None, :, None, :]
    return jnp.concatenate([x1 * c - x2 * s, x2 * c + x1 * s], axis=-1)

def swa_attention(q, k, v, q_gain, k_gain, sinks, cos, sin):
    B, T = q.shape[0], q.shape[1]
    G = SWA_HEADS // SWA_KV_HEADS
    nb = T // SWA_BLOCK
    q = apply_rope_2(rmsnorm(q, q_gain).astype(jnp.float32), cos, sin)
    k = apply_rope_2(rmsnorm(k, k_gain).astype(jnp.float32), cos, sin)
    v = v.astype(jnp.float32)
    q = q.reshape(B, nb, SWA_BLOCK, SWA_KV_HEADS, G, SWA_HEAD_DIM)
    k = k.reshape(B, nb, SWA_BLOCK, SWA_KV_HEADS, SWA_HEAD_DIM)
    v = v.reshape(B, nb, SWA_BLOCK, SWA_KV_HEADS, SWA_HEAD_DIM)

    def band(t):
        prev = jnp.pad(t[:, :-1], ((0, 0), (1, 0), (0, 0), (0, 0), (0, 0)))
        return jnp.concatenate([prev, t], axis=2)

    kb, vb = band(k), band(v)
    s = jnp.einsum('bnqhgd,bnkhd->bnhgqk', q, kb) * (SWA_HEAD_DIM ** -0.5)
    i = jnp.arange(SWA_BLOCK)[:, None]
    j = jnp.arange(2 * SWA_BLOCK)[None, :]
    rel = i + SWA_BLOCK - j
    blk = jnp.arange(nb)[:, None, None]
    valid = (rel >= 0) & (rel < SWA_WINDOW) & ((blk > 0) | (j >= SWA_BLOCK))
    s = jnp.where(valid[None, :, None, None], s, -jnp.inf)
    sink = sinks.astype(jnp.float32).reshape(1, 1, SWA_KV_HEADS, G, 1, 1)
    m = jnp.maximum(jnp.max(s, axis=-1, keepdims=True), sink)
    p = jnp.exp(s - m)
    denom = jnp.sum(p, axis=-1, keepdims=True) + jnp.exp(sink - m)
    o = jnp.einsum('bnhgqk,bnkhd->bnqhgd', p / denom, vb)
    return o.reshape(B, T, SWA_Q_W)

def gla_attention(q, k, v, log_a):
    B, T = q.shape[0], q.shape[1]
    nc = T // GLA_CHUNK

    def chunks(t, d):
        return t.astype(jnp.float32).reshape(B, nc, GLA_CHUNK, GLA_HEADS, d).transpose(1, 0, 3, 2, 4)

    qc = chunks(q, GLA_DK) * (GLA_DK ** -0.5)
    kc = chunks(k, GLA_DK)
    vc = chunks(v, GLA_DV)
    gc = chunks(log_a, GLA_DK)
    causal = jnp.tril(jnp.ones((GLA_CHUNK, GLA_CHUNK), dtype=bool))[:, :, None]

    def step(S, inp):
        qi, ki, vi, gi = inp
        b = jnp.cumsum(gi, axis=-2)
        b_last = b[:, :, -1:, :]
        o_inter = jnp.einsum('bhtc,bhcv->bhtv', qi * jnp.exp(b), S)
        diff = b[:, :, :, None, :] - b[:, :, None, :, :]
        decay = jnp.exp(jnp.where(causal, diff, -jnp.inf))
        attn = jnp.einsum('bhtsc,bhsc->bhts', qi[:, :, :, None, :] * decay, ki)
        o_intra = jnp.einsum('bhts,bhsv->bhtv', attn, vi)
        S = jnp.exp(b_last[:, :, 0, :])[..., None] * S + jnp.einsum('bhsc,bhsv->bhcv', ki * jnp.exp(b_last - b), vi)
        return S, o_inter + o_intra

    S0 = jnp.zeros((B, GLA_HEADS, GLA_DK, GLA_DV), jnp.float32)
    _, o = lax.scan(step, S0, (qc, kc, vc, gc))
    return o.transpose(1, 0, 3, 2, 4).reshape(B, T, GLA_HEADS, GLA_DV)

def second_inputs(seed: int = 0) -> dict:
    key = jax.random.key(seed)
    ks = jax.random.split(key, 24)
    L, D = DEPTH_2, D_MODEL

    def w(k, shape, fan_in):
        return jax.random.normal(k, shape, jnp.float32) * (fan_in ** -0.5)

    def gain(k, shape):
        return 1.0 + 0.02 * jax.random.normal(k, shape, jnp.float32)

    return {
        "x": jax.random.normal(ks[0], (BATCH, SEQ, D), jnp.float32),
        "ffn1_norm": gain(ks[1], (L, D)),
        "ffn1_w_gate": w(ks[2], (L, D, D_FF), D),
        "ffn1_w_up": w(ks[3], (L, D, D_FF), D),
        "ffn1_w_down": w(ks[4], (L, D_FF, D), D_FF),
        "mix_norm": gain(ks[5], (L, D)),
        "w_in": w(ks[6], (L, D, IN_COLS_2), D),
        "swa_q_norm": gain(ks[7], (L, SWA_HEAD_DIM)),
        "swa_k_norm": gain(ks[8], (L, SWA_HEAD_DIM)),
        "swa_sinks": 0.5 * jax.random.normal(ks[9], (L, SWA_HEADS), jnp.float32),
        "gla_w_gate": w(ks[10], (L, GLA_GATE_RANK, GLA_K_W), GLA_GATE_RANK),
        "gla_gate_bias": 0.1 * jax.random.normal(ks[11], (L, GLA_K_W), jnp.float32),
        "gla_out_norm": gain(ks[12], (L, GLA_V_W)),
        "w_proj_a": w(ks[13], (L, SWA_Q_W, D), SWA_Q_W),
        "w_proj_b": w(ks[14], (L, GLA_V_W, D), GLA_V_W),
        "w_out": w(ks[15], (L, D, D), D),
        "ffn2_norm": gain(ks[16], (L, D)),
        "ffn2_w_gate": w(ks[17], (L, D, D_FF), D),
        "ffn2_w_up": w(ks[18], (L, D, D_FF), D),
        "ffn2_w_down": w(ks[19], (L, D_FF, D), D_FF),
    }

def second_block(x, ffn1_norm, ffn1_w_gate, ffn1_w_up, ffn1_w_down, mix_norm, w_in,
              swa_q_norm, swa_k_norm, swa_sinks, gla_w_gate, gla_gate_bias, gla_out_norm,
              w_proj_a, w_proj_b, w_out, ffn2_norm, ffn2_w_gate, ffn2_w_up, ffn2_w_down):
    B, T = x.shape[0], x.shape[1]
    cos, sin = rope_tables_2(T)
    for l in range(DEPTH_2):
        h = rmsnorm(x, ffn1_norm[l])
        x = x + 0.5 * swiglu(h, ffn1_w_gate[l], ffn1_w_up[l], ffn1_w_down[l])

        h = rmsnorm(x, mix_norm[l])
        z = h @ w_in[l]
        q_a, k_a, v_a, q_b, k_b, v_b, r_b, g_lr, gate_a, gate_b = split_cols(z, IN_SPLITS_2)

        o_a = swa_attention(q_a.reshape(B, T, SWA_HEADS, SWA_HEAD_DIM),
                            k_a.reshape(B, T, SWA_KV_HEADS, SWA_HEAD_DIM),
                            v_a.reshape(B, T, SWA_KV_HEADS, SWA_HEAD_DIM),
                            swa_q_norm[l], swa_k_norm[l], swa_sinks[l], cos, sin).astype(x.dtype)

        log_a = jax.nn.log_sigmoid((g_lr @ gla_w_gate[l] + gla_gate_bias[l]).astype(jnp.float32)) / GLA_TAU
        o_b = gla_attention(q_b.reshape(B, T, GLA_HEADS, GLA_DK),
                            k_b.reshape(B, T, GLA_HEADS, GLA_DK),
                            v_b.reshape(B, T, GLA_HEADS, GLA_DV),
                            log_a.reshape(B, T, GLA_HEADS, GLA_DK))
        o_b = rmsnorm(o_b, gla_out_norm[l].reshape(GLA_HEADS, GLA_DV)).reshape(B, T, GLA_V_W).astype(x.dtype)
        o_b = o_b * jax.nn.silu(r_b)

        y_a = o_a @ w_proj_a[l]
        y_b = o_b @ w_proj_b[l]
        merged = jax.nn.sigmoid(gate_a) * y_a + jax.nn.sigmoid(gate_b) * y_b
        x = x + merged @ w_out[l]

        h = rmsnorm(x, ffn2_norm[l])
        x = x + 0.5 * swiglu(h, ffn2_w_gate[l], ffn2_w_up[l], ffn2_w_down[l])
    return x


def setup_inputs(seed=0):
    out = dict(first_inputs(seed))
    for name, value in second_inputs(seed + 1).items():
        if name != "x":
            out[name + "_2"] = value
    return out


def reference(
    x, mem, positions, g_mix, g_mem, w_in, lam_re, lam_im, log_dt, b_re, b_im, c_re, c_im,
    d_skip, w_glu, g_q, g_k, g_qm, g_km, w_mem_kv, w_up_ssm, w_up_dsa, w_up_mem, w_out, g_ffn,
    w_group, b_group, w_expert, b_expert, w_gate, w_up, w_down, ffn1_norm_2, ffn1_w_gate_2,
    ffn1_w_up_2, ffn1_w_down_2, mix_norm_2, w_in_2, swa_q_norm_2, swa_k_norm_2, swa_sinks_2,
    gla_w_gate_2, gla_gate_bias_2, gla_out_norm_2, w_proj_a_2, w_proj_b_2, w_out_2, ffn2_norm_2,
    ffn2_w_gate_2, ffn2_w_up_2, ffn2_w_down_2,
):
    x = first_block(
        x, mem, positions, g_mix, g_mem, w_in, lam_re, lam_im, log_dt, b_re, b_im, c_re, c_im,
        d_skip, w_glu, g_q, g_k, g_qm, g_km, w_mem_kv, w_up_ssm, w_up_dsa, w_up_mem, w_out,
        g_ffn, w_group, b_group, w_expert, b_expert, w_gate, w_up, w_down,
    )
    return second_block(
        x, ffn1_norm_2, ffn1_w_gate_2, ffn1_w_up_2, ffn1_w_down_2, mix_norm_2, w_in_2,
        swa_q_norm_2, swa_k_norm_2, swa_sinks_2, gla_w_gate_2, gla_gate_bias_2, gla_out_norm_2,
        w_proj_a_2, w_proj_b_2, w_out_2, ffn2_norm_2, ffn2_w_gate_2, ffn2_w_up_2, ffn2_w_down_2,
    )


_drawn_inputs = setup_inputs


def setup_inputs(seed=0):
    import zlib

    import numpy as np

    out = dict(_drawn_inputs(seed))
    spreads = {}
    factors = {'g_mem': 2.828,
     'lam_re': 8.0,
     'g_q': 3.005,
     'g_k': 4.494,
     'g_qm': 4.674,
     'g_km': 3.171,
     'b_group': 3.103,
     'b_expert': 3.42,
     'ffn1_norm_2': 4.233,
     'mix_norm_2': 3.057,
     'swa_q_norm_2': 8.0,
     'swa_k_norm_2': 8.0,
     'swa_sinks_2': 4.661,
     'gla_gate_bias_2': 2.988,
     'gla_out_norm_2': 6.419,
     'ffn2_norm_2': 5.13}
    for name, (base, spread) in spreads.items():
        noise = np.random.default_rng([zlib.crc32(name.encode()), seed]).standard_normal(out[name].shape)
        drawn = base * np.exp(spread * noise) if base else spread * noise
        out[name] = __import__('jax').numpy.asarray(drawn.astype(out[name].dtype))
    for name, factor in factors.items():
        out[name] = (out[name] * factor).astype(out[name].dtype)
    return out
```

```python
from contextlib import ExitStack

import numpy as np
import concourse.bass as bass
from concourse import mybir

F32 = mybir.dt.float32
F32R = mybir.dt.float32r
BF16 = mybir.dt.bfloat16
I32 = mybir.dt.int32
ALU = mybir.AluOpType
ACT = mybir.ActivationFunctionType
AX = mybir.AxisListType.X

P = 128
D = 1024
KB = D // P
SEQ = 256
NT = SEQ // P
EPS = 1e-6
NEG = -1e30
GONE = -3e38
TWO_PI = 6.283185307179586
ROUND = 12582912.0
COARSE = 768.0

SSM_TILES = 16
EXPERTS = 32
GROUPS = 4
LAYERS = 2
FF2 = 2816
CHUNK_FF = 512
FULL_CHUNKS = FF2 // CHUNK_FF
TAIL_FF = FF2 - FULL_CHUNKS * CHUNK_FF
GLA_CHUNK = 64
TOPK = SEQ // 4

RAW = 3
SPLIT = 3
UNIT = 2048

IN1 = dict(u=(0, 512), q=(512, 512), kvi=(1024, 452), qm=(1476, 512), gate=(1988, 3072))
IN2 = dict(qa=(0, 512), kva=(512, 256), qb=(768, 512), kb=(1280, 512), vb=(1792, 1024),
           rb=(2816, 1024), glr=(3840, 16), ga=(3856, 1024), gb=(4880, 1024))


SIGNALS = ("summed meansq rstd rows turned ssm_act ssm_vec ssm_params ssm_weights trig angle rope_angle "
           "rope_trig u_rows scanned rotated mixed gelu_in gelu gelu_split evacuated heads heads_turned values "
           "relued maxed exped probs probs_turned branch gates residual route_in route silu hidden "
           "hidden_turned gate_ln decay decay_exp decayed gk_turned masked state").split()
CONSTS = 16 * 34
SSM_LOADS = 16 * 26
VECTOR_STEPS_LAYER = 90
SCALAR_STEPS_LAYER = 32


class Order:

    def __init__(self):
        self.n, self.at, self.open, self.per = 0, {}, [], {}

    def event(self, name, by=1):
        assert name not in self.at, name
        self.at[name] = (self.n, tuple(x for x, _ in self.open))
        self.n += by

    def begin(self, loop):
        self.open.append((loop, self.n))

    def end(self, trips):
        loop, start = self.open.pop()
        self.per[loop] = self.n - start
        self.n = start + self.per[loop] * trips

    def number(self, name, regs):
        n, loops = self.at[name]
        for x in loops:
            n = regs[x] * self.per[x] + n
        return n


class Tally:

    def __init__(self):
        self.n, self.open = 0, []

    def next(self):
        self.n += 1
        return self.value()

    def value(self, back=0):
        value = self.n + back
        for reg, per, _ in self.open:
            value = reg * per + value
        return value

    def begin(self, reg, per):
        self.open.append((reg, per, self.n))

    def end(self, trips):
        _, per, start = self.open.pop()
        assert self.n - start == per, ("steps in a trip", self.n - start, per)
        self.n = start + per * trips


def plan():
    units, shape = Order(), {}
    marks = {s: Order() for s in SIGNALS}
    banks, fills, bank_of = [Order() for _ in range(8)], [], {}

    def unit(name, nk, w):
        units.event(name)
        shape[name] = (nk, w)

    def fill(name, b):
        banks[b].event(name)
        bank_of[name] = b
        fills.append(name)

    def begin(loop):
        units.begin(loop)
        for b in (*banks, *marks.values()):
            b.begin(loop)

    def end(trips):
        units.end(trips)
        for b in (*banks, *marks.values()):
            b.end(trips)

    def mark(signal, *events):
        for e in events:
            marks[signal].event(e)

    def norm(tag):
        mark("summed", (tag, 0), (tag, 1)); mark("meansq", tag); mark("rstd", tag)
        turn_rows(tag)

    def turn_rows(tag):
        mark("rows", (tag, 0), (tag, 1))
        mark("turned", *((tag, t, hh) for t in range(2) for hh in range(2)))

    def panel(name, w=512, halves=2):
        for kh in range(halves):
            unit((name, kh), 4, w)

    norm("mem"); norm("x")
    for t in range(2):
        for hh in range(2):
            fill(("memT", t, hh), 2 * t + hh)
    panel("km"); panel("vm")
    for i, n in enumerate(("km", "vm")):
        for t in range(2):
            fill((n, t), 4 + 2 * i + t)
    for t in range(2):
        for hh in range(2):
            fill(("xT", t, hh), 2 * t + hh)
    mark("ssm_act", 0, 1); mark("ssm_vec", 0); mark("ssm_params", "b")
    mark("ssm_weights", 0, 1, 2, 3)
    mark("trig", 0, 1, 2, 3)
    mark("angle", 0, 1, 2, 3)
    mark("rope_angle", 0); mark("rope_trig", 0)
    mark("u_rows", 0, 1)
    mark("scanned", *range(SSM_TILES)); mark("rotated", *range(SSM_TILES)); mark("mixed", *range(SSM_TILES))
    mark("gelu_in", 0, 1); mark("gelu", 0, 1); mark("gelu_split", 0, 1)
    mark("meansq", "heads1"); mark("rstd", "heads1")
    mark("evacuated", *((n, t) for n in ("km", "vm", "kvi", "q", "qm") for t in range(2)))
    mark("evacuated", ("glu", 0), ("glu", 1))
    mark("heads", "dq", "dk", "mq", "mk")
    panel("u")
    fill(("uT", 0), 4); fill(("uT", 1), 5)
    for i in range(4):
        fill(("ssmT", i), i)
    for n in ("kvi", "q", "qm"):
        panel(n, IN1[n][1])
    for h in range(2):
        fill(("y", h), 6 + h)
    for T in range(SSM_TILES):
        fill(("bu", T), T % 4)
        if T % 4 == 0 and T < 12:
            for t in range(2):
                fill((("kvi", "q", "qm")[T // 4], t), 4 + t)
    for c in range(6):
        panel(("gate", c))
        for t in range(2):
            fill(("gate", c, t), 4 + 2 * (c % 2) + t)
        if c == 0:
            unit(("glu", 0), 4, 512)
            fill(("glu", 0), 0); fill(("glu", 1), 1)
    turn = [0]

    def small(name):
        fill(name, turn[0] % 4)
        turn[0] += 1
    turn[0] = 2
    for t in range(2):
        small(("dqT", t)); small(("dkT", t))
    for t in range(2):
        for p in range(2):
            small(("isc", t, p))

    mark("heads_turned", ("dqT", 0), ("dkT", 0), ("dqT", 1), ("dkT", 1))
    mark("values", "dsa")
    mark("relued", (0, 0), (0, 1), (1, 0), (1, 1))

    def attention(tag, pairs):
        for t in range(2):
            mark("maxed", (tag, t)); mark("exped", (tag, t)); mark("probs", (tag, t))
            mark("probs_turned", *((tag, t, p) for p in range(pairs)))
            mark("branch", (tag, t))
            for p in range(pairs):
                small((tag, "S", t, p))
            for p in range(pairs):
                small((tag, "PT", t, p))
            small((tag, "O", t))
    mark("branch", "ssm")
    attention("dsa", 4)
    mark("heads_turned", ("mqT", 0), ("mkT", 0), ("mqT", 1), ("mkT", 1))
    for t in range(2):
        small(("mqT", t)); small(("mkT", t))
    attention("mem", 2)
    mark("gates", "ssm", "dsa", "mem")
    for i, br in enumerate(("ssm", "dsa", "mem")):
        for c in range(2):
            unit(("up", br, c), 4, 512)
            for t in range(2):
                fill(("up", br, c, t), 4 * (i % 2) + 2 * c + t)
    turn_rows("m")
    for t in range(2):
        for hh in range(2):
            fill(("mT", t, hh), 4 + 2 * t + hh)
    for c in range(2):
        panel(("wo", c))
        for t in range(2):
            fill(("wo", c, t), 2 * c + t)
    mark("residual", ("wo", 0), ("wo", 1))
    norm("f")
    mark("route_in", 0, 1); mark("route", "exp", "expert")
    for t in range(2):
        for hh in range(2):
            fill(("fT", t, hh), 4 + 2 * t + hh)
    for t in range(2):
        fill(("rt", t), 2 + t)

    def gate_up(name, tag, w):
        for kh in range(2 if w == 512 else 1):
            unit((name, tag, kh), 4 if w == 512 else 8, w)

    def glu_loop(tag, loop, trips, tail):
        for t in range(2):
            for c in range(2):
                fill((tag, "acc", t, c), 4 + 2 * t + c)
        gate_up("g", (tag, "first"), 512)
        for t in range(2):
            fill((tag, "first", "g", t), t)
        mark("silu", (tag, "first", 0), (tag, "first", 1))
        begin(loop)
        body(tag, "loop", 512)
        end(trips)
        if tail:
            body(tag, "last", tail)
            last(tag, tail)
        else:
            last(tag, 512)
        mark("residual", (tag, 0), (tag, 1))

    def body(tag, which, w_next):
        k = (tag, which)
        mark("hidden", (*k, 0), (*k, 1)); mark("silu", (*k, 0), (*k, 1)); mark("hidden_turned", (*k, 0), (*k, 1))
        gate_up("u", k, 512)
        for t in range(2):
            fill((*k, "u", t), 2 + t)
        gate_up("g", k, w_next)
        for t in range(2):
            fill((*k, "g", t), t)
        for t in range(2):
            fill((*k, "hT", t), 2 + t)
        for c in range(2):
            unit(("d", k, c), 4, 512)

    def last(tag, w):
        k = (tag, "end")
        mark("hidden", (*k, 0), (*k, 1)); mark("hidden_turned", (*k, 0), (*k, 1))
        gate_up("u", k, w)
        for t in range(2):
            fill((*k, "u", t), 2 + t)
        for t in range(2):
            fill((*k, "hT", t), 2 + t)
        for c in range(2):
            unit(("d", k, c), w // P, 512)

    glu_loop("moe", "moe", EXPERTS - 1, 0)

    begin("layer")
    norm("n1")
    for t in range(2):
        for hh in range(2):
            fill(("n1T", t, hh), 2 * t + hh)
    glu_loop("ff1", "ff1", FULL_CHUNKS - 1, TAIL_FF)
    norm("n2")
    mark("evacuated", *((n, t) for n in ("qa", "kva") for t in range(2)))
    mark("evacuated", "qbT", "kbT", "glrT")
    mark("meansq", "heads2"); mark("rstd", "heads2")
    mark("heads", "sq", "sk")
    mark("heads_turned", ("sqT", 0), ("sqT", 1), ("skT", 0))
    mark("values", "swa")
    mark("gate_ln", 0); mark("decay", 0, 1, 2); mark("decay_exp", *range(4)); mark("decayed", "ku", "qq", "q", "k")
    mark("evacuated", *((n, c, t) for n in ("vb",) for c in range(2) for t in range(2)))
    mark("gk_turned", 0, 1); mark("masked", 0, 1); mark("state", *range(3))
    mark("evacuated", *(("ob", t, hp) for t in range(2) for hp in range(2)))
    mark("gates", "rb", "ga", "gb")
    for t in range(2):
        for hh in range(2):
            fill(("n2T", t, hh), 2 * t + hh)
    panel("qa")
    for t in range(2):
        fill(("qa", t), 4 + t)
    unit(("kva", 0), 8, 256)
    for t in range(2):
        fill(("kva", t), 6 + t)
    turn[0] = 0
    for t in range(2):
        small(("sqT", t))
    small(("skT", 0))
    panel("qb")
    fill(("qbT", 0), 4); fill(("qbT", 1), 5)
    panel("kb")
    fill(("kbT", 0), 6); fill(("kbT", 1), 7)
    unit(("glr", 0), 8, 16)
    small(("glrT", 0))
    for i in range(2):
        small(("lgT", i))
    for i, n in enumerate(("vb", "rb", "ga", "gb")):
        for c in range(2):
            panel((n, c))
            for t in range(2):
                fill((n, c, t), 4 + 2 * (c % 2) + t)
    attention("swa", 4)
    for t in range(2):
        small(("gkT", t))
    for t in range(2):
        small(("A", t))
    for c in range(3):
        for hp in range(2):
            small(("kv", c, hp))
    turn[0] = 0
    for t in range(2):
        for hp in range(2):
            fill(("ob", t, hp), 4 + 2 * t + hp)
    norm("o")
    for t in range(2):
        for hh in range(2):
            fill(("oT", t, hh), 2 * t + hh)
    for c in range(2):
        unit(("pa", c), 4, 512)
        for t in range(2):
            fill(("pa", c, t), 4 + 2 * c + t)
    for c in range(2):
        panel(("pb", c))
        for t in range(2):
            fill(("pb", c, t), 2 * c + t)
    turn_rows("m2")
    for t in range(2):
        for hh in range(2):
            fill(("m2T", t, hh), 4 + 2 * t + hh)
    for c in range(2):
        panel(("wo2", c))
        for t in range(2):
            fill(("wo2", c, t), 2 * c + t)
    mark("residual", ("wo2", 0), ("wo2", 1))
    norm("n3")
    for t in range(2):
        for hh in range(2):
            fill(("n3T", t, hh), 4 + 2 * t + hh)
    glu_loop("ff2", "ff2", FULL_CHUNKS - 1, TAIL_FF)
    end(LAYERS)
    assert units.per["layer"] % (RAW * SPLIT // 3) == 0 and units.per["layer"] % 6 == 0, units.per
    return units, shape, banks, bank_of, marks


def bass_hybrid_moe_then_swa_gla(nc, A, out, upto=None):
    units, unit_shape, banks, bank_of, marks = plan()
    unit_names = list(units.at)

    with ExitStack() as ctx:
        def sbuf(name, shape, dt=F32):
            return ctx.enter_context(nc.sbuf_tensor(name, shape, dt))

        def semaphore(name):
            return ctx.enter_context(nc.semaphore(name))

        raw = sbuf("raw", [P, RAW, UNIT])
        w_hi = sbuf("w_hi", [P, SPLIT, UNIT], F32R)
        w_lo = sbuf("w_lo", [P, SPLIT, UNIT], F32R)
        a_hi = sbuf("a_hi", [P, KB, SEQ], F32R)
        a_lo = sbuf("a_lo", [P, KB, SEQ], F32R)
        y_hi = sbuf("y_hi", [P, 3, 4, SEQ], F32R)
        y_lo = sbuf("y_lo", [P, 3, 4, SEQ], F32R)
        x_sb = sbuf("x_sb", [P, NT, D])
        xn = sbuf("xn", [P, NT, D])
        C_SIZE = 1048
        C = sbuf("C", [P, C_SIZE])
        W_SIZE = 19304
        W = sbuf("W", [P, W_SIZE])
        zero_b = sbuf("zero_b", [P, P], BF16)
        half_pi = sbuf("half_pi", [P, 2])
        posi = sbuf("posi", [P, 2], I32)
        ps = ctx.enter_context(nc.psum_tensor("ps", [P, 8, 512], F32))

        used = [0]

        def const(n):
            used[0] += n
            assert used[0] <= C_SIZE
            return C[:, used[0] - n:used[0]]

        ident = const(P)
        gain = {n: const(KB) for n in ("mem", "x", "f")}
        gain2 = {n: const(LAYERS * KB).rearrange("p (l k) -> p l k", k=KB) for n in ("n1", "n2", "n3", "o")}
        swa_gain = const(LAYERS * 2 * 64).rearrange("p (l a d) -> p l a d", a=2, d=64)
        sinks = const(LAYERS * 8).rearrange("p (l h) -> p l h", h=8)
        gate_bias = const(LAYERS * 4).rearrange("p (l m) -> p l m", m=4)
        d_skip = const(4)
        w_route = const(KB * 36).rearrange("p (k n) -> p k n", n=36)
        b_route = const(36)
        pos_col = const(2)
        first_key = const(40)
        st_ss = const(2)
        st_v = const(2)
        st_rstd = const(2)
        comb = const(2 * EXPERTS).rearrange("p (t e) -> p t e", e=EXPERTS)
        comb4 = comb[:, 0, 0:16].rearrange("p (h c) -> p h c", c=4)
        hs = const(40)
        hr = const(40)
        mx = const(8)
        sm = const(8)
        rs = const(8)
        snk = const(8)

        def area(off, *shape):
            n = int(np.prod(shape))
            assert off + n <= W_SIZE, (off, shape)
            v = W[:, off:off + n]
            if len(shape) == 2:
                return v.rearrange("p (a b) -> p a b", b=shape[1])
            if len(shape) == 3:
                return v.rearrange("p (a b c) -> p a b c", b=shape[1], c=shape[2])
            if len(shape) == 4:
                return v.rearrange("p (a b c d) -> p a b c d", b=shape[1], c=shape[2], d=shape[3])
            return v

        o = 0
        o_q = o; q_sb = area(o, 2, 512); o += 1024
        o_kvi = o; kvi = area(o, 2, 452); o += 904
        o_qm = o; qm_sb = area(o, 2, 512); o += 1024
        km_sb = area(o, 2, 512); o += 1024
        vm_sb = area(o, 2, 512); o += 1024
        rope1 = area(o, 2, 2, 64); o += 256
        t_row = area(o, SEQ); o += 256
        pos_row = area(o, SEQ); o += 256
        g_q1 = area(o, 64); g_k1 = area(o + 64, 64); g_qm1 = area(o + 128, P); g_km1 = area(o + 256, P); o += 384
        inv_freq = area(o, 32); o += 32
        base1 = o
        cos_t = area(o, SSM_TILES, SEQ); o_cos = o; o += 4096
        sin_t = area(o, SSM_TILES, SEQ); o_sin = o; o += 4096
        full_x = area(o, KB, SEQ)
        bb = area(o, 2, 4, P); o += 1024
        cc = area(o, 2, SSM_TILES, 32); o += 1024
        o_scan = o
        s_rot = area(o, 2, 2, SEQ); o += 1024
        s_out = area(o, 2, SEQ); o += 512
        par = area(o, 12, SSM_TILES); o += 192
        u_f = area(o, 4, SEQ); u_flat = area(o, 1024); o += 1024
        rope_tmp = area(o, 2, 64); o += 128
        assert o <= W_SIZE, o
        pos_row_i = area(o_sin, SEQ).bitcast(I32)
        full1 = area(o_cos, KB, SEQ)
        bn = area(o_q, 2, SSM_TILES, 32)
        cn = area(o_qm, 2, 4, P)
        bsc = area(o_scan, 2, SSM_TILES, 32)
        y_g = area(o_scan, 4, SEQ)
        sc_a = xn[:, 0, 0:512].rearrange("p (a b) -> p a b", b=SEQ)
        sc_b = xn[:, 0, 512:1024].rearrange("p (a b) -> p a b", b=SEQ)
        sc_p = xn[:, 1, 0:512].rearrange("p (a b) -> p a b", b=SEQ)
        o = base1
        gates1 = area(o, 2, 6, 512); o += 6144
        qT = area(o, 4, SEQ); o += 1024
        kT = area(o, 4, SEQ); o += 1024
        key_bias = area(o_q, 2, SEQ)
        vpad = area(o_q + 512, 2, 2, P)
        o_P = o; probs = area(o, 8, SEQ); o += 2048
        relu = area(o_P, 4, 2, SEQ)
        kdup = area(o_P, 2, 2, P)
        o_pT = o; probsT = area(o, 2, 8, P); o += 2048
        isc = area(o_pT, 2, SEQ)
        allow = area(o_pT + 512, 2, SEQ)
        top8 = area(o_pT + 1024, 8)
        scr1 = xn[:, 0, :]
        gated = area(o_P, 512)
        assert o <= W_SIZE, o
        h_full = area(o_cos, KB, SEQ)
        sil = area(o_cos + 2048, 2, 512)
        hid = area(o_cos + 3072, 2, 512)
        rt = area(o_cos + 4096, 2, 36)

        def rts(i, n):
            return area(o_cos + 4200 + 64 * i, 2, n)
        o = 0
        rope2 = area(o, 2, 2, 64); o += 256
        swa_bias = area(o, 2, SEQ); o += 512
        reset = area(o, SEQ); o += 256
        gla_mask = area(o, P); o += 128
        wgl = area(o, 512); o += 512
        o_qa = o; qa_sb = area(o, 2, 512); o += 1024
        kk = area(o_qa, 2, 512)
        kva = area(o, 2, 256); o += 512
        glrT = area(o, SEQ)
        vb = area(o, 2, 1024); o += 2048
        rb = area(o, 2, 1024); o += 2048
        gab = area(o, 2, 2, 1024); o += 4096
        qbT = area(o, 4, SEQ); o += 1024
        kbT = area(o, 4, SEQ); o += 1024
        o_l = o
        qT2 = area(o, 4, SEQ); kT2 = area(o + 1024, 2, SEQ); vpad2 = area(o + 1536, 2, 2, 2, P)
        probsT2 = area(o + 2560, 2, 8, P); kdup2 = area(o + 2560, 2, 2, P)
        scr2 = area(o + 4608, 1024)
        gb_ = area(o + 4608, 4, SEQ)
        qqT = area(o, 4, SEQ)
        state = area(o + 1024, 3, 4, SEQ)
        am = area(o + 4608, 2, 4, P)
        probs2 = xn[:, :, :].rearrange("p a (h s) -> p (a h) s", s=SEQ)
        etmp = xn[:, 0, :].rearrange("p (a b) -> p a b", b=SEQ)
        kuT = xn[:, 1, :].rearrange("p (a b) -> p a b", b=SEQ)
        h_full2 = area(o, KB, SEQ)
        sil2 = area(o + 2048, 2, 512)
        hid2 = area(o + 3072, 2, 512)

        done = {s: semaphore(s) for s in SIGNALS}
        bank_filled = [semaphore(f"bank_filled{b}") for b in range(8)]
        bank_freed = [semaphore(f"bank_freed{b}") for b in range(8)]
        weights_loaded = [semaphore(f"weights_loaded{i}") for i in range(RAW)]
        hi_split = semaphore("hi_split")
        lo_split = semaphore("lo_split")
        unit_used = semaphore("unit_used")
        x_loaded = semaphore("x_loaded")
        mem_loaded = semaphore("mem_loaded")
        const_loaded = semaphore("const_loaded")
        ssm_loaded = semaphore("ssm_loaded")
        ssm_zeroed = semaphore("ssm_zeroed")
        zeroed = semaphore("zeroed")
        block2_loaded = semaphore("block2_loaded")
        wgl_loaded = semaphore("wgl_loaded")
        stored = semaphore("stored")
        vector_step = semaphore("vector_step")
        scalar_step = semaphore("scalar_step")
        pool_step = semaphore("pool_step")
        pe_step = semaphore("pe_step")

        class Engine:

            def __init__(self, counts_steps=False):
                self.regs, self.cursor = {}, 0
                self.step = Tally() if counts_steps else None

            def nth(self, signal, event):
                return marks[signal].number(event, self.regs) + 1

            def fills(self, name):
                return banks[bank_of[name]].number(name, self.regs) + 1

            def psum(self, name):
                return ps[:, bank_of[name], :]

            def slot(self, name):
                return units.at[name][0] % 3

            def view(self, buf, name, rows=None):
                nk, w = unit_shape[name]
                return buf[:, self.slot(name), 0:nk * w].rearrange("p (k n) -> p k n", n=w)

            def unit_value(self, name, div=1, scale=1):
                n, loops = units.at[name]
                v = (n // div) * scale
                for x in loops:
                    v = self.regs[x] * (units.per[x] // div * scale) + v
                return v

        x_dram = A["x"].rearrange("a (t p) d -> p (a t) d", p=P)
        out_dram = out.rearrange("a (t p) d -> p (a t) d", p=P)

        def unit_source(name, regs):
            nk, w = unit_shape[name]

            def rows(m, kh, c0):
                return m[kh * nk * P:(kh + 1) * nk * P, c0:c0 + w].rearrange("(k p) n -> p k n", p=P)
            n0, n1 = name[0], name[1]
            if n0 in ("km", "vm"):
                return rows(A["w_mem_kv"][0], n1, 512 * (n0 == "vm"))
            if n0 in IN1 and len(name) == 2:
                return rows(A["w_in"][0], n1, IN1[n0][0])
            if n0 == "glu":
                return rows(A["w_glu"][0], 0, 0)
            if n0 == "up":
                return rows(A["w_up_" + n1][0], 0, 512 * name[2])
            if n0 in ("g", "u", "d"):
                (tag, which), part = name[1], name[2]
                shift = {"first": 0, "loop": 0, "last": FULL_CHUNKS - 1, "end": FULL_CHUNKS}[which]
                if tag == "moe":
                    e = EXPERTS - 1 if which == "end" else 0 if which == "first" else regs["moe"]
                    if n0 == "g" and which == "loop":
                        e = e + 1
                    m = A[{"g": "w_gate", "u": "w_up", "d": "w_down"}[n0]][0, e]
                    return rows(m, 0, 512 * part) if n0 == "d" else rows(m, part, 0)
                l = regs["layer"]
                m = A["ffn" + tag[2] + {"g": "_w_gate_2", "u": "_w_up_2", "d": "_w_down_2"}[n0]][l]
                c = shift if which in ("last", "end") else 0 if which == "first" else regs[tag]
                if n0 == "g" and which in ("loop", "last"):
                    c = c + 1
                if n0 == "d":
                    if which == "loop":
                        return m[bass.ds(c * 512, nk * P), 512 * part:512 * part + 512].rearrange("(k p) n -> p k n", p=P)
                    return m[c * 512:c * 512 + nk * P, 512 * part:512 * part + 512].rearrange("(k p) n -> p k n", p=P)
                if which == "loop":
                    return m[part * nk * P:(part + 1) * nk * P, bass.ds(c * 512, w)].rearrange("(k p) n -> p k n", p=P)
                return rows(m, part, c * 512)
            if isinstance(n0, tuple):
                kind, c = n0
                if kind == "gate":
                    return rows(A["w_in"][0], n1, IN1["gate"][0] + 512 * c)
                if kind == "wo":
                    return rows(A["w_out"][0], n1, 512 * c)
                if kind == "wo2":
                    return rows(A["w_out_2"][regs["layer"]], n1, 512 * c)
                if kind == "pb":
                    return rows(A["w_proj_b_2"][regs["layer"]], n1, 512 * c)
                return rows(A["w_in_2"][regs["layer"]], n1, IN2[kind][0] + 512 * c)
            if n0 == "pa":
                return rows(A["w_proj_a_2"][regs["layer"]], 0, 512 * n1)
            return rows(A["w_in_2"][regs["layer"]], n1, IN2[n0][0])

        def loops_of(names):
            return [n for n in unit_names if n in names]

        def straight(lo_name, hi_name):
            i, j = unit_names.index(lo_name), unit_names.index(hi_name)
            return unit_names[i:j + 1]

        def in_trip(tag):
            return [n for n in unit_names if n[0] in ("g", "u", "d") and n[1] == (tag, "loop")]

        def after_trips(tag):
            return [n for n in unit_names if n[0] in ("g", "u", "d") and n[1] in ((tag, "last"), (tag, "end"))]

        FIRST = ("g", ("moe", "first"), 1)
        stretch1 = straight(("km", 0), FIRST)
        stretch_l1 = straight(("g", ("ff1", "first"), 0), ("g", ("ff1", "first"), 1))
        mid = unit_names[unit_names.index(("d", ("ff1", "end"), 1)) + 1:unit_names.index(("g", ("ff2", "first"), 1)) + 1]

        def trips_of(tag):
            return EXPERTS - 1 if tag == "moe" else FULL_CHUNKS - 1

        block = ctx.enter_context(nc.Block())

        @block.sync
        def _(sp):
            E = Engine()
            sp.dma_start(xn[:, :, :], A["mem"].rearrange("a (t p) d -> p (a t) d", p=P)).then_inc(mem_loaded, 16)
            sp.dma_start(x_sb[:, :, :], x_dram).then_inc(x_loaded, 16)

            def load(name):
                n0 = units.at[name][0]
                if n0 >= RAW or E.regs:
                    sp.wait_ge(lo_split, E.unit_value(name) - (RAW - 1))
                sp.dma_start(E.view(raw, name), unit_source(name, E.regs)).then_inc(weights_loaded[E.slot(name)], 16)

            def load_loop(tag):
                with sp.Fori(0, trips_of(tag)) as i:
                    E.regs[tag] = i
                    for name in in_trip(tag):
                        load(name)
                    del E.regs[tag]
                for name in after_trips(tag):
                    load(name)

            for name in stretch1:
                load(name)
            load_loop("moe")
            sp.wait_ge(done["residual"], marks["residual"].number(("moe", 1), {}) + 1)
            sp.dma_start(rope2, A["rope2"].rearrange("(t p) (a d) -> p t a d", p=P, d=64)).then_inc(block2_loaded, 16)
            sp.dma_start(swa_bias, A["swa_bias"].rearrange("(t p) s -> p t s", p=P)).then_inc(block2_loaded, 16)
            sp.dma_start(reset, A["reset"].partition_broadcast(P)).then_inc(block2_loaded, 16)
            sp.dma_start(gla_mask, A["gla_mask"]).then_inc(block2_loaded, 16)
            with sp.Fori(0, LAYERS) as l:
                E.regs["layer"] = l
                for name in stretch_l1:
                    load(name)
                load_loop("ff1")
                sp.wait_ge(done["residual"], E.nth("residual", ("ff1", 1)))
                sp.dma_start(wgl[0:16, :], A["gla_w_gate_2"][l]).then_inc(wgl_loaded, 16)
                for name in mid:
                    load(name)
                load_loop("ff2")
                del E.regs["layer"]
            sp.wait_ge(done["residual"], marks["residual"].n)
            sp.dma_start(out_dram, x_sb[:, :, :]).then_inc(stored, 16)
            sp.wait_ge(stored, 16)

        @block.tensor
        def _(pe):
            E = Engine(counts_steps=True)
            nth, regs, step = E.nth, E.regs, E.step

            def bank(name):
                b = bank_of[name]
                if banks[b].at[name][0] > 0:
                    pe.wait_ge(bank_freed[b], banks[b].number(name, regs))
                return ps[:, b, :]

            def fill(ins, name):
                ins.then_inc(bank_filled[bank_of[name]], 1)

            def unit(name):
                pe.wait_ge(lo_split, E.unit_value(name) + 1)
                return E.view(w_hi, name), E.view(w_lo, name)

            def split_products(dst, a_h, a_l, b_h, b_l, first, final, **kw):
                pe.matmul(dst, a_h, b_h, start=first, stop=False, **kw)
                pe.matmul(dst, a_h, b_l, start=False, stop=False, **kw)
                return pe.matmul(dst, a_l, b_h, start=False, stop=final, **kw)

            def close(name, dst, row=0, col=0):
                fill(pe.matmul(dst[row:row + 1, col:col + 1], zero_b[:, 0:1], zero_b[:, 0:1], start=False, stop=True,
                               skip_group_check=True, tile_position=(0, row)), name)

            def rows_unit(name, fills, dst, lhs, k0, first, final):
                hi, lo = unit(name)
                nk, w = unit_shape[name]
                for t in range(2):
                    for k in range(nk):
                        m = split_products(dst[t][:, 0:w], lhs[0][:, k0 + k, t * P:t * P + P],
                                           lhs[1][:, k0 + k, t * P:t * P + P], hi[:, k, :], lo[:, k, :],
                                           first and k == 0, final and k == nk - 1 and t == 0, skip_group_check=True)
                    if final and t == 0:
                        fill(m, fills[0])
                m.then_inc(unit_used, 1)
                if final:
                    close(fills[1], dst[1])

            def rows_panel(names, fills, lhs=(a_hi, a_lo)):
                dst, k0 = [bank(f) for f in fills], 0
                for i, name in enumerate(names):
                    rows_unit(name, fills, dst, lhs, k0, i == 0, i == len(names) - 1)
                    k0 += unit_shape[name][0]

            def columns_panel(names, fills, rhs=(a_hi, a_lo), m_blocks=4, m_width=P):
                dst, k0 = [bank(f) for f in fills], 0
                for i, name in enumerate(names):
                    hi, lo = unit(name)
                    nk = unit_shape[name][0]
                    for mb in range(m_blocks):
                        o_ = dst[mb // 2][0:m_width, (mb % 2) * SEQ:(mb % 2) * SEQ + SEQ]
                        for k in range(nk):
                            sl = slice(mb * m_width, (mb + 1) * m_width)
                            first = i == 0 and k == 0 and mb % 2 == 0
                            kw = dict(stop=False, skip_group_check=True)
                            pe.matmul(o_, hi[:, k, sl], rhs[0][:, k0 + k, :], start=first, **kw)
                            pe.matmul(o_, lo[:, k, sl], rhs[0][:, k0 + k, :], start=False, **kw)
                            m = pe.matmul(o_, hi[:, k, sl], rhs[1][:, k0 + k, :], start=False, **kw)
                    k0 += nk
                    m.then_inc(unit_used, 1)
                for f, d in zip(fills, dst):
                    close(f, d)

            def half_rows(names, lhs_of, rhs_of):
                dst = [bank(name) for name in names]
                for j in range(2):
                    for p, name in enumerate(names):
                        if j == 1:
                            pe.wait_ge(pe_step, step.value(p + 1 - len(names)))
                        m = pe.matmul(dst[p][:, j * SEQ:j * SEQ + SEQ], lhs_of(j, p), rhs_of(j, p), start=True, stop=True)
                        if j == 0:
                            m.then_inc(pe_step, 1)
                            step.n += 1
                        else:
                            fill(m, name)

            def halves(n):
                return [(n, 0), (n, 1)]

            def turn_blocks(name, sources):
                dst = bank(name)
                for j, src in enumerate(sources):
                    m = pe.transpose(dst[:, j * P:j * P + P], src, ident)
                fill(m, name)

            def turn_rows(tag):
                for t in range(2):
                    pe.wait_ge(done["rows"], nth("rows", (tag, t)))
                    for hh in range(2):
                        turn_blocks((tag + "T", t, hh), [xn[:, t, (4 * hh + j) * P:(4 * hh + j + 1) * P] for j in range(4)])

            def turned(tag):
                pe.wait_ge(done["turned"], nth("turned", (tag, 1, 1)))

            pe.wait_ge(const_loaded, CONSTS)
            pe.wait_ge(zeroed, 1)
            turn_rows("mem")
            turned("mem")
            rows_panel(halves("km"), [("km", t) for t in range(2)])
            rows_panel(halves("vm"), [("vm", t) for t in range(2)])
            turn_rows("x")
            turned("x")
            columns_panel(halves("u"), [("uT", 0), ("uT", 1)])
            for i in range(4):
                if i < 2:
                    pe.wait_ge(done["ssm_params"], nth("ssm_params", "b"))
                else:
                    pe.wait_ge(ssm_loaded, SSM_LOADS)
                turn_blocks(("ssmT", i), [bsc[:, i, 4 * j:4 * j + 4, :].rearrange("p a b -> p (a b)") if i < 2
                                          else cn[:, i - 2, j, :] for j in range(4)])
            pe.wait_ge(done["ssm_weights"], nth("ssm_weights", 3))
            pe.wait_ge(done["u_rows"], nth("u_rows", 1))
            y_dst = [bank(("y", h)) for h in range(2)]

            def read_out(T):
                pe.wait_ge(done["rotated"], nth("rotated", T))
                r, j = 32 * (T % 4), T // 4
                o_ = y_dst[j // 2][r:r + 32, (j % 2) * SEQ:(j % 2) * SEQ + SEQ]
                pe.matmul(o_, cc[:, 0, T, :], s_out[:, 0, :], start=True, stop=False, skip_group_check=True,
                          tile_position=(0, r))
                pe.matmul(o_, cc[:, 1, T, :], s_out[:, 1, :], start=False, stop=True, skip_group_check=True,
                          tile_position=(0, r)).then_inc(done["mixed"], 1)

            for T in range(SSM_TILES):
                r, j = 32 * (T % 4), T // 4
                dst = bank(("bu", T))
                for i in range(2):
                    m = pe.matmul(dst[:, i * SEQ:i * SEQ + SEQ], bb[r:r + 32, i, j, :], u_f[r:r + 32, j, :],
                                  start=True, stop=True, tile_position=(r, 0))
                fill(m, ("bu", T))
                if T % 4 == 0 and T < 12:
                    n = ("kvi", "q", "qm")[T // 4]
                    rows_panel(halves(n), [(n, t) for t in range(2)])
                if T >= 2:
                    read_out(T - 2)
            read_out(SSM_TILES - 2)
            read_out(SSM_TILES - 1)
            for h in range(2):
                close(("y", h), y_dst[h], 96, SEQ)

            def gate(c):
                rows_panel(halves(("gate", c)), [("gate", c, t) for t in range(2)])

            gate(0)
            pe.wait_ge(done["gelu_split"], nth("gelu_split", 1))
            columns_panel([("glu", 0)], [("glu", 0), ("glu", 1)], (y_hi[:, 1], y_lo[:, 1]))
            gate(1)
            for t in range(2):
                pe.wait_ge(done["heads"], nth("heads", "dq"))
                turn_blocks(("dqT", t), [q_sb[:, t, j * P:j * P + P] for j in range(4)])
                pe.wait_ge(done["heads"], nth("heads", "dk"))
                turn_blocks(("dkT", t), [kdup[:, 0, t, :], kdup[:, 1, t, :], kvi[:, t, 128:256], kvi[:, t, 256:384]])
            pe.wait_ge(done["heads_turned"], nth("heads_turned", ("dkT", 1)))
            for t in range(2):
                half_rows([("isc", t, p) for p in range(2)],
                          lambda j, p: kT[64 * j:64 * j + 64, 2 + p, t * P:t * P + P],
                          lambda j, p: kT[64 * j:64 * j + 64, 1, :])
            gate(2)

            def attention(tag, pairs, q_of, k_of, v_of, pT, p_src, meanwhile):
                for t in range(2):
                    half_rows([(tag, "S", t, p) for p in range(pairs)],
                              lambda j, p: q_of(2 * p + j, t), lambda j, p: k_of(2 * p + j))
                    meanwhile(t)
                    pe.wait_ge(done["probs"], nth("probs", (tag, t)))
                    for p in range(pairs):
                        turn_blocks((tag, "PT", t, p), [p_src[:, 2 * p + j, s_ * P:s_ * P + P]
                                                        for j in range(2) for s_ in range(2)])
                    dst = bank((tag, "O", t))
                    for i in range(4):
                        heads = [i] if pairs == 2 else [2 * i, 2 * i + 1]
                        pe.wait_ge(done["probs_turned"], nth("probs_turned", (tag, t, heads[-1] // 2)))
                        terms = [(h, s_) for h in heads for s_ in range(2)]
                        for n, (h, s_) in enumerate(terms):
                            m = pe.matmul(dst[:, i * P:i * P + P], v_of(h, s_), pT[:, s_, h, :],
                                          start=n == 0, stop=n == len(terms) - 1)
                    fill(m, (tag, "O", t))

            pe.wait_ge(done["values"], nth("values", "dsa"))
            attention("dsa", 4, lambda h, t: qT[64 * (h % 2):64 * (h % 2) + 64, h // 2, t * P:t * P + P],
                      lambda h: kT[64 * (h % 2):64 * (h % 2) + 64, 0, :], lambda h, s_: vpad[:, s_, h % 2, :],
                      probsT, probs, lambda t: gate(3 + t))
            pe.wait_ge(done["heads"], nth("heads", "mk"))
            for t in range(2):
                turn_blocks(("mqT", t), [qm_sb[:, t, j * P:j * P + P] for j in range(4)])
                turn_blocks(("mkT", t), [km_sb[:, t, j * P:j * P + P] for j in range(4)])
            pe.wait_ge(done["heads_turned"], nth("heads_turned", ("mkT", 1)))
            attention("mem", 2, lambda h, t: qT[:, h, t * P:t * P + P], lambda h: kT[:, h, :],
                      lambda h, s_: vm_sb[:, s_, h * P:h * P + P], probsT, probs,
                      lambda t: gate(5) if t == 0 else None)
            for i, br in enumerate(("ssm", "dsa", "mem")):
                pe.wait_ge(done["branch"], nth("branch", "ssm" if i == 0 else (br, 1)))
                for c in range(2):
                    rows_panel([("up", br, c)], [("up", br, c, t) for t in range(2)], (y_hi[:, i], y_lo[:, i]))
            turn_rows("m")
            turned("m")
            for c in range(2):
                rows_panel(halves(("wo", c)), [("wo", c, t) for t in range(2)])
            turn_rows("f")
            turned("f")
            for t in range(2):
                dst = bank(("rt", t))
                for k in range(KB):
                    m = pe.matmul(dst[:, 0:36], h_full[:, k, t * P:t * P + P], w_route[:, k, :],
                                  start=k == 0, stop=k == KB - 1)
                fill(m, ("rt", t))

            def turn_hidden(k, src, nb):
                for t in range(2):
                    pe.wait_ge(done["hidden"], nth("hidden", (*k, t)))
                    turn_blocks((*k, "hT", t), [src[:, t, j * P:j * P + P] for j in range(nb)])

            def down(k, acc, nb):
                pe.wait_ge(done["hidden_turned"], nth("hidden_turned", (*k, 1)))
                for c in range(2):
                    hi, lo = unit(("d", k, c))
                    for t in range(2):
                        for j in range(nb):
                            m = split_products(acc[t][c], y_hi[:, 0, j, t * P:t * P + P], y_lo[:, 0, j, t * P:t * P + P],
                                               hi[:, j, :], lo[:, j, :], False, False, skip_group_check=True)
                    m.then_inc(unit_used, 1)

            def glu_trip(tag, which, acc, src, w_next):
                k = (tag, which)
                rows_panel([("u", k, 0), ("u", k, 1)], [(*k, "u", t) for t in range(2)])
                fills = [(*k, "g", t) for t in range(2)]
                dst = [bank(f) for f in fills]
                if w_next == 512:
                    rows_unit(("g", k, 0), fills, dst, (a_hi, a_lo), 0, True, False)
                    turn_hidden(k, src, 4)
                    rows_unit(("g", k, 1), fills, dst, (a_hi, a_lo), 4, False, True)
                else:
                    rows_unit(("g", k, 0), fills, dst, (a_hi, a_lo), 0, True, True)
                    turn_hidden(k, src, 4)
                down(k, acc, 4)

            def glu(tag, src, tail):
                acc = [[bank((tag, "acc", t, c)) for c in range(2)] for t in range(2)]
                for t in range(2):
                    for c in range(2):
                        for q in range(4):
                            pe.matmul(acc[t][c][:, q * P:q * P + P], zero_b[:, :], zero_b[:, :], start=q == 0,
                                      stop=False, skip_group_check=True)
                rows_panel([("g", (tag, "first"), 0), ("g", (tag, "first"), 1)],
                           [(tag, "first", "g", t) for t in range(2)])
                with pe.Fori(0, trips_of(tag)) as i:
                    regs[tag] = i
                    glu_trip(tag, "loop", acc, src, 512)
                    del regs[tag]
                if tail:
                    glu_trip(tag, "last", acc, src, tail)
                k = (tag, "end")
                w = tail or 512
                rows_panel([("u", k, 0), ("u", k, 1)] if w == 512 else [("u", k, 0)], [(*k, "u", t) for t in range(2)])
                turn_hidden(k, src, w // P)
                down(k, acc, w // P)
                for t in range(2):
                    for c in range(2):
                        close((tag, "acc", t, c), acc[t][c])

            glu("moe", hid, 0)

            with pe.Fori(0, LAYERS) as l:
                regs["layer"] = l
                step.begin(l, 8)
                turn_rows("n1")
                turned("n1")
                glu("ff1", hid2, TAIL_FF)
                turn_rows("n2")
                turned("n2")
                rows_panel(halves("qa"), [("qa", t) for t in range(2)])
                rows_panel([("kva", 0)], [("kva", t) for t in range(2)])
                columns_panel(halves("qb"), [("qbT", 0), ("qbT", 1)])
                columns_panel(halves("kb"), [("kbT", 0), ("kbT", 1)])
                pe.wait_ge(done["heads"], nth("heads", "sq"))
                for t in range(2):
                    turn_blocks(("sqT", t), [qa_sb[:, t, j * P:j * P + P] for j in range(4)])
                pe.wait_ge(done["heads"], nth("heads", "sk"))
                turn_blocks(("skT", 0), [kdup2[:, g, t, :] for g in range(2) for t in range(2)])
                columns_panel([("glr", 0)], [("glrT", 0)], m_blocks=1, m_width=16)
                pe.wait_ge(done["evacuated"], nth("evacuated", "glrT"))
                pe.wait_ge(wgl_loaded, l * 16 + 16)
                for i in range(2):
                    dst = bank(("lgT", i))
                    for j in range(2):
                        mb = 2 * i + j
                        m = pe.matmul(dst[:, j * SEQ:j * SEQ + SEQ], wgl[0:16, mb * P:mb * P + P], glrT[0:16, :],
                                      start=True, stop=True)
                    fill(m, ("lgT", i))

                def wide(n, c):
                    rows_panel(halves((n, c)), [(n, c, t) for t in range(2)])

                pe.wait_ge(done["heads_turned"], nth("heads_turned", ("skT", 0)))
                pe.wait_ge(done["values"], nth("values", "swa"))
                attention("swa", 4, lambda h, t: qT2[64 * (h % 2):64 * (h % 2) + 64, h // 2, t * P:t * P + P],
                          lambda h: kT2[64 * (h % 2):64 * (h % 2) + 64, h // 4, :],
                          lambda h, s_: vpad2[:, s_, h // 4, h % 2, :], probsT2, probs2, lambda t: wide("vb", t))
                wide("rb", 0)
                wide("rb", 1)
                pe.wait_ge(done["decayed"], nth("decayed", "ku"))
                for t in range(2):
                    turn_blocks(("gkT", t), [kuT[:, j, t * P:t * P + P] for j in range(4)])
                pe.wait_ge(done["decayed"], nth("decayed", "k"))
                for t in range(2):
                    dst = bank(("A", t))
                    for h in range(4):
                        m = pe.matmul(dst[:, h * P:h * P + P], kbT[:, h, t * P:t * P + P], qbT[:, h, t * P:t * P + P],
                                      start=True, stop=True)
                    fill(m, ("A", t))
                wide("ga", 0)
                pe.wait_ge(done["evacuated"], nth("evacuated", ("vb", 1, 1)))
                pe.wait_ge(done["gk_turned"], nth("gk_turned", 1))
                for c in range(3):
                    r = 64 * (c % 2)
                    for hp in range(2):
                        dst = bank(("kv", c, hp))
                        for j in range(2):
                            h = 2 * hp + j
                            m = pe.matmul(dst[:, j * SEQ:j * SEQ + SEQ], kk[r:r + 64, c // 2, h * P:h * P + P],
                                          vb[r:r + 64, c // 2, h * SEQ:h * SEQ + SEQ], start=True, stop=True)
                        fill(m, ("kv", c, hp))
                wide("ga", 1)
                wide("gb", 0)
                wide("gb", 1)
                pe.wait_ge(done["decayed"], nth("decayed", "qq"))
                pe.wait_ge(done["masked"], nth("masked", 1))
                pe.wait_ge(done["state"], nth("state", 2))
                for t in range(2):
                    for hp in range(2):
                        dst = bank(("ob", t, hp))
                        for j in range(2):
                            h = 2 * hp + j
                            o_ = slice(j * SEQ, j * SEQ + SEQ)
                            pe.matmul(dst[:, o_], am[:, t, h, :], vb[:, t, h * SEQ:h * SEQ + SEQ], start=True,
                                      stop=False, skip_group_check=True)
                            for c in (1,) if t == 0 else (2, 3):
                                r = 64 * (c % 2)
                                pe.matmul(dst[r:r + 64, o_], qqT[:, h, c * 64:c * 64 + 64], state[:, c - 1, h, :],
                                          start=False, stop=False, skip_group_check=True, tile_position=(0, r))
                        close(("ob", t, hp), dst, 0, SEQ)
                turn_rows("o")
                pe.wait_ge(done["branch"], nth("branch", ("swa", 1)))
                for c in range(2):
                    rows_panel([("pa", c)], [("pa", c, t) for t in range(2)], (y_hi[:, 0], y_lo[:, 0]))
                turned("o")
                for c in range(2):
                    rows_panel(halves(("pb", c)), [("pb", c, t) for t in range(2)])
                turn_rows("m2")
                turned("m2")
                for c in range(2):
                    rows_panel(halves(("wo2", c)), [("wo2", c, t) for t in range(2)])
                turn_rows("n3")
                turned("n3")
                glu("ff2", hid2, TAIL_FF)
                step.end(LAYERS)
                del regs["layer"]

        def split_ahead(E, names, emit, name, extra):
            stop = min(names.index(name) + extra + 1, len(names))
            while E.cursor < stop:
                emit(names[E.cursor])
                E.cursor += 1

        @block.scalar
        def _(act):
            E = Engine(counts_steps=True)
            nth, regs, step, fills, psum = E.nth, E.regs, E.step, E.fills, E.psum

            def load(dst, src):
                act.dma_start(dst, src).then_inc(const_loaded, 16)
                loads.append(1)
            loads = []

            def columns(dst, src):
                load(dst, src.rearrange("(k p) -> p k", p=P))
            load(ident, A["ident"])
            with nc.allow_non_contiguous_dma(reason="gains as columns: one word for each feature"):
                columns(gain["mem"], A["g_mem"][0])
                columns(gain["x"], A["g_mix"][0])
                columns(gain["f"], A["g_ffn"][0])
                for l in range(LAYERS):
                    columns(gain2["n1"][:, l], A["ffn1_norm_2"][l])
                    columns(gain2["n2"][:, l], A["mix_norm_2"][l])
                    columns(gain2["n3"][:, l], A["ffn2_norm_2"][l])
                    columns(gain2["o"][:, l], A["gla_out_norm_2"][l])
                    columns(gate_bias[:, l], A["gla_gate_bias_2"][l])
                columns(d_skip, A["d_skip"][0])
                load(posi[:, :], A["positions"].rearrange("a (t p) -> p (a t)", p=P))
                load(w_route[:, :, 0:GROUPS], A["w_group"][0].rearrange("(k p) n -> p k n", p=P))
                load(w_route[:, :, GROUPS:36], A["w_expert"][0].rearrange("(k p) n -> p k n", p=P))
            for l in range(LAYERS):
                load(swa_gain[:, l, 0], A["swa_q_norm_2"][l].partition_broadcast(P))
                load(swa_gain[:, l, 1], A["swa_k_norm_2"][l].partition_broadcast(P))
                load(sinks[:, l], A["swa_sinks_2"][l].partition_broadcast(P))
            load(b_route[:, 0:GROUPS], A["b_group"][0].partition_broadcast(P))
            load(b_route[:, GROUPS:36], A["b_expert"][0].rearrange("g e -> (g e)").partition_broadcast(P))
            load(first_key, A["first_key"].partition_broadcast(P))
            load(g_q1, A["g_q"][0].partition_broadcast(P))
            load(g_k1, A["g_k"][0].partition_broadcast(P))
            load(g_qm1, A["g_qm"][0].partition_broadcast(P))
            load(g_km1, A["g_km"][0].partition_broadcast(P))
            load(inv_freq, A["inv_freq"].partition_broadcast(P))
            load(t_row, A["t_row"].partition_broadcast(P))
            load(pos_row_i, A["positions"][0].partition_broadcast(P))
            assert 16 * len(loads) == CONSTS, len(loads)

            def hi(name, ahead=0):
                n0 = units.at[name][0] + ahead
                if n0 >= SPLIT or regs:
                    act.wait_ge(unit_used, E.unit_value(name) + (ahead - (SPLIT - 1)))
                act.wait_ge(weights_loaded[E.slot(name)], 16 + E.unit_value(name, 3, 16) + ahead // 3 * 16)
                act.activation(E.view(w_hi, name), E.view(raw, name), ACT.Copy).then_inc(hi_split, 1)

            def copy_out(name, signal_event, dst, src=None, func=ACT.Copy, scale=1.0, signal="evacuated"):
                act.wait_ge(bank_filled[bank_of[name]], fills(name))
                p_ = psum(name)
                if src is not None:
                    p_ = src(p_)
                act.activation(dst, p_, func, scale=scale).then_inc(bank_freed[bank_of[name]], 1)
                act.wait_ge(bank_freed[bank_of[name]], fills(name))
                if signal_event is not None:
                    act.sem_inc(done[signal], 1)

            def squares(tag, src, junk):
                for t in range(2):
                    act.activation(junk, src[:, t, :], ACT.Square, accum_out=st_ss[:, t:t + 1]).then_inc(done["summed"], 1)
                    act.wait_ge(done["summed"], nth("summed", (tag, t)))

            def inverse_root(event, v, r):
                act.wait_ge(done["meansq"], nth("meansq", event))
                act.activation(r, v, ACT.Ln).then_inc(scalar_step, 1)
                act.wait_ge(scalar_step, step.next())
                act.activation(r, r, ACT.Exp, scale=-0.5).then_inc(done["rstd"], 1)
                act.wait_ge(done["rstd"], nth("rstd", event))

            def ahead(name, extra=1):
                split_ahead(E, stretch, hi, name, extra)

            stretch = stretch1
            act.wait_ge(mem_loaded, 16)
            squares("mem", xn, u_flat)
            inverse_root("mem", st_v, st_rstd)
            ahead(("km", 0))
            act.wait_ge(x_loaded, 16)
            squares("x", x_sb, u_flat)
            ahead(("km", 0), 2)
            inverse_root("x", st_v, st_rstd)
            act.wait_ge(ssm_loaded, SSM_LOADS)
            act.activation(par[:, 3], par[:, 0], ACT.Exp).then_inc(done["ssm_act"], 1)
            act.wait_ge(done["ssm_act"], nth("ssm_act", 0))
            act.wait_ge(done["ssm_vec"], nth("ssm_vec", 0))
            act.activation(par[:, 9], par[:, 4], ACT.Exp).then_inc(scalar_step, 1)
            act.wait_ge(scalar_step, step.next())
            act.activation(par[:, 10], par[:, 6], ACT.Abs).then_inc(scalar_step, 1)
            act.wait_ge(scalar_step, step.next())
            act.activation(par[:, 10], par[:, 10], ACT.Sin, scale=-6.283185, bias=half_pi[:, 0:1]).then_inc(scalar_step, 1)
            act.wait_ge(scalar_step, step.next())
            act.activation(par[:, 11], par[:, 6], ACT.Sin, scale=6.283185).then_inc(done["ssm_act"], 1)
            act.wait_ge(done["ssm_act"], nth("ssm_act", 1))
            act.wait_ge(done["rope_angle"], nth("rope_angle", 0))
            act.activation(rope_tmp[:, 1], rope_tmp[:, 0], ACT.Abs).then_inc(scalar_step, 1)
            act.wait_ge(scalar_step, step.next())
            r32 = lambda i: rope_tmp[:, i].rearrange("p (t d) -> p t d", d=32)
            act.activation(rope1[:, 0, :, 0:32], r32(1), ACT.Sin, scale=-1.0, bias=half_pi[:, 0:1]).then_inc(scalar_step, 1)
            act.wait_ge(scalar_step, step.next())
            act.activation(rope1[:, 0, :, 32:64], r32(1), ACT.Sin, scale=-1.0, bias=half_pi[:, 0:1]).then_inc(scalar_step, 1)
            act.wait_ge(scalar_step, step.next())
            act.activation(rope1[:, 1, :, 0:32], r32(0), ACT.Sin, scale=-1.0).then_inc(scalar_step, 1)
            act.wait_ge(scalar_step, step.next())
            act.activation(rope1[:, 1, :, 32:64], r32(0), ACT.Sin).then_inc(done["rope_trig"], 1)
            act.wait_ge(done["rope_trig"], nth("rope_trig", 0))
            ahead(("km", 1), 2)
            copy_out(("km", 0), ("km", 0), km_sb[:, 0, :])
            copy_out(("km", 1), ("km", 1), km_sb[:, 1, :])
            ahead(("vm", 1), 2)
            copy_out(("vm", 0), ("vm", 0), vm_sb[:, 0, :])
            copy_out(("vm", 1), ("vm", 1), vm_sb[:, 1, :])
            ahead(("u", 1), 1)
            for g in range(4):
                act.wait_ge(done["angle"], nth("angle", g))
                s_ = slice(4 * g, 4 * g + 4)
                act.activation(cos_t[:, s_], sin_t[:, s_], ACT.Abs).then_inc(scalar_step, 1)
                act.wait_ge(scalar_step, step.next())
                act.activation(cos_t[:, s_], cos_t[:, s_], ACT.Sin, scale=-6.283185, bias=half_pi[:, 0:1]).then_inc(scalar_step, 1)
                act.wait_ge(scalar_step, step.next())
                act.activation(sin_t[:, s_], sin_t[:, s_], ACT.Sin, scale=6.283185).then_inc(done["trig"], 1)
                act.wait_ge(done["trig"], nth("trig", g))
            ahead(("u", 1), 2)
            for h in range(2):
                act.wait_ge(bank_filled[bank_of[("uT", h)]], fills(("uT", h)))
                p_ = psum(("uT", h)).rearrange("p (m s) -> p m s", s=SEQ)
                act.activation(u_f[:, 2 * h:2 * h + 2], p_, ACT.Copy).then_inc(bank_freed[bank_of[("uT", h)]], 1)
                act.wait_ge(bank_freed[bank_of[("uT", h)]], fills(("uT", h)))
                act.sem_inc(done["u_rows"], 1)
            for i in range(4):
                dst = bb[:, i].rearrange("p j s -> p (j s)") if i < 2 else cc[:, i - 2].rearrange("p t c -> p (t c)")
                copy_out(("ssmT", i), i, dst, scale=-1.0 if i == 3 else 1.0, signal="ssm_weights")
            for n, dst, w in (("kvi", kvi, 452), ("q", q_sb, 512), ("qm", qm_sb, 512)):
                ahead((n, 1), 2)
                for t in range(2):
                    copy_out((n, t), (n, t), dst[:, t, 0:w], lambda p_: p_[:, 0:w])

            def gate(c, extra=1):
                ahead((("gate", c), 1), extra)
                for t in range(2):
                    copy_out(("gate", c, t), None, gates1[:, t, c, :])

            for h in range(2):
                act.wait_ge(done["gelu_in"], nth("gelu_in", h))
                act.activation(y_g[:, 2 * h:2 * h + 2], y_g[:, 2 * h:2 * h + 2], ACT.Gelu_apprx_tanh).then_inc(done["gelu"], 1)
                act.wait_ge(done["gelu"], nth("gelu", h))
            gate(0)
            ahead(("glu", 0), 1)
            for h in range(2):
                act.wait_ge(bank_filled[bank_of[("glu", h)]], fills(("glu", h)))
                p_ = psum(("glu", h)).rearrange("p (m s) -> p m s", s=SEQ)
                act.activation(u_f[:, 2 * h:2 * h + 2], p_, ACT.Sigmoid).then_inc(bank_freed[bank_of[("glu", h)]], 1)
                act.wait_ge(bank_freed[bank_of[("glu", h)]], fills(("glu", h)))
                act.sem_inc(done["evacuated"], 1)
            ahead((("gate", 1), 1), 0)
            inverse_root("heads1", hs[:, 0:34], hr[:, 0:34])
            gate(1)

            def turned_out(name, dst):
                copy_out(name, name, dst, lambda p_: p_.rearrange("p (j s) -> p j s", s=P), signal="heads_turned")

            for t in range(2):
                ts_ = slice(t * P, t * P + P)
                turned_out(("dqT", t), qT[:, :, ts_])
                turned_out(("dkT", t), kT[:, :, ts_])
            for t in range(2):
                for p in range(2):
                    act.wait_ge(bank_filled[bank_of[("isc", t, p)]], fills(("isc", t, p)))
                    p_ = psum(("isc", t, p)).rearrange("p (j s) -> p j s", s=SEQ)
                    act.activation(relu[:, 2 * t + p], p_, ACT.Relu).then_inc(bank_freed[bank_of[("isc", t, p)]], 1)
                    act.wait_ge(bank_freed[bank_of[("isc", t, p)]], fills(("isc", t, p)))
                    act.sem_inc(done["relued"], 1)
            gate(2)

            def attention(tag, pairs, pr, pT, meanwhile):
                for t in range(2):
                    meanwhile(t, 0)
                    act.wait_ge(done["maxed"], nth("maxed", (tag, t)))
                    if tag == "swa":
                        act.activation(snk, snk, ACT.Exp).then_inc(scalar_step, 1)
                        act.wait_ge(scalar_step, step.next())
                    for h in range(2 * pairs):
                        ins = act.activation(pr[:, h, :], pr[:, h, :], ACT.Exp, bias=mx[:, h:h + 1],
                                             accum_out=rs[:, h:h + 1])
                        if h == 2 * pairs - 1:
                            ins.then_inc(done["exped"], 1)
                            act.wait_ge(done["exped"], nth("exped", (tag, t)))
                        else:
                            ins.then_inc(scalar_step, 1)
                            act.wait_ge(scalar_step, step.next())
                    meanwhile(t, 1)
                    for p in range(pairs):
                        act.wait_ge(bank_filled[bank_of[(tag, "PT", t, p)]], fills((tag, "PT", t, p)))
                        p_ = psum((tag, "PT", t, p)).rearrange("p (h s q) -> p s h q", h=2, s=2)
                        act.activation(pT[:, :, 2 * p:2 * p + 2, :], p_, ACT.Copy).then_inc(bank_freed[bank_of[(tag, "PT", t, p)]], 1)
                        act.wait_ge(bank_freed[bank_of[(tag, "PT", t, p)]], fills((tag, "PT", t, p)))
                        act.sem_inc(done["probs_turned"], 1)

            def with_gate(c):
                def f(t, when):
                    if c + t > 5:
                        return
                    if when == 0:
                        ahead((("gate", c + t), 1), 0)
                    else:
                        gate(c + t)
                return f
            attention("dsa", 4, probs, probsT, with_gate(3))
            for t in range(2):
                ts_ = slice(t * P, t * P + P)
                turned_out(("mqT", t), qT[:, :, ts_])
                turned_out(("mkT", t), kT[:, :, ts_])
            attention("mem", 2, probs, probsT, with_gate(5))
            for i, br in enumerate(("ssm", "dsa", "mem")):
                act.activation(gates1[:, :, 2 * i:2 * i + 2, :], gates1[:, :, 2 * i:2 * i + 2, :], ACT.Sigmoid).then_inc(done["gates"], 1)
                act.wait_ge(done["gates"], nth("gates", br))
            ahead(("up", "mem", 1), 1)
            ahead((("wo", 1), 1), 1)
            for t in range(2):
                act.wait_ge(done["residual"], nth("residual", ("wo", t)))
            squares("f", x_sb, hid[:, :, :].rearrange("p a b -> p (a b)"))
            inverse_root("f", st_v, st_rstd)
            ahead(FIRST, 0)
            act.wait_ge(done["route_in"], nth("route_in", 0))
            act.activation(rts(0, 4), rts(0, 4), ACT.Exp).then_inc(done["route"], 1)
            act.wait_ge(done["route"], nth("route", "exp"))
            act.wait_ge(done["route_in"], nth("route_in", 1))
            act.activation(rts(5, 1), rts(5, 1), ACT.Exp).then_inc(done["route"], 1)
            act.wait_ge(done["route"], nth("route", "expert"))

            def silu(k, dst, w, prior):
                for t in range(2):
                    if prior is not None:
                        act.wait_ge(done["hidden"], nth("hidden", (*prior, t)))
                    act.wait_ge(bank_filled[bank_of[(*k, "g", t)]], fills((*k, "g", t)))
                    p_ = psum((*k, "g", t))[:, 0:w]
                    act.activation(dst[:, t, 0:w], p_, ACT.Silu).then_inc(bank_freed[bank_of[(*k, "g", t)]], 1)
                    act.wait_ge(bank_freed[bank_of[(*k, "g", t)]], fills((*k, "g", t)))
                    act.sem_inc(done["silu"], 1)

            def glu(tag, dst, tail):
                L = (tag, "loop")
                regs[tag] = 0
                hi(("u", L, 0))
                hi(("u", L, 1))
                del regs[tag]
                silu((tag, "first"), dst, 512, None)
                with act.Fori(0, trips_of(tag)) as i:
                    regs[tag] = i
                    for part in range(2):
                        hi(("g", L, part))
                    hi(("d", L, 0))
                    hi(("d", L, 1))
                    silu(L, dst, 512, L)
                    for part in range(2):
                        hi(("u", L, part), units.per[tag])
                    del regs[tag]
                if tail:
                    K, Z = (tag, "last"), (tag, "end")
                    hi(("g", K, 0))
                    hi(("d", K, 0))
                    hi(("d", K, 1))
                    silu(K, dst, tail, K)
                    hi(("u", Z, 0))
                    hi(("d", Z, 0))
                    hi(("d", Z, 1))
                else:
                    hi(("d", (tag, "end"), 0))
                    hi(("d", (tag, "end"), 1))

            glu("moe", sil, 0)
            act.wait_ge(done["residual"], nth("residual", ("moe", 1)))

            hid2_flat = hid2[:, :, :].rearrange("p a b -> p (a b)")
            with act.Fori(0, LAYERS) as l:
                regs["layer"] = l
                step.begin(l, SCALAR_STEPS_LAYER)
                stretch, E.cursor = stretch_l1, 0
                squares("n1", x_sb, hid2_flat)
                inverse_root("n1", st_v, st_rstd)
                ahead(("g", ("ff1", "first"), 1), 0)
                glu("ff1", sil2, TAIL_FF)
                stretch, E.cursor = mid, 0
                ahead(mid[0], 1)
                act.wait_ge(done["residual"], nth("residual", ("ff1", 1)))
                squares("n2", x_sb, hid2_flat)
                inverse_root("n2", st_v, st_rstd)
                ahead(("qa", 1), 1)
                for t in range(2):
                    copy_out(("qa", t), ("qa", t), qa_sb[:, t, :])
                ahead(("kva", 0), 1)
                for t in range(2):
                    copy_out(("kva", t), ("kva", t), kva[:, t, :], lambda p_: p_[:, 0:256])
                ahead(("qb", 1), 1)
                inverse_root("heads2", hs[:, 0:20], hr[:, 0:20])

                def columns_out(n, dst):
                    for h in range(2):
                        act.wait_ge(bank_filled[bank_of[(n, h)]], fills((n, h)))
                        p_ = psum((n, h)).rearrange("p (m s) -> p m s", s=SEQ)
                        act.activation(dst[:, 2 * h:2 * h + 2], p_, ACT.Copy).then_inc(bank_freed[bank_of[(n, h)]], 1)
                        act.wait_ge(bank_freed[bank_of[(n, h)]], fills((n, h)))
                    act.sem_inc(done["evacuated"], 1)
                columns_out("qbT", qbT)
                ahead(("kb", 1), 1)
                columns_out("kbT", kbT)
                ahead(("glr", 0), 1)
                for t in range(2):
                    turned_out(("sqT", t), qT2[:, :, t * P:t * P + P])
                copy_out(("skT", 0), ("skT", 0), kT2[:, :, :].rearrange("p g s -> p (g s)"), signal="heads_turned")
                act.wait_ge(bank_filled[bank_of[("glrT", 0)]], fills(("glrT", 0)))
                p_ = psum(("glrT", 0))
                act.activation(glrT[0:16, :], p_[0:16, 0:SEQ], ACT.Copy).then_inc(bank_freed[bank_of[("glrT", 0)]], 1)
                act.wait_ge(bank_freed[bank_of[("glrT", 0)]], fills(("glrT", 0)))
                act.sem_inc(done["evacuated"], 1)
                for i in range(2):
                    act.wait_ge(bank_filled[bank_of[("lgT", i)]], fills(("lgT", i)))
                    p_ = psum(("lgT", i))
                    for j in range(2):
                        ins = act.activation(gb_[:, 2 * i + j, :], p_[:, j * SEQ:j * SEQ + SEQ], ACT.Identity,
                                             bias=gate_bias[:, bass.ds(l, 1), 2 * i + j])
                        if j == 1:
                            ins.then_inc(bank_freed[bank_of[("lgT", i)]], 1)
                            act.wait_ge(bank_freed[bank_of[("lgT", i)]], fills(("lgT", i)))
                        else:
                            ins.then_inc(scalar_step, 1)
                            act.wait_ge(scalar_step, step.next())

                def wide(n, c, dst, extra=1):
                    ahead(((n, c), 1), extra)
                    for t in range(2):
                        copy_out((n, c, t), (n, c, t) if n == "vb" else None, dst[:, t, c * 512:c * 512 + 512])

                def with_v(t, when):
                    if when == 0:
                        ahead((("vb", t), 1), 0)
                    else:
                        wide("vb", t, vb)
                attention("swa", 4, probs2, probsT2, with_v)
                act.wait_ge(done["branch"], nth("branch", ("swa", 1)))
                flat = lambda v: v.rearrange("p a b -> p (a b)")
                act.activation(flat(etmp), flat(gb_), ACT.Abs).then_inc(scalar_step, 1)
                act.wait_ge(scalar_step, step.next())
                act.activation(flat(etmp), flat(etmp), ACT.Exp, scale=-1.0).then_inc(scalar_step, 1)
                act.wait_ge(scalar_step, step.next())
                act.activation(flat(etmp), flat(etmp), ACT.Ln, bias=1.0).then_inc(done["gate_ln"], 1)
                act.wait_ge(done["gate_ln"], nth("gate_ln", 0))
                wide("rb", 0, rb)
                act.wait_ge(done["decay"], nth("decay", 0))
                act.activation(flat(gb_), flat(gb_), ACT.Exp, scale=-1.0).then_inc(scalar_step, 1)
                act.wait_ge(scalar_step, step.next())
                ends = etmp[:, :, GLA_CHUNK - 1:SEQ:GLA_CHUNK]
                act.activation(comb4, ends, ACT.Exp).then_inc(done["decay_exp"], 1)
                act.wait_ge(done["decay_exp"], nth("decay_exp", 0))
                wide("rb", 1, rb)
                for t in range(2):
                    copy_out(("gkT", t), t, kk[:, t, :], signal="gk_turned")
                act.wait_ge(done["decayed"], nth("decayed", "ku"))
                act.activation(flat(gb_), flat(etmp), ACT.Exp).then_inc(done["decay_exp"], 1)
                act.wait_ge(done["decay_exp"], nth("decay_exp", 1))
                act.wait_ge(done["decay"], nth("decay", 1))
                act.activation(flat(gb_), flat(gb_), ACT.Exp).then_inc(done["decay_exp"], 1)
                act.wait_ge(done["decay_exp"], nth("decay_exp", 2))
                act.wait_ge(done["decay"], nth("decay", 2))
                act.activation(flat(gb_), flat(gb_), ACT.Exp, scale=-1.0).then_inc(done["decay_exp"], 1)
                act.wait_ge(done["decay_exp"], nth("decay_exp", 3))
                wide("ga", 0, gab[:, :, 0])
                wide("ga", 1, gab[:, :, 0])
                wide("gb", 0, gab[:, :, 1])
                wide("gb", 1, gab[:, :, 1])
                for t in range(2):
                    for hp in range(2):
                        copy_out(("ob", t, hp), ("ob", t, hp), xn[:, t, hp * 512:hp * 512 + 512])
                for t in range(2):
                    for h in range(4):
                        ins = act.activation(glrT, xn[:, t, h * SEQ:h * SEQ + SEQ], ACT.Square,
                                             accum_out=hs[:, 4 * t + h:4 * t + h + 1])
                        if h == 3:
                            ins.then_inc(done["summed"], 1)
                            act.wait_ge(done["summed"], nth("summed", ("o", t)))
                        else:
                            ins.then_inc(scalar_step, 1)
                            act.wait_ge(scalar_step, step.next())
                inverse_root("o", hs[:, 0:8], hr[:, 0:8])
                act.activation(rb[:, :, :], rb[:, :, :], ACT.Silu).then_inc(done["gates"], 1)
                act.wait_ge(done["gates"], nth("gates", "rb"))
                ahead(("pa", 0), 1)
                act.activation(gab[:, :, 0], gab[:, :, 0], ACT.Sigmoid).then_inc(done["gates"], 1)
                act.wait_ge(done["gates"], nth("gates", "ga"))
                act.activation(gab[:, :, 1], gab[:, :, 1], ACT.Sigmoid).then_inc(done["gates"], 1)
                act.wait_ge(done["gates"], nth("gates", "gb"))
                ahead((("pb", 1), 1), 1)
                ahead((("wo2", 1), 1), 1)
                for t in range(2):
                    act.wait_ge(done["residual"], nth("residual", ("wo2", t)))
                squares("n3", x_sb, hid2_flat)
                inverse_root("n3", st_v, st_rstd)
                ahead(mid[-1], 0)
                glu("ff2", sil2, TAIL_FF)
                act.wait_ge(done["residual"], nth("residual", ("ff2", 1)))
                step.end(LAYERS)
                del regs["layer"]

        @block.vector
        def _(dve):
            E = Engine(counts_steps=True)
            nth, regs, step, fills, psum = E.nth, E.regs, E.step, E.fills, E.psum
            tt, ts, stt = dve.tensor_tensor, dve.tensor_scalar, dve.scalar_tensor_tensor

            def lo(name, ahead=0):
                dve.wait_ge(hi_split, E.unit_value(name) + 1 + ahead)
                tt(E.view(w_lo, name), E.view(raw, name), E.view(w_hi, name).bitcast(F32), ALU.subtract)\
                    .then_inc(lo_split, 1)

            def ahead(name, extra=1):
                split_ahead(E, stretch, lo, name, extra)

            def split_out(src, hi_, lo_):
                dve.tensor_copy(hi_, src).then_inc(vector_step, 1)
                dve.wait_ge(vector_step, step.next())
                return tt(lo_, src, hi_.bitcast(F32), ALU.subtract)

            def normed(tag, src, width=D):
                dve.wait_ge(done["summed"], nth("summed", (tag, 1)))
                ts(st_v, st_ss, 1.0 / width, EPS, ALU.mult, ALU.add).then_inc(done["meansq"], 1)
                dve.wait_ge(done["meansq"], nth("meansq", tag))
                dve.wait_ge(done["rstd"], nth("rstd", tag))
                for t in range(2):
                    ts(xn[:, t, :], src[:, t, :], st_rstd[:, t:t + 1], None, ALU.mult).then_inc(done["rows"], 1)
                    dve.wait_ge(done["rows"], nth("rows", (tag, t)))

            def turned(tag, g, full):
                for t in range(2):
                    for hh in range(2):
                        name = (tag + "T", t, hh)
                        dve.wait_ge(bank_filled[bank_of[name]], fills(name))
                        p_ = psum(name).rearrange("p (k s) -> p k s", s=P)
                        at = (slice(None), slice(4 * hh, 4 * hh + 4), slice(t * P, t * P + P))
                        if g is not None:
                            tt(full[at], p_, g[:, 4 * hh:4 * hh + 4].unsqueeze(2).broadcast_to([P, 4, P]),
                               ALU.mult).then_inc(bank_freed[bank_of[name]], 1)
                            dve.wait_ge(bank_freed[bank_of[name]], fills(name))
                            split_out(full[at], a_hi[at], a_lo[at]).then_inc(done["turned"], 1)
                            dve.wait_ge(done["turned"], nth("turned", (tag, t, hh)))
                        else:
                            split_out(p_, a_hi[at], a_lo[at]).then_inc(bank_freed[bank_of[name]], 1)
                            dve.wait_ge(bank_freed[bank_of[name]], fills(name))
                            dve.sem_inc(done["turned"], 1)

            stretch = stretch1
            dve.memset(half_pi[:, :], 1.5707963).then_inc(vector_step, 1)
            dve.wait_ge(vector_step, step.next())
            dve.wait_ge(const_loaded, CONSTS)
            normed("mem", xn)
            ahead(("km", 0))
            turned("mem", gain["mem"], full1)
            normed("x", x_sb)
            ahead(("km", 1), 1)
            dve.tensor_copy(pos_row, pos_row_i).then_inc(vector_step, 1)
            dve.wait_ge(vector_step, step.next())
            dve.tensor_copy(pos_col, posi[:, :]).then_inc(vector_step, 1)
            dve.wait_ge(vector_step, step.next())
            ra, rb_ = rope_tmp[:, 0], rope_tmp[:, 1]
            for t in range(2):
                ts(ra[:, 32 * t:32 * t + 32], inv_freq, pos_col[:, t:t + 1], None, ALU.mult).then_inc(vector_step, 1)
                dve.wait_ge(vector_step, step.next())
            ts(rb_, ra, 1.0 / TWO_PI, None, ALU.mult).then_inc(vector_step, 1)
            dve.wait_ge(vector_step, step.next())
            ts(rb_, rb_, ROUND, -ROUND, ALU.add, ALU.add).then_inc(vector_step, 1)
            dve.wait_ge(vector_step, step.next())
            stt(out=ra, in0=rb_, scalar=-6.28125, in1=ra, op0=ALU.mult, op1=ALU.add).then_inc(vector_step, 1)
            dve.wait_ge(vector_step, step.next())
            stt(out=ra, in0=rb_, scalar=-(TWO_PI - 6.28125), in1=ra, op0=ALU.mult, op1=ALU.add).then_inc(vector_step, 1)
            dve.wait_ge(vector_step, step.next())
            ts(ra, ra, 3.1415925, -3.1415925, ALU.min, ALU.max).then_inc(done["rope_angle"], 1)
            dve.wait_ge(done["rope_angle"], nth("rope_angle", 0))
            dve.wait_ge(done["ssm_act"], nth("ssm_act", 0))
            tt(par[:, 4], par[:, 1], par[:, 3], ALU.mult).then_inc(vector_step, 1)
            dve.wait_ge(vector_step, step.next())
            tt(par[:, 5], par[:, 2], par[:, 3], ALU.mult).then_inc(vector_step, 1)
            dve.wait_ge(vector_step, step.next())
            ts(par[:, 6], par[:, 5], 1.0 / TWO_PI, None, ALU.mult).then_inc(vector_step, 1)
            dve.wait_ge(vector_step, step.next())
            ts(par[:, 7], par[:, 6], ROUND, -ROUND, ALU.add, ALU.add).then_inc(vector_step, 1)
            dve.wait_ge(vector_step, step.next())
            tt(par[:, 6], par[:, 6], par[:, 7], ALU.subtract).then_inc(vector_step, 1)
            dve.wait_ge(vector_step, step.next())
            ts(par[:, 7], par[:, 6], COARSE, -COARSE, ALU.add, ALU.add).then_inc(vector_step, 1)
            dve.wait_ge(vector_step, step.next())
            tt(par[:, 8], par[:, 6], par[:, 7], ALU.subtract).then_inc(done["ssm_vec"], 1)
            dve.wait_ge(done["ssm_vec"], nth("ssm_vec", 0))
            ahead(("vm", 0), 0)
            for g in range(4):
                s_ = slice(4 * g, 4 * g + 4)
                t_b = t_row.unsqueeze(1).broadcast_to([P, 4, SEQ])
                c_, s__ = cos_t[:, s_], sin_t[:, s_]
                per = lambda i: par[:, i, s_].unsqueeze(2).broadcast_to([P, 4, SEQ])
                tt(c_, t_b, per(7), ALU.mult).then_inc(vector_step, 1)
                dve.wait_ge(vector_step, step.next())
                ts(s__, c_, ROUND, -ROUND, ALU.add, ALU.add).then_inc(vector_step, 1)
                dve.wait_ge(vector_step, step.next())
                tt(c_, c_, s__, ALU.subtract).then_inc(vector_step, 1)
                dve.wait_ge(vector_step, step.next())
                tt(s__, t_b, per(8), ALU.mult).then_inc(vector_step, 1)
                dve.wait_ge(vector_step, step.next())
                tt(c_, c_, s__, ALU.add).then_inc(vector_step, 1)
                dve.wait_ge(vector_step, step.next())
                ts(s__, c_, ROUND, -ROUND, ALU.add, ALU.add).then_inc(vector_step, 1)
                dve.wait_ge(vector_step, step.next())
                tt(s__, c_, s__, ALU.subtract).then_inc(done["angle"], 1)
                dve.wait_ge(done["angle"], nth("angle", g))
                if g == 1:
                    ahead(("vm", 1), 1)
            turned("x", gain["x"], full_x)
            ahead(("u", 1), 1)
            dve.wait_ge(done["ssm_act"], nth("ssm_act", 1))
            tt(par[:, 10], par[:, 10], par[:, 9], ALU.mult).then_inc(vector_step, 1)
            dve.wait_ge(vector_step, step.next())
            ts(par[:, 10], par[:, 10], -1.0, None, ALU.add).then_inc(vector_step, 1)
            dve.wait_ge(vector_step, step.next())
            tt(par[:, 11], par[:, 11], par[:, 9], ALU.mult).then_inc(vector_step, 1)
            dve.wait_ge(vector_step, step.next())
            tt(par[:, 0], par[:, 1], par[:, 1], ALU.mult).then_inc(vector_step, 1)
            dve.wait_ge(vector_step, step.next())
            tt(par[:, 3], par[:, 2], par[:, 2], ALU.mult).then_inc(vector_step, 1)
            dve.wait_ge(vector_step, step.next())
            tt(par[:, 0], par[:, 0], par[:, 3], ALU.add).then_inc(vector_step, 1)
            dve.wait_ge(vector_step, step.next())
            dve.reciprocal(par[:, 0], par[:, 0]).then_inc(vector_step, 1)
            dve.wait_ge(vector_step, step.next())
            tt(par[:, 3], par[:, 10], par[:, 1], ALU.mult).then_inc(vector_step, 1)
            dve.wait_ge(vector_step, step.next())
            tt(par[:, 4], par[:, 11], par[:, 2], ALU.mult).then_inc(vector_step, 1)
            dve.wait_ge(vector_step, step.next())
            tt(par[:, 4], par[:, 3], par[:, 4], ALU.add).then_inc(vector_step, 1)
            dve.wait_ge(vector_step, step.next())
            tt(par[:, 4], par[:, 4], par[:, 0], ALU.mult).then_inc(vector_step, 1)
            dve.wait_ge(vector_step, step.next())
            tt(par[:, 3], par[:, 11], par[:, 1], ALU.mult).then_inc(vector_step, 1)
            dve.wait_ge(vector_step, step.next())
            tt(par[:, 5], par[:, 10], par[:, 2], ALU.mult).then_inc(vector_step, 1)
            dve.wait_ge(vector_step, step.next())
            tt(par[:, 5], par[:, 3], par[:, 5], ALU.subtract).then_inc(vector_step, 1)
            dve.wait_ge(vector_step, step.next())
            tt(par[:, 5], par[:, 5], par[:, 0], ALU.mult).then_inc(vector_step, 1)
            dve.wait_ge(vector_step, step.next())
            f_re, f_im = (par[:, i].unsqueeze(2).broadcast_to([P, SSM_TILES, 32]) for i in (4, 5))
            b_t = area(o_scan + 1024, SSM_TILES, 32)
            tt(bsc[:, 0], bn[:, 0], f_re, ALU.mult).then_inc(vector_step, 1)
            dve.wait_ge(vector_step, step.next())
            tt(b_t, bn[:, 1], f_im, ALU.mult).then_inc(vector_step, 1)
            dve.wait_ge(vector_step, step.next())
            tt(bsc[:, 0], bsc[:, 0], b_t, ALU.subtract).then_inc(vector_step, 1)
            dve.wait_ge(vector_step, step.next())
            tt(bsc[:, 1], bn[:, 1], f_re, ALU.mult).then_inc(vector_step, 1)
            dve.wait_ge(vector_step, step.next())
            tt(b_t, bn[:, 0], f_im, ALU.mult).then_inc(vector_step, 1)
            dve.wait_ge(vector_step, step.next())
            tt(bsc[:, 1], bsc[:, 1], b_t, ALU.add).then_inc(done["ssm_params"], 1)
            dve.wait_ge(done["ssm_params"], nth("ssm_params", "b"))
            ahead(("u", 1), 2)
            dve.wait_ge(done["trig"], nth("trig", 3))
            for T in range(SSM_TILES):
                if T % 4 == 0 and T < 12:
                    ahead((("kvi", "q", "qm")[T // 4], 1), 1)
                dve.wait_ge(bank_filled[bank_of[("bu", T)]], fills(("bu", T)))
                v = psum(("bu", T)).rearrange("p (a s) -> p a s", s=SEQ)
                cosb, sinb = (x_[:, T:T + 1, :].broadcast_to([P, 2, SEQ]) for x_ in (cos_t, sin_t))
                tt(sc_a, v, cosb, ALU.mult).then_inc(vector_step, 1)
                dve.wait_ge(vector_step, step.next())
                tt(sc_b, v, sinb, ALU.mult).then_inc(bank_freed[bank_of[("bu", T)]], 1)
                dve.wait_ge(bank_freed[bank_of[("bu", T)]], fills(("bu", T)))
                tt(sc_a[:, 0], sc_a[:, 0], sc_b[:, 1], ALU.add).then_inc(vector_step, 1)
                dve.wait_ge(vector_step, step.next())
                tt(sc_a[:, 1], sc_a[:, 1], sc_b[:, 0], ALU.subtract).then_inc(vector_step, 1)
                dve.wait_ge(vector_step, step.next())
                if T >= 2:
                    dve.wait_ge(done["rotated"], nth("rotated", T - 2))
                r_ = par[:, 9, T:T + 1].broadcast_to([P, SEQ])
                dve.tensor_tensor_scan(s_rot[:, T % 2, 0], r_, sc_a[:, 0], 0.0, ALU.mult, ALU.add).then_inc(vector_step, 1)
                dve.wait_ge(vector_step, step.next())
                dve.tensor_tensor_scan(s_rot[:, T % 2, 1], r_, sc_a[:, 1], 0.0, ALU.mult, ALU.add).then_inc(done["scanned"], 1)
                dve.wait_ge(done["scanned"], nth("scanned", T))
            ahead((("gate", 0), 1), 0)
            for h in range(2):
                dve.wait_ge(bank_filled[bank_of[("y", h)]], fills(("y", h)))
                p_ = psum(("y", h))
                for j in range(2):
                    ins = stt(out=y_g[:, 2 * h + j], in0=u_f[:, 2 * h + j], scalar=d_skip[:, 2 * h + j:2 * h + j + 1],
                              in1=p_[:, j * SEQ:j * SEQ + SEQ], op0=ALU.mult, op1=ALU.add)
                    if j == 1:
                        ins.then_inc(bank_freed[bank_of[("y", h)]], 1)
                        dve.wait_ge(bank_freed[bank_of[("y", h)]], fills(("y", h)))
                        dve.sem_inc(done["gelu_in"], 1)
                    else:
                        ins.then_inc(vector_step, 1)
                        dve.wait_ge(vector_step, step.next())
            for h in range(2):
                dve.wait_ge(done["gelu"], nth("gelu", h))
                at = (slice(None), slice(2 * h, 2 * h + 2))
                split_out(y_g[at], y_hi[:, 1][at], y_lo[:, 1][at]).then_inc(done["gelu_split"], 1)
                dve.wait_ge(done["gelu_split"], nth("gelu_split", h))
            ahead(("glu", 0), 0)
            ahead((("gate", 1), 0), 0)
            dve.wait_ge(done["evacuated"], nth("evacuated", ("glu", 1)))
            tt(y_g[:, :, :], y_g[:, :, :], u_f[:, :, :], ALU.mult).then_inc(vector_step, 1)
            dve.wait_ge(vector_step, step.next())
            split_out(y_g[:, :, :], y_hi[:, 0], y_lo[:, 0]).then_inc(done["branch"], 1)
            dve.wait_ge(done["branch"], nth("branch", "ssm"))
            ahead((("gate", 1), 1), 0)

            def rms_heads(src, n, d, at):
                tmp = scr[:, 0:n * d].rearrange("p (h d) -> p h d", d=d)
                if src.ndim == 4:
                    tmp4 = scr[:, 0:n * d].rearrange("p (a h d) -> p a h d", d=d, a=src.shape[1])
                    tt(tmp4, src, src, ALU.mult).then_inc(vector_step, 1)
                    dve.wait_ge(vector_step, step.next())
                else:
                    tt(tmp, src, src, ALU.mult).then_inc(vector_step, 1)
                    dve.wait_ge(vector_step, step.next())
                dve.tensor_reduce(hs[:, at:at + n], tmp, AX, ALU.add).then_inc(vector_step, 1)
                dve.wait_ge(vector_step, step.next())

            def scaled(src, n, d, at, g, last=None):
                ins = tt(src, src, hr[:, at:at + n].unsqueeze(2).broadcast_to([P, n, d]), ALU.mult)
                ins.then_inc(vector_step, 1)
                dve.wait_ge(vector_step, step.next())
                return tt(src, src, g.broadcast_to([P, n, d]), ALU.mult)

            def rope(x4, heads, table):
                n = 2 * heads * 64
                t1 = scr[:, 0:n].rearrange("p (t h d) -> p t h d", t=2, d=64)
                t2 = scrb[:, 0:n].rearrange("p (t h d) -> p t h d", t=2, d=64)
                tab = lambda i, a, b: table[:, i, :, a:b].unsqueeze(2).broadcast_to([P, 2, heads, b - a])
                tt(t1, x4, tab(0, 0, 64), ALU.mult).then_inc(vector_step, 1)
                dve.wait_ge(vector_step, step.next())
                tt(t2[:, :, :, 0:32], x4[:, :, :, 32:64], tab(1, 0, 32), ALU.mult).then_inc(vector_step, 1)
                dve.wait_ge(vector_step, step.next())
                tt(t2[:, :, :, 32:64], x4[:, :, :, 0:32], tab(1, 32, 64), ALU.mult).then_inc(vector_step, 1)
                dve.wait_ge(vector_step, step.next())
                return tt(x4, t1, t2, ALU.add)

            scr, scrb = scr1, area(o_P + 1024, 1024)
            dve.wait_ge(done["evacuated"], nth("evacuated", ("qm", 1)))
            k3 = kvi[:, :, 0:64]
            q3 = q_sb[:, :, :].rearrange("p t (h d) -> p (t h) d", d=64)
            qm3 = qm_sb[:, :, :].rearrange("p t (h d) -> p (t h) d", d=P)
            km3 = km_sb[:, :, :].rearrange("p t (h d) -> p (t h) d", d=P)
            rms_heads(q3, 16, 64, 0)
            rms_heads(k3, 2, 64, 16)
            rms_heads(qm3, 8, P, 18)
            rms_heads(km3, 8, P, 26)
            ts(hs[:, 0:18], hs[:, 0:18], 1.0 / 64, EPS, ALU.mult, ALU.add).then_inc(vector_step, 1)
            dve.wait_ge(vector_step, step.next())
            ts(hs[:, 18:34], hs[:, 18:34], 1.0 / P, EPS, ALU.mult, ALU.add).then_inc(done["meansq"], 1)
            dve.wait_ge(done["meansq"], nth("meansq", "heads1"))
            dve.wait_ge(done["rstd"], nth("rstd", "heads1"))
            dve.wait_ge(done["rope_trig"], nth("rope_trig", 0))
            scaled(q3, 16, 64, 0, g_q1.unsqueeze(1)).then_inc(vector_step, 1)
            dve.wait_ge(vector_step, step.next())
            rope(q_sb[:, :, :].rearrange("p t (h d) -> p t h d", d=64), 8, rope1).then_inc(done["heads"], 1)
            dve.wait_ge(done["heads"], nth("heads", "dq"))
            scaled(k3, 2, 64, 16, g_k1.unsqueeze(1)).then_inc(vector_step, 1)
            dve.wait_ge(vector_step, step.next())
            rope(k3.unsqueeze(2), 1, rope1).then_inc(vector_step, 1)
            dve.wait_ge(vector_step, step.next())
            rope(kvi[:, :, 128:448].rearrange("p t (h d) -> p t h d", d=64), 5, rope1).then_inc(vector_step, 1)
            dve.wait_ge(vector_step, step.next())
            for j in range(2):
                dve.tensor_copy(kdup[:, 0, :, 64 * j:64 * j + 64], k3).then_inc(vector_step, 1)
                dve.wait_ge(vector_step, step.next())
                ins = dve.tensor_copy(kdup[:, 1, :, 64 * j:64 * j + 64], kvi[:, :, 384:448])
                if j == 0:
                    ins.then_inc(vector_step, 1)
                    dve.wait_ge(vector_step, step.next())
            ins.then_inc(done["heads"], 1)
            dve.wait_ge(done["heads"], nth("heads", "dk"))
            ahead((("gate", 2), 0), 0)
            scaled(qm3, 8, P, 18, g_qm1.unsqueeze(1)).then_inc(vector_step, 1)
            dve.wait_ge(vector_step, step.next())
            dve.sem_inc(done["heads"], 1)
            scaled(km3, 8, P, 26, g_km1.unsqueeze(1)).then_inc(done["heads"], 1)
            dve.wait_ge(done["heads"], nth("heads", "mk"))
            dve.wait_ge(bank_filled[bank_of[("dqT", 1)]], fills(("dqT", 1)))
            dve.memset(vpad[:, :, :, :], 0.0).then_inc(vector_step, 1)
            dve.wait_ge(vector_step, step.next())
            dve.tensor_copy(vpad[:, :, 0, 0:64], kvi[:, :, 64:128]).then_inc(vector_step, 1)
            dve.wait_ge(vector_step, step.next())
            dve.tensor_copy(vpad[:, :, 1, 64:128], kvi[:, :, 64:128]).then_inc(done["values"], 1)
            dve.wait_ge(done["values"], nth("values", "dsa"))
            ahead((("gate", 2), 1), 0)
            for t in range(2):
                ts(allow[:, t], pos_row, pos_col[:, t:t + 1], None, ALU.is_le).then_inc(vector_step, 1)
                dve.wait_ge(vector_step, step.next())
                ts(key_bias[:, t], allow[:, t], -NEG, NEG, ALU.mult, ALU.add).then_inc(vector_step, 1)
                dve.wait_ge(vector_step, step.next())
                for h in range(4):
                    dve.wait_ge(done["relued"], nth("relued", (t, h // 2)))
                    w = kvi[:, t, 448 + h:449 + h]
                    r_ = relu[:, 2 * t + h // 2, h % 2]
                    if h == 0:
                        ts(isc[:, t], r_, w, None, ALU.mult).then_inc(vector_step, 1)
                        dve.wait_ge(vector_step, step.next())
                    else:
                        stt(out=isc[:, t], in0=r_, scalar=w, in1=isc[:, t], op0=ALU.mult, op1=ALU.add).then_inc(vector_step, 1)
                        dve.wait_ge(vector_step, step.next())
                tt(isc[:, t], isc[:, t], key_bias[:, t], ALU.add).then_inc(vector_step, 1)
                dve.wait_ge(vector_step, step.next())
                for _r in range(TOPK // 8):
                    dve.max(top8, isc[:, t]).then_inc(vector_step, 1)
                    dve.wait_ge(vector_step, step.next())
                    dve.match_replace(isc[:, t], top8, isc[:, t], GONE).then_inc(vector_step, 1)
                    dve.wait_ge(vector_step, step.next())
                stt(out=key_bias[:, t], in0=isc[:, t], scalar=GONE / 2, in1=allow[:, t], op0=ALU.is_le, op1=ALU.mult).then_inc(vector_step, 1)
                dve.wait_ge(vector_step, step.next())
                ts(key_bias[:, t], key_bias[:, t], -NEG, NEG, ALU.mult, ALU.add).then_inc(vector_step, 1)
                dve.wait_ge(vector_step, step.next())

            def attention(tag, pairs, scale, bias, pr, slot, meanwhile):
                n = 2 * pairs
                for t in range(2):
                    meanwhile(t)
                    for p in range(pairs):
                        dve.wait_ge(bank_filled[bank_of[(tag, "S", t, p)]], fills((tag, "S", t, p)))
                        p_ = psum((tag, "S", t, p)).rearrange("p (j s) -> p j s", s=SEQ)
                        dst = pr[:, 2 * p:2 * p + 2, :]
                        if bias is None:
                            ts(dst, p_, scale, None, ALU.mult).then_inc(bank_freed[bank_of[(tag, "S", t, p)]], 1)
                            dve.wait_ge(bank_freed[bank_of[(tag, "S", t, p)]], fills((tag, "S", t, p)))
                        else:
                            stt(out=dst, in0=p_, scalar=scale, in1=bias[:, t:t + 1, :].broadcast_to([P, 2, SEQ]),
                                op0=ALU.mult, op1=ALU.add).then_inc(bank_freed[bank_of[(tag, "S", t, p)]], 1)
                            dve.wait_ge(bank_freed[bank_of[(tag, "S", t, p)]], fills((tag, "S", t, p)))
                    dve.tensor_reduce(mx[:, 0:n], pr[:, 0:n, :], AX, ALU.max).then_inc(vector_step, 1)
                    dve.wait_ge(vector_step, step.next())
                    if tag == "swa":
                        sink = sinks[:, bass.ds(regs["layer"], 1), :].rearrange("p a h -> p (a h)")
                        tt(mx, mx, sink, ALU.max).then_inc(vector_step, 1)
                        dve.wait_ge(vector_step, step.next())
                        tt(snk, sink, mx, ALU.subtract).then_inc(vector_step, 1)
                        dve.wait_ge(vector_step, step.next())
                    ts(mx[:, 0:n], mx[:, 0:n], -1.0, None, ALU.mult).then_inc(done["maxed"], 1)
                    dve.wait_ge(done["maxed"], nth("maxed", (tag, t)))
                    dve.wait_ge(done["exped"], nth("exped", (tag, t)))
                    if tag == "swa":
                        tt(rs, rs, snk, ALU.add).then_inc(vector_step, 1)
                        dve.wait_ge(vector_step, step.next())
                    dve.reciprocal(rs[:, 0:n], rs[:, 0:n]).then_inc(vector_step, 1)
                    dve.wait_ge(vector_step, step.next())
                    tt(pr[:, 0:n, :], pr[:, 0:n, :], rs[:, 0:n].unsqueeze(2).broadcast_to([P, n, SEQ]), ALU.mult).then_inc(done["probs"], 1)
                    dve.wait_ge(done["probs"], nth("probs", (tag, t)))
                    dve.wait_ge(bank_filled[bank_of[(tag, "O", t)]], fills((tag, "O", t)))
                    p_ = psum((tag, "O", t)).rearrange("p (i s) -> p i s", s=P)
                    at = (slice(None), slot, slice(0, 4), slice(t * P, t * P + P))
                    split_out(p_, y_hi[at], y_lo[at]).then_inc(bank_freed[bank_of[(tag, "O", t)]], 1)
                    dve.wait_ge(bank_freed[bank_of[(tag, "O", t)]], fills((tag, "O", t)))
                    dve.sem_inc(done["branch"], 1)

            attention("dsa", 4, 0.125, key_bias, probs, 1, lambda t: ahead((("gate", 3 + t), 1), 0))
            attention("mem", 2, float(P) ** -0.5, None, probs, 2,
                      lambda t: ahead((("gate", 5), 1), 0) if t == 0 else None)
            for i, br in enumerate(("ssm", "dsa", "mem")):
                for c in range(2):
                    ahead(("up", br, c), 1)
                    dve.wait_ge(done["gates"], nth("gates", br))
                    for t in range(2):
                        dve.wait_ge(bank_filled[bank_of[("up", br, c, t)]], fills(("up", br, c, t)))
                        p_ = psum(("up", br, c, t))
                        dst, g_ = xn[:, t, c * 512:c * 512 + 512], gates1[:, t, 2 * i + c, :]
                        if i == 0:
                            tt(dst, p_, g_, ALU.mult).then_inc(bank_freed[bank_of[("up", br, c, t)]], 1)
                            dve.wait_ge(bank_freed[bank_of[("up", br, c, t)]], fills(("up", br, c, t)))
                        else:
                            tt(gated, p_, g_, ALU.mult).then_inc(bank_freed[bank_of[("up", br, c, t)]], 1)
                            dve.wait_ge(bank_freed[bank_of[("up", br, c, t)]], fills(("up", br, c, t)))
                            ins = tt(dst, dst, gated, ALU.add)
                            if i == 2 and c == 1:
                                ins.then_inc(done["rows"], 1)
                                dve.wait_ge(done["rows"], nth("rows", ("m", t)))
                            else:
                                ins.then_inc(vector_step, 1)
                                dve.wait_ge(vector_step, step.next())
            turned("m", None, None)

            def residual(tag_of, event, scale=None):
                for c in range(2):
                    for t in range(2):
                        name = tag_of(c, t)
                        dve.wait_ge(bank_filled[bank_of[name]], fills(name))
                        p_, dst = psum(name), x_sb[:, t, c * 512:c * 512 + 512]
                        if scale is None:
                            tt(dst, dst, p_, ALU.add).then_inc(bank_freed[bank_of[name]], 1)
                            dve.wait_ge(bank_freed[bank_of[name]], fills(name))
                        else:
                            stt(out=dst, in0=p_, scalar=scale, in1=dst, op0=ALU.mult, op1=ALU.add).then_inc(bank_freed[bank_of[name]], 1)
                            dve.wait_ge(bank_freed[bank_of[name]], fills(name))
                        if c == 1:
                            dve.sem_inc(done["residual"], 1)
            ahead((("wo", 1), 1), 1)
            residual(lambda c, t: ("wo", c, t), "wo")
            normed("f", x_sb)
            turned("f", gain["f"], h_full)
            ahead(FIRST, 0)
            for t in range(2):
                dve.wait_ge(bank_filled[bank_of[("rt", t)]], fills(("rt", t)))
                tt(rt[:, t], psum(("rt", t))[:, 0:36], b_route, ALU.add).then_inc(bank_freed[bank_of[("rt", t)]], 1)
                dve.wait_ge(bank_freed[bank_of[("rt", t)]], fills(("rt", t)))
            bc = lambda v, n: v.broadcast_to([P, 2, n])
            G, Lx = rt[:, :, 0:4], rt[:, :, 4:36]
            dve.tensor_reduce(rts(1, 1), G, AX, ALU.max).then_inc(vector_step, 1)
            dve.wait_ge(vector_step, step.next())
            tt(rts(0, 4), G, bc(rts(1, 1), 4), ALU.subtract).then_inc(done["route_in"], 1)
            dve.wait_ge(done["route_in"], nth("route_in", 0))
            tt(rts(2, 4), G, bc(rts(1, 1), 4), ALU.is_equal).then_inc(vector_step, 1)
            dve.wait_ge(vector_step, step.next())
            tt(rts(2, 4), rts(2, 4), first_key[:, 32:36].unsqueeze(1).broadcast_to([P, 2, 4]), ALU.mult).then_inc(vector_step, 1)
            dve.wait_ge(vector_step, step.next())
            dve.tensor_reduce(rts(1, 1), rts(2, 4), AX, ALU.max).then_inc(vector_step, 1)
            dve.wait_ge(vector_step, step.next())
            tt(rts(2, 4), rts(2, 4), bc(rts(1, 1), 4), ALU.is_equal).then_inc(vector_step, 1)
            dve.wait_ge(vector_step, step.next())
            ts(rts(2, 4), rts(2, 4), -NEG, NEG, ALU.mult, ALU.add).then_inc(vector_step, 1)
            dve.wait_ge(vector_step, step.next())
            tt(rts(3, 32).rearrange("p t (g e) -> p t g e", e=8), Lx.rearrange("p t (g e) -> p t g e", e=8),
               rts(2, 4).unsqueeze(3).broadcast_to([P, 2, 4, 8]), ALU.add).then_inc(vector_step, 1)
            dve.wait_ge(vector_step, step.next())
            keys = first_key[:, 0:32].unsqueeze(1).broadcast_to([P, 2, 32])

            def best(src, top, sel):
                dve.tensor_reduce(top, src, AX, ALU.max).then_inc(vector_step, 1)
                dve.wait_ge(vector_step, step.next())
                tt(sel, src, bc(top, 32), ALU.is_equal).then_inc(vector_step, 1)
                dve.wait_ge(vector_step, step.next())
                tt(sel, sel, keys, ALU.mult).then_inc(vector_step, 1)
                dve.wait_ge(vector_step, step.next())
                dve.tensor_reduce(rts(7, 1), sel, AX, ALU.max).then_inc(vector_step, 1)
                dve.wait_ge(vector_step, step.next())
                tt(sel, sel, bc(rts(7, 1), 32), ALU.is_equal).then_inc(vector_step, 1)
                dve.wait_ge(vector_step, step.next())
            best(rts(3, 32), rts(4, 1), rts(8, 32))
            stt(out=rts(3, 32), in0=rts(8, 32), scalar=2 * NEG, in1=rts(3, 32), op0=ALU.mult, op1=ALU.add).then_inc(vector_step, 1)
            dve.wait_ge(vector_step, step.next())
            best(rts(3, 32), rts(5, 1), rts(9, 32))
            tt(rts(5, 1), rts(5, 1), rts(4, 1), ALU.subtract).then_inc(done["route_in"], 1)
            dve.wait_ge(done["route_in"], nth("route_in", 1))
            dve.wait_ge(done["route"], nth("route", "exp"))
            dve.tensor_reduce(rts(6, 1), rts(0, 4), AX, ALU.add).then_inc(vector_step, 1)
            dve.wait_ge(vector_step, step.next())
            dve.wait_ge(done["route"], nth("route", "expert"))
            ts(rts(7, 1), rts(5, 1), 1.0, None, ALU.add).then_inc(vector_step, 1)
            dve.wait_ge(vector_step, step.next())
            tt(rts(6, 1), rts(6, 1), rts(7, 1), ALU.mult).then_inc(vector_step, 1)
            dve.wait_ge(vector_step, step.next())
            dve.reciprocal(rts(6, 1), rts(6, 1)).then_inc(vector_step, 1)
            dve.wait_ge(vector_step, step.next())
            tt(rts(7, 1), rts(6, 1), rts(5, 1), ALU.mult).then_inc(vector_step, 1)
            dve.wait_ge(vector_step, step.next())
            tt(rts(8, 32), rts(8, 32), bc(rts(6, 1), 32), ALU.mult).then_inc(vector_step, 1)
            dve.wait_ge(vector_step, step.next())
            tt(rts(9, 32), rts(9, 32), bc(rts(7, 1), 32), ALU.mult).then_inc(vector_step, 1)
            dve.wait_ge(vector_step, step.next())
            tt(comb, rts(8, 32), rts(9, 32), ALU.add).then_inc(vector_step, 1)
            dve.wait_ge(vector_step, step.next())

            def hidden(k, dst, gate_, w, weight):
                for t in range(2):
                    dve.wait_ge(bank_filled[bank_of[(*k, "u", t)]], fills((*k, "u", t)))
                    p_ = psum((*k, "u", t))[:, 0:w]
                    dve.wait_ge(done["silu"], marks["hidden"].number((*k, t), regs) + 1)
                    if weight is None:
                        ins = tt(dst[:, t, 0:w], p_, gate_[:, t, 0:w], ALU.mult)
                    else:
                        ins = stt(out=dst[:, t, 0:w], in0=p_, scalar=weight(t), in1=gate_[:, t, 0:w], op0=ALU.mult,
                                  op1=ALU.mult)
                    ins.then_inc(bank_freed[bank_of[(*k, "u", t)]], 1)
                    dve.wait_ge(bank_freed[bank_of[(*k, "u", t)]], fills((*k, "u", t)))
                    dve.sem_inc(done["hidden"], 1)

            def hidden_turned(k, nb):
                for t in range(2):
                    dve.wait_ge(bank_filled[bank_of[(*k, "hT", t)]], fills((*k, "hT", t)))
                    p_ = psum((*k, "hT", t)).rearrange("p (i s) -> p i s", s=P)[:, 0:nb]
                    at = (slice(None), 0, slice(0, nb), slice(t * P, t * P + P))
                    split_out(p_, y_hi[at], y_lo[at]).then_inc(bank_freed[bank_of[(*k, "hT", t)]], 1)
                    dve.wait_ge(bank_freed[bank_of[(*k, "hT", t)]], fills((*k, "hT", t)))
                    dve.sem_inc(done["hidden_turned"], 1)

            def glu(tag, dst, gate_, tail, steps):
                L = (tag, "loop")
                regs[tag] = 0
                lo(("u", L, 0))
                lo(("u", L, 1))
                del regs[tag]
                with dve.Fori(0, trips_of(tag)) as i:
                    regs[tag] = i
                    step.begin(i, steps)
                    weight = (lambda t: comb[:, t, bass.ds(i, 1)]) if tag == "moe" else None
                    lo(("g", L, 0))
                    lo(("g", L, 1))
                    hidden(L, dst, gate_, 512, weight)
                    lo(("d", L, 0))
                    hidden_turned(L, 4)
                    lo(("d", L, 1))
                    lo(("u", L, 0), units.per[tag])
                    lo(("u", L, 1), units.per[tag])
                    step.end(trips_of(tag))
                    del regs[tag]
                Z = (tag, "end")
                if tail:
                    K = (tag, "last")
                    lo(("g", K, 0))
                    hidden(K, dst, gate_, 512, None)
                    lo(("d", K, 0))
                    hidden_turned(K, 4)
                    lo(("d", K, 1))
                    lo(("u", Z, 0))
                    lo(("d", Z, 0))
                    hidden(Z, dst, gate_, tail, None)
                    hidden_turned(Z, tail // P)
                    lo(("d", Z, 1))
                else:
                    lo(("d", Z, 0))
                    hidden(Z, dst, gate_, 512, lambda t: comb[:, t, EXPERTS - 1:EXPERTS])
                    hidden_turned(Z, 4)
                    lo(("d", Z, 1))

            glu("moe", hid, sil, 0, 2)
            residual(lambda c, t: ("moe", "acc", t, c), "moe")

            dve.wait_ge(block2_loaded, 64)
            with dve.Fori(0, LAYERS) as l:
                regs["layer"] = l
                step.begin(l, VECTOR_STEPS_LAYER)
                g2 = lambda n: gain2[n][:, bass.ds(l, 1), :].rearrange("p a k -> p (a k)")
                stretch, E.cursor = stretch_l1, 0
                normed("n1", x_sb)
                ahead(("g", ("ff1", "first"), 0), 0)
                turned("n1", g2("n1"), h_full2)
                ahead(("g", ("ff1", "first"), 1), 0)
                glu("ff1", hid2, sil2, TAIL_FF, 2)
                residual(lambda c, t: ("ff1", "acc", t, c), "ff1", 0.5)
                stretch, E.cursor = mid, 0
                normed("n2", x_sb)
                ahead(("qa", 0), 1)
                turned("n2", g2("n2"), h_full2)
                ahead(("qa", 1), 1)
                ahead(("kva", 0), 1)
                dve.wait_ge(done["evacuated"], nth("evacuated", ("qa", 1)))
                scr, scrb = scr2, xn[:, 1, :]
                q3 = qa_sb[:, :, :].rearrange("p t (h d) -> p (t h) d", d=64)
                k4 = kva[:, :, 0:128].rearrange("p t (g d) -> p t g d", d=64)
                v4 = kva[:, :, 128:256].rearrange("p t (g d) -> p t g d", d=64)
                rms_heads(q3, 16, 64, 0)
                dve.wait_ge(done["evacuated"], nth("evacuated", ("kva", 1)))
                rms_heads(k4, 4, 64, 16)
                ahead(("qb", 1), 0)
                ts(hs[:, 0:20], hs[:, 0:20], 1.0 / 64, EPS, ALU.mult, ALU.add).then_inc(done["meansq"], 1)
                dve.wait_ge(done["meansq"], nth("meansq", "heads2"))
                gn = lambda i: swa_gain[:, bass.ds(l, 1), i, :]
                dve.wait_ge(done["rstd"], nth("rstd", "heads2"))
                scaled(q3, 16, 64, 0, gn(0)).then_inc(vector_step, 1)
                dve.wait_ge(vector_step, step.next())
                ahead(("kb", 0), 0)
                rope(qa_sb[:, :, :].rearrange("p t (h d) -> p t h d", d=64), 8, rope2.rearrange("p t a d -> p a t d")).then_inc(done["heads"], 1)
                dve.wait_ge(done["heads"], nth("heads", "sq"))
                ahead(("kb", 1), 0)
                for t in range(2):
                    kt_ = kva[:, t, 0:128].rearrange("p (g d) -> p g d", d=64)
                    tt(kt_, kt_, hr[:, 16 + 2 * t:18 + 2 * t].unsqueeze(2).broadcast_to([P, 2, 64]), ALU.mult).then_inc(vector_step, 1)
                    dve.wait_ge(vector_step, step.next())
                    tt(kt_, kt_, gn(1).broadcast_to([P, 2, 64]), ALU.mult).then_inc(vector_step, 1)
                    dve.wait_ge(vector_step, step.next())
                rope(k4, 2, rope2.rearrange("p t a d -> p a t d")).then_inc(vector_step, 1)
                dve.wait_ge(vector_step, step.next())
                for j in range(2):
                    ins = dve.tensor_copy(kdup2[:, :, :, 64 * j:64 * j + 64], k4.rearrange("p t g d -> p g t d"))
                    if j == 0:
                        ins.then_inc(vector_step, 1)
                        dve.wait_ge(vector_step, step.next())
                ins.then_inc(done["heads"], 1)
                dve.wait_ge(done["heads"], nth("heads", "sk"))
                dve.memset(vpad2[:, :, :, :, :], 0.0).then_inc(vector_step, 1)
                dve.wait_ge(vector_step, step.next())
                dve.tensor_copy(vpad2[:, :, :, 0, 0:64], v4).then_inc(vector_step, 1)
                dve.wait_ge(vector_step, step.next())
                dve.tensor_copy(vpad2[:, :, :, 1, 64:128], v4).then_inc(done["values"], 1)
                dve.wait_ge(done["values"], nth("values", "swa"))
                ahead(("glr", 0), 0)
                attention("swa", 4, 0.125, swa_bias, probs2, 0, lambda t: ahead((("vb", t), 1), 0))
                ahead((("rb", 0), 1), 0)
                flat = lambda v: v.rearrange("p a b -> p (a b)")
                dve.wait_ge(done["gate_ln"], nth("gate_ln", 0))
                stt(out=flat(gb_), in0=flat(gb_), scalar=0.0, in1=flat(etmp), op0=ALU.min, op1=ALU.subtract).then_inc(vector_step, 1)
                dve.wait_ge(vector_step, step.next())
                ts(flat(gb_), flat(gb_), 1.0 / 16, None, ALU.mult).then_inc(vector_step, 1)
                dve.wait_ge(vector_step, step.next())
                for h in range(4):
                    dve.tensor_tensor_scan(etmp[:, h, :], reset, gb_[:, h, :], 0.0, ALU.mult, ALU.add).then_inc(vector_step, 1)
                    dve.wait_ge(vector_step, step.next())
                chunks = lambda v: v.rearrange("p m (c s) -> p (m c) s", s=GLA_CHUNK)
                ref = lambda i: chunks(etmp)[:, :, i:i + 1].broadcast_to([P, 16, GLA_CHUNK])
                tt(chunks(gb_), chunks(etmp), ref(GLA_CHUNK - 1), ALU.subtract).then_inc(done["decay"], 1)
                dve.wait_ge(done["decay"], nth("decay", 0))
                dve.wait_ge(done["decay_exp"], nth("decay_exp", 0))
                tt(kuT, kbT, gb_, ALU.mult).then_inc(done["decayed"], 1)
                dve.wait_ge(done["decayed"], nth("decayed", "ku"))
                ahead((("rb", 1), 1), 0)
                scale = float(P) ** -0.5
                dve.wait_ge(done["decay_exp"], nth("decay_exp", 1))
                stt(out=flat(qqT), in0=flat(qbT), scalar=scale, in1=flat(gb_), op0=ALU.mult, op1=ALU.mult).then_inc(done["decayed"], 1)
                dve.wait_ge(done["decayed"], nth("decayed", "qq"))
                tt(chunks(gb_), chunks(etmp), ref(GLA_CHUNK // 2 - 1), ALU.subtract).then_inc(done["decay"], 1)
                dve.wait_ge(done["decay"], nth("decay", 1))
                dve.wait_ge(done["decay_exp"], nth("decay_exp", 2))
                stt(out=flat(qbT), in0=flat(qbT), scalar=scale, in1=flat(gb_), op0=ALU.mult, op1=ALU.mult).then_inc(done["decayed"], 1)
                dve.wait_ge(done["decayed"], nth("decayed", "q"))
                tt(chunks(gb_), chunks(etmp), ref(GLA_CHUNK // 2 - 1), ALU.subtract).then_inc(done["decay"], 1)
                dve.wait_ge(done["decay"], nth("decay", 2))
                dve.wait_ge(done["decay_exp"], nth("decay_exp", 3))
                tt(flat(kbT), flat(kbT), flat(gb_), ALU.mult).then_inc(done["decayed"], 1)
                dve.wait_ge(done["decayed"], nth("decayed", "k"))
                ahead((("ga", 0), 1), 0)
                for t in range(2):
                    dve.wait_ge(bank_filled[bank_of[("A", t)]], fills(("A", t)))
                    p_ = psum(("A", t)).rearrange("p (h s) -> p h s", s=P)
                    tt(am[:, t], p_, gla_mask.unsqueeze(1).broadcast_to([P, 4, P]), ALU.mult).then_inc(bank_freed[bank_of[("A", t)]], 1)
                    dve.wait_ge(bank_freed[bank_of[("A", t)]], fills(("A", t)))
                    dve.sem_inc(done["masked"], 1)
                for c in range(3):
                    for hp in range(2):
                        dve.wait_ge(bank_filled[bank_of[("kv", c, hp)]], fills(("kv", c, hp)))
                        p_ = psum(("kv", c, hp)).rearrange("p (j s) -> p j s", s=SEQ)
                        if c == 0:
                            dve.tensor_copy(state[:, 0, 2 * hp:2 * hp + 2, :], p_).then_inc(bank_freed[bank_of[("kv", c, hp)]], 1)
                            dve.wait_ge(bank_freed[bank_of[("kv", c, hp)]], fills(("kv", c, hp)))
                        else:
                            for j in range(2):
                                h = 2 * hp + j
                                ins = stt(out=state[:, c, h, :], in0=state[:, c - 1, h, :],
                                          scalar=comb4[:, h, c:c + 1], in1=p_[:, j, :], op0=ALU.mult, op1=ALU.add)
                                if j == 0:
                                    ins.then_inc(vector_step, 1)
                                    dve.wait_ge(vector_step, step.next())
                            ins.then_inc(bank_freed[bank_of[("kv", c, hp)]], 1)
                            dve.wait_ge(bank_freed[bank_of[("kv", c, hp)]], fills(("kv", c, hp)))
                    dve.sem_inc(done["state"], 1)
                ahead((("gb", 1), 1), 0)
                dve.wait_ge(done["summed"], nth("summed", ("o", 1)))
                ts(hs[:, 0:8], hs[:, 0:8], 1.0 / SEQ, EPS, ALU.mult, ALU.add).then_inc(done["meansq"], 1)
                dve.wait_ge(done["meansq"], nth("meansq", "o"))
                dve.wait_ge(done["rstd"], nth("rstd", "o"))
                dve.wait_ge(done["gates"], nth("gates", "rb"))
                for t in range(2):
                    o3 = xn[:, t, :].rearrange("p (h s) -> p h s", s=SEQ)
                    tt(o3, o3, hr[:, 4 * t:4 * t + 4].unsqueeze(2).broadcast_to([P, 4, SEQ]), ALU.mult).then_inc(vector_step, 1)
                    dve.wait_ge(vector_step, step.next())
                    tt(xn[:, t, :], xn[:, t, :], rb[:, t, :], ALU.mult).then_inc(done["rows"], 1)
                    dve.wait_ge(done["rows"], nth("rows", ("o", t)))
                ahead(("pa", 1), 0)
                turned("o", g2("o"), h_full2)
                for i, n in enumerate(("pa", "pb")):
                    for c in range(2):
                        ahead(("pa", c) if i == 0 else (("pb", c), 1), 1)
                        dve.wait_ge(done["gates"], nth("gates", ("ga", "gb")[i]))
                        for t in range(2):
                            dve.wait_ge(bank_filled[bank_of[(n, c, t)]], fills((n, c, t)))
                            p_ = psum((n, c, t))
                            dst, g_ = xn[:, t, c * 512:c * 512 + 512], gab[:, t, i, c * 512:c * 512 + 512]
                            if i == 0:
                                tt(dst, p_, g_, ALU.mult).then_inc(bank_freed[bank_of[(n, c, t)]], 1)
                                dve.wait_ge(bank_freed[bank_of[(n, c, t)]], fills((n, c, t)))
                            else:
                                tt(scr2[:, 0:512], p_, g_, ALU.mult).then_inc(bank_freed[bank_of[(n, c, t)]], 1)
                                dve.wait_ge(bank_freed[bank_of[(n, c, t)]], fills((n, c, t)))
                                ins = tt(dst, dst, scr2[:, 0:512], ALU.add)
                                if c == 1:
                                    ins.then_inc(done["rows"], 1)
                                    dve.wait_ge(done["rows"], nth("rows", ("m2", t)))
                                else:
                                    ins.then_inc(vector_step, 1)
                                    dve.wait_ge(vector_step, step.next())
                turned("m2", None, None)
                ahead((("wo2", 1), 1), 1)
                residual(lambda c, t: ("wo2", c, t), "wo2")
                normed("n3", x_sb)
                ahead(mid[-1], 0)
                turned("n3", g2("n3"), h_full2)
                glu("ff2", hid2, sil2, TAIL_FF, 2)
                residual(lambda c, t: ("ff2", "acc", t, c), "ff2", 0.5)
                step.end(LAYERS)
                del regs["layer"]

        @block.gpsimd
        def _(pool):
            E = Engine(counts_steps=True)
            nth, step = E.nth, E.step
            pool.memset(zero_b[:, :], 0.0).then_inc(zeroed, 1)
            pool.memset(bn, 0.0).then_inc(ssm_zeroed, 1)
            pool.memset(cn, 0.0).then_inc(ssm_zeroed, 1)
            pool.wait_ge(ssm_zeroed, 2)
            n = 0
            with nc.allow_non_contiguous_dma(reason="state space parameters, one word for each state"):
                for g in range(2):
                    rows = slice(64 * g, 64 * g + 64)
                    for i, name in ((1, "lam_re"), (2, "lam_im")):
                        pool.dma_start(par[rows, i, :], A[name][0, g::2].rearrange("t p -> p t")).then_inc(ssm_loaded, 16)
                        n += 1
                    pool.dma_start(par[rows, 0, :], A["log_dt"][0, g::2].partition_broadcast(64)).then_inc(ssm_loaded, 16)
                    n += 1
                    for i, name in enumerate(("b_re", "b_im")):
                        pool.dma_start(bn[rows, i, :, 16 * g:16 * g + 16],
                                       A[name][0, g::2].rearrange("t p h -> p t h")).then_inc(ssm_loaded, 16)
                        n += 1
            for r in range(8):
                for i, name in enumerate(("c_re", "c_im")):
                    pool.dma_start(cn[16 * r:16 * r + 16, i, :, 64 * (r % 2):64 * (r % 2) + 64],
                                   A[name][0, r::8].rearrange("j h p -> h j p")).then_inc(ssm_loaded, 16)
                    n += 1
            assert 16 * n == SSM_LOADS, n
            for T in range(SSM_TILES):
                pool.wait_ge(done["scanned"], nth("scanned", T))
                s_ = s_rot[:, T % 2]
                cosb, sinb = (x_[:, T:T + 1, :].broadcast_to([P, 2, SEQ]) for x_ in (cos_t, sin_t))
                pool.tensor_tensor(sc_p, s_, sinb, ALU.mult).then_inc(pool_step, 1)
                pool.wait_ge(pool_step, step.next())
                pool.tensor_tensor(s_, s_, cosb, ALU.mult).then_inc(pool_step, 1)
                pool.wait_ge(pool_step, step.next())
                if T >= 1:
                    pool.wait_ge(done["mixed"], nth("mixed", T - 1))
                pool.tensor_tensor(s_out[:, 0], s_[:, 0], sc_p[:, 1], ALU.subtract).then_inc(pool_step, 1)
                pool.wait_ge(pool_step, step.next())
                pool.tensor_tensor(s_out[:, 1], s_[:, 1], sc_p[:, 0], ALU.add).then_inc(done["rotated"], 1)
                pool.wait_ge(done["rotated"], nth("rotated", T))


_CONSTANTS = ("ident", "inv_freq", "t_row", "first_key", "rope2", "swa_bias", "reset", "gla_mask")


def shape_constants():
    pos = np.arange(SEQ, dtype=np.float32)
    inv = (1.0 / (10000.0 ** (np.arange(0, 64, 2, dtype=np.float32) / 64))).astype(np.float32)
    ang = (pos[:, None] * inv[None, :]).astype(np.float32)
    cos, sin = np.cos(ang), np.sin(ang)
    q, k = np.arange(SEQ)[:, None], np.arange(SEQ)[None, :]
    s, t = np.arange(P)[:, None], np.arange(P)[None, :]
    return {
        "ident": np.eye(P, dtype=np.float32),
        "inv_freq": inv,
        "t_row": pos,
        "first_key": np.concatenate([np.arange(32, 0, -1), np.arange(8, 0, -1) - 4]).astype(np.float32),
        "rope2": np.concatenate([cos, cos, -sin, sin], axis=1).astype(np.float32),
        "swa_bias": np.where((k <= q) & (k > q - 128), 0.0, NEG).astype(np.float32),
        "reset": (np.arange(SEQ) % GLA_CHUNK != 0).astype(np.float32),
        "gla_mask": ((s <= t) & (s // GLA_CHUNK == t // GLA_CHUNK)).astype(np.float32),
    }


def kernel(**inputs):
    import concourse.bacc as _bacc
    from concourse.bass_utils import run_bass_kernel_spmd as _run

    nc = _bacc.Bacc("TRN2", target_bir_lowering=False, num_devices=1)
    arrays, aps = {}, {}
    for name, a in {**inputs, **shape_constants()}.items():
        a = np.ascontiguousarray(a)
        arrays[f"in_{name}"] = a
        aps[name] = nc.dram_tensor(f"in_{name}", a.shape, mybir.dt.from_np(a.dtype), kind="ExternalInput").ap()
    out = nc.dram_tensor("out_x", (1, SEQ, D), F32, kind="ExternalOutput").ap()
    bass_hybrid_moe_then_swa_gla(nc, aps, out)
    r = _run(nc, [arrays], core_ids=[0])
    return r.results[0]["out_x"]
```

```python
from contextlib import ExitStack

import numpy as np
import concourse.bass as bass
from concourse import mybir

F32 = mybir.dt.float32
F32R = mybir.dt.float32r
BF16 = mybir.dt.bfloat16
I32 = mybir.dt.int32
ALU = mybir.AluOpType
ACT = mybir.ActivationFunctionType
AX = mybir.AxisListType.X

P = 128
D = 1024
KB = D // P
SEQ = 256
NT = SEQ // P
EPS = 1e-6
NEG = -1e30
GONE = -3e38
TWO_PI = 6.283185307179586
ROUND = 12582912.0
COARSE = 768.0

SSM_TILES = 16
EXPERTS = 32
GROUPS = 4
LAYERS = 2
FF2 = 2816
CHUNK_FF = 512
FULL_CHUNKS = FF2 // CHUNK_FF
TAIL_FF = FF2 - FULL_CHUNKS * CHUNK_FF
GLA_CHUNK = 64
TOPK = SEQ // 4

RAW = 3
SPLIT = 3
UNIT = 2048

IN1 = dict(u=(0, 512), q=(512, 512), kvi=(1024, 452), qm=(1476, 512), gate=(1988, 3072))
SCAN_PANELS = ("km", "vm", "kvi", "q", "qm")
IN2 = dict(qa=(0, 512), kva=(512, 256), qb=(768, 512), kb=(1280, 512), vb=(1792, 1024),
           rb=(2816, 1024), glr=(3840, 16), ga=(3856, 1024), gb=(4880, 1024))


SIGNALS = ("meansq rstd rows gained turned_hi turned ssm_act ssm_vec ssm_params ssm_weights trig angle rope_angle "
           "rope_trig u_rows scanned rotated mixed gelu_in gelu gelu_split evacuated heads heads_turned values "
           "relued maxed exped probs probs_turned branch gates residual route_in route silu hidden "
           "hidden_turned gate_ln decay decay_exp decayed gk_turned masked state columns").split()
VECTOR_STEPS_LAYER = 70
SCALAR_STEPS_LAYER = 40


class Order:

    def __init__(self):
        self.n, self.at, self.open, self.per = 0, {}, [], {}

    def event(self, name, by=1):
        assert name not in self.at, name
        self.at[name] = (self.n, tuple(x for x, _ in self.open))
        self.n += by

    def begin(self, loop):
        self.open.append((loop, self.n))

    def end(self, trips):
        loop, start = self.open.pop()
        self.per[loop] = self.n - start
        self.n = start + self.per[loop] * trips

    def number(self, name, regs):
        n, loops = self.at[name]
        for x in loops:
            n = regs[x] * self.per[x] + n
        return n


class Tally:

    def __init__(self):
        self.n, self.open = 0, []

    def next(self):
        self.n += 1
        return self.value()

    def value(self, back=0):
        value = self.n + back
        for reg, per, _ in self.open:
            value = reg * per + value
        return value

    def begin(self, reg, per):
        self.open.append((reg, per, self.n))

    def end(self, trips):
        _, per, start = self.open.pop()
        assert self.n - start == per, ("steps in a trip", self.n - start, per)
        self.n = start + per * trips


def plan():
    units, shape = Order(), {}
    marks = {s: Order() for s in SIGNALS}
    banks, fills, bank_of = [Order() for _ in range(8)], [], {}

    def unit(name, nk, w):
        units.event(name)
        shape[name] = (nk, w)

    def fill(name, b):
        banks[b].event(name)
        bank_of[name] = b
        fills.append(name)

    def begin(loop):
        units.begin(loop)
        for b in (*banks, *marks.values()):
            b.begin(loop)

    def end(trips):
        units.end(trips)
        for b in (*banks, *marks.values()):
            b.end(trips)

    def mark(signal, *events):
        for e in events:
            marks[signal].event(e)

    def turn(tag, into, rows=False, gained=True, stats=True):
        parts = [(tag, hh, t) for hh in range(2) for t in range(2)]
        if rows:
            mark("rows", *parts)
        if gained:
            mark("gained", *parts)
        mark("turned_hi", *parts); mark("turned", *parts)
        if stats:
            mark("rstd", tag)
        for b, (_, hh, t) in zip(into, parts):
            fill((tag + "T", hh, t), b)

    def panel(name, w=512, halves=2):
        for kh in range(halves):
            unit((name, kh), 4, w)

    turn("x", (0, 1, 2, 3))
    panel("u")
    fill(("uT", 0), 4); fill(("uT", 1), 5)
    fill(("rrow", "x"), 0)
    fill(("ssmT", 0), 1); fill(("ssmT", 1), 2)
    turn("mem", (3, 0, 1, 2))
    mark("ssm_act", 0, 1); mark("ssm_vec", 0, 1); mark("ssm_params", "b")
    mark("ssm_weights", 0, 1)
    mark("trig", 0, 1, 2, 3)
    mark("angle", 0, 1, 2, 3)
    mark("rope_angle", 0); mark("rope_trig", 0)
    mark("u_rows", 0, 1)
    mark("scanned", *range(SSM_TILES)); mark("rotated", *range(SSM_TILES)); mark("mixed", *range(SSM_TILES))
    mark("gelu_in", 0, 1); mark("gelu", 0, 1); mark("gelu_split", 0, 1)
    mark("meansq", "heads1"); mark("rstd", "heads1")
    mark("evacuated", *((n, t) for n in SCAN_PANELS for t in range(2)))
    mark("evacuated", ("glu", 0), ("glu", 1))
    mark("heads", "dq", "dk", "mq", "mk")
    for n in SCAN_PANELS:
        panel(n, IN1[n][1] if n in IN1 else 512)
    for h in range(2):
        fill(("y", h), 6 + h)
    for T in range(SSM_TILES):
        fill(("bu", T), T % 4)
        if T % 3 == 0 and T // 3 < len(SCAN_PANELS):
            for t in range(2):
                fill((SCAN_PANELS[T // 3], t), 4 + t)
    for c in range(6):
        panel(("gate", c))
        for t in range(2):
            fill(("gate", c, t), 4 + 2 * (c % 2) + t)
        if c == 0:
            unit(("glu", 0), 4, 512)
            fill(("glu", 0), 0); fill(("glu", 1), 1)
    small_bank = [0]

    def small(name):
        fill(name, small_bank[0] % 4)
        small_bank[0] += 1
    small_bank[0] = 2
    for t in range(2):
        small(("dqT", t)); small(("dkT", t))
    for t in range(2):
        for p in range(2):
            small(("isc", t, p))

    mark("heads_turned", ("dqT", 0), ("dkT", 0), ("dqT", 1), ("dkT", 1))
    mark("values", "dsa")
    mark("relued", (0, 0), (0, 1), (1, 0), (1, 1))

    def attention(tag, pairs):
        for t in range(2):
            mark("maxed", (tag, t)); mark("exped", (tag, t)); mark("probs", (tag, t))
            mark("probs_turned", *((tag, t, p) for p in range(pairs)))
            mark("branch", (tag, t))
            for p in range(pairs):
                small((tag, "S", t, p))
            for p in range(pairs):
                small((tag, "PT", t, p))
            small((tag, "O", t))
    mark("branch", "ssm")
    attention("dsa", 4)
    mark("heads_turned", ("mqT", 0), ("mkT", 0), ("mqT", 1), ("mkT", 1))
    for t in range(2):
        small(("mqT", t)); small(("mkT", t))
    attention("mem", 2)
    mark("gates", "ssm", "dsa", "mem")
    for i, br in enumerate(("ssm", "dsa", "mem")):
        for c in range(2):
            unit(("up", br, c), 4, 512)
            for t in range(2):
                fill(("up", br, c, t), 4 * ((i + 1) % 2) + 2 * c + t)
    turn("m", (0, 1, 2, 3), rows=True, gained=False, stats=False)
    for c in range(2):
        panel(("wo", c))
        for t in range(2):
            fill(("wo", c, t), 4 + 2 * c + t)
    mark("residual", *(("wo", c, t) for c in range(2) for t in range(2)))
    turn("f", (0, 1, 2, 3))
    mark("route_in", 0, 1); mark("route", "exp", "expert")
    for t in range(2):
        fill(("rt", t), 6 + t)

    def gate_up(name, tag, w):
        for kh in range(2 if w == 512 else 1):
            unit((name, tag, kh), 4 if w == 512 else 8, w)

    def glu_loop(tag, loop, trips, tail):
        gate_up("g", (tag, "first"), 512)
        for t in range(2):
            fill((tag, "first", "g", t), t)
        for c in range(2):
            for t in range(2):
                fill((tag, "acc", c, t), 4 + 2 * c + t)
        mark("silu", (tag, "first", 0), (tag, "first", 1))
        begin(loop)
        body(tag, "loop", 512)
        end(trips)
        if tail:
            body(tag, "last", tail)
            last(tag, tail)
        else:
            last(tag, 512)
        mark("residual", *((tag, c, t) for c in range(2) for t in range(2)))

    def body(tag, which, w_next):
        k = (tag, which)
        mark("hidden", (*k, 0), (*k, 1)); mark("silu", (*k, 0), (*k, 1)); mark("hidden_turned", (*k, 0), (*k, 1))
        gate_up("u", k, 512)
        for t in range(2):
            fill((*k, "u", t), 2 + t)
        gate_up("g", k, w_next)
        for t in range(2):
            fill((*k, "g", t), t)
        for t in range(2):
            fill((*k, "hT", t), 2 + t)
        for c in range(2):
            unit(("d", k, c), 4, 512)

    def last(tag, w):
        k = (tag, "end")
        mark("hidden", (*k, 0), (*k, 1)); mark("hidden_turned", (*k, 0), (*k, 1))
        gate_up("u", k, w)
        for t in range(2):
            fill((*k, "u", t), 2 + t)
        for t in range(2):
            fill((*k, "hT", t), 2 + t)
        for c in range(2):
            unit(("d", k, c), w // P, 512)

    glu_loop("moe", "moe", EXPERTS - 1, 0)

    begin("layer")
    turn("n1", (2, 3, 4, 5))
    glu_loop("ff1", "ff1", FULL_CHUNKS - 1, TAIL_FF)
    turn("n2", (2, 3, 0, 1))
    mark("evacuated", *((n, t) for n in ("qa", "kva") for t in range(2)))
    mark("meansq", "heads2"); mark("rstd", "heads2")
    mark("heads", "sq", "sk")
    mark("heads_turned", ("sqT", 0), ("sqT", 1), ("skT", 0))
    mark("values", "swa")
    mark("columns", "qbT", "kbT", "glrT"); mark("gate_ln", 0); mark("decay", 0, 1, 2); mark("decay_exp", *range(4)); mark("decayed", "ku", "qq", "q", "k")
    mark("evacuated", *((n, c, t) for n in ("vb",) for c in range(2) for t in range(2)))
    mark("gk_turned", 0, 1); mark("masked", 0, 1); mark("state", *range(3))
    mark("evacuated", *(("ob", t, hp) for t in range(2) for hp in range(2)))
    mark("gates", "rb", "ga", "gb")
    panel("qa")
    for t in range(2):
        fill(("qa", t), 4 + t)
    unit(("kva", 0), 8, 256)
    for t in range(2):
        fill(("kva", t), 6 + t)
    small_bank[0] = 0
    small(("rrow", "n2"))
    for t in range(2):
        small(("sqT", t))
    small(("skT", 0))
    panel("qb")
    fill(("qbT", 0), 4); fill(("qbT", 1), 5)
    panel("kb")
    fill(("kbT", 0), 6); fill(("kbT", 1), 7)
    unit(("glr", 0), 8, 16)
    small(("glrT", 0))
    for i in range(2):
        small(("lgT", i))
    for i, n in enumerate(("vb", "rb", "ga", "gb")):
        for c in range(2):
            panel((n, c))
            for t in range(2):
                if (n, c) != ("gb", 1):
                    fill((n, c, t), 4 + 2 * (c % 2) + t)
    attention("swa", 4)
    for t in range(2):
        small(("gkT", t))
    for t in range(2):
        small(("A", t))
    for c in range(3):
        for hp in range(2):
            small(("kv", c, hp))
    for t in range(2):
        for hp in range(2):
            fill(("ob", t, hp), 4 + 2 * t + hp)
    fill(("gb", 1, 0), 6); fill(("gb", 1, 1), 7)
    mark("rstd", "o")
    turn("o", (0, 1, 2, 3), rows=True, stats=False)
    for c in range(2):
        unit(("pa", c), 4, 512)
        for t in range(2):
            fill(("pa", c, t), 4 + 2 * c + t)
    for c in range(2):
        panel(("pb", c))
        for t in range(2):
            fill(("pb", c, t), 2 * c + t)
    turn("m2", (4, 5, 6, 7), rows=True, gained=False, stats=False)
    for c in range(2):
        panel(("wo2", c))
        for t in range(2):
            fill(("wo2", c, t), 2 * c + t)
    mark("residual", *(("wo2", c, t) for c in range(2) for t in range(2)))
    turn("n3", (4, 5, 6, 7))
    glu_loop("ff2", "ff2", FULL_CHUNKS - 1, TAIL_FF)
    end(LAYERS)
    assert RAW == SPLIT == 3 and all(n % RAW == 0 for n in units.per.values()), units.per
    return units, shape, banks, bank_of, marks


def bass_hybrid_moe_then_swa_gla(nc, A, out):
    units, unit_shape, banks, bank_of, marks = plan()
    unit_names = list(units.at)

    with ExitStack() as ctx:
        def sbuf(name, shape, dt=F32):
            return ctx.enter_context(nc.sbuf_tensor(name, shape, dt))

        def semaphore(name):
            return ctx.enter_context(nc.semaphore(name))

        raw = sbuf("raw", [P, RAW, UNIT])
        w_hi = sbuf("w_hi", [P, SPLIT, UNIT], F32R)
        w_lo = sbuf("w_lo", [P, SPLIT, UNIT], F32R)
        a_hi = sbuf("a_hi", [P, KB, SEQ], F32R)
        a_lo = sbuf("a_lo", [P, KB, SEQ], F32R)
        y_hi = sbuf("y_hi", [P, 3, 4, SEQ], F32R)
        y_lo = sbuf("y_lo", [P, 3, 4, SEQ], F32R)
        x_sb = sbuf("x_sb", [P, NT, D])
        xn = sbuf("xn", [P, NT, D])
        C_SIZE = 1064
        C = sbuf("C", [P, C_SIZE])
        W_SIZE = 19304
        W = sbuf("W", [P, W_SIZE])
        zero_b = sbuf("zero_b", [P, P], BF16)
        posi = sbuf("posi", [P, 2], I32)
        ps = ctx.enter_context(nc.psum_tensor("ps", [P, 8, 512], F32))

        used = [0]

        def const(n):
            used[0] += n
            assert used[0] <= C_SIZE
            return C[:, used[0] - n:used[0]]

        ident = const(P)
        gain = {n: const(KB) for n in ("mem", "x", "f")}
        gain2 = {n: const(LAYERS * KB).rearrange("p (l k) -> p l k", k=KB) for n in ("n1", "n2", "n3", "o")}
        swa_gain = const(LAYERS * 2 * 64).rearrange("p (l a d) -> p l a d", a=2, d=64)
        sinks = const(LAYERS * 8).rearrange("p (l h) -> p l h", h=8)
        gate_bias = const(LAYERS * 4).rearrange("p (l m) -> p l m", m=4)
        d_skip = const(4)
        w_route = const(KB * 36).rearrange("p (k n) -> p k n", n=36)
        b_route = const(36)
        first_key = const(40)
        half_pi = const(1)
        eps = const(1)
        packed = used[0]
        pos_col = const(2)
        st_ss = const(2)
        r_of = {n: const(2) for n in ("mem", "x", "f", "n1", "n2", "n3")}
        comb = const(2 * EXPERTS).rearrange("p (t e) -> p t e", e=EXPERTS)
        comb4 = comb[:, 0, 0:16].rearrange("p (h c) -> p h c", c=4)
        hs = const(40)
        hr = const(40)
        mx = const(8)
        sm = const(8)
        rs = const(8)
        snk = const(8)

        def area(off, *shape):
            n = int(np.prod(shape))
            assert off + n <= W_SIZE, (off, shape)
            v = W[:, off:off + n]
            if len(shape) == 2:
                return v.rearrange("p (a b) -> p a b", b=shape[1])
            if len(shape) == 3:
                return v.rearrange("p (a b c) -> p a b c", b=shape[1], c=shape[2])
            if len(shape) == 4:
                return v.rearrange("p (a b c d) -> p a b c d", b=shape[1], c=shape[2], d=shape[3])
            return v

        o = 0
        o_q = o; q_sb = area(o, 2, 512); o += 1024
        o_kvi = o; kvi = area(o, 2, 452); o += 904
        o_qm = o; qm_sb = area(o, 2, 512); o += 1024
        o_km = o; km_sb = area(o, 2, 512); o += 1024
        vm_sb = area(o, 2, 512); o += 1024
        rope1 = area(o, 2, 2, 64); o += 256
        pos_row = area(o, SEQ); o += 256
        head_rows = area(o, SEQ + 384 + 32)
        t_row = area(o, SEQ); o += 256
        g_q1 = area(o, 64); g_k1 = area(o + 64, 64); g_qm1 = area(o + 128, P); g_km1 = area(o + 256, P); o += 384
        inv_freq = area(o, 32); o += 32
        base1 = o
        cos_t = area(o, SSM_TILES, SEQ); o_cos = o; o += 4096
        sin_t = area(o, SSM_TILES, SEQ); o_sin = o; o += 4096
        bb = area(o, 2, 4, P); o += 1024
        cc = area(o, 2, SSM_TILES, 32); o += 1024
        o_scan = o
        s_rot = area(o, 2, 2, SEQ); o += 1024
        s_out = area(o, 2, SEQ); o += 512
        par = area(o, 12, SSM_TILES); o += 192
        u_f = area(o, 4, SEQ); u_flat = area(o, 1024); o += 1024
        junk_mem = area(o_cos + 3072, 1024)
        rope_tmp = area(o, 2, 64); o += 128
        assert o <= W_SIZE, o
        pos_row_i = area(o_kvi, SEQ).bitcast(I32)
        full1 = area(o_km, KB, SEQ)
        bn = area(o_q, 2, SSM_TILES, 32)
        rrow1 = area(o_qm, SEQ)
        bsc = area(o_scan, 2, SSM_TILES, 32)
        y_g = area(o_scan, 4, SEQ)
        m_hi, m_lo = (b[:, 0:2].rearrange("p a k s -> p (a k) s") for b in (y_hi, y_lo))
        sc_a = xn[:, 0, 0:512].rearrange("p (a b) -> p a b", b=SEQ)
        sc_b = xn[:, 0, 512:1024].rearrange("p (a b) -> p a b", b=SEQ)
        sc_p = xn[:, 1, 0:512].rearrange("p (a b) -> p a b", b=SEQ)
        o = base1
        gates1 = area(o, 2, 6, 512); o += 6144
        qT = area(o, 4, SEQ); o += 1024
        kT = area(o, 4, SEQ); o += 1024
        key_bias = area(o_q, 2, SEQ)
        vpad = area(o_q + 512, 2, 2, P)
        o_P = o; probs = area(o, 8, SEQ); o += 2048
        relu = area(o_P, 4, 2, SEQ)
        kdup = area(o_P, 2, 2, P)
        o_pT = o; probsT = area(o, 2, 8, P); o += 2048
        isc = area(o_pT, 2, SEQ)
        allow = area(o_pT + 512, 2, SEQ)
        top8 = area(o_pT + 1024, 8)
        scr1 = xn[:, 0, :]
        gated = area(o_P, 512)
        assert o <= W_SIZE, o
        h_full = area(o_cos, KB, SEQ)
        sil = area(o_cos + 2048, 2, 512)
        hid = area(o_cos + 3072, 2, 512)
        rt = area(o_cos + 4096, 2, 36)

        def rts(i, n):
            return area(o_cos + 4200 + 64 * i, 2, n)
        o = 0
        rope2 = area(o, 2, 2, 64); o += 256
        swa_bias = area(o, 2, SEQ); o += 512
        reset = area(o, SEQ); o += 256
        gla_mask = area(o, P); o += 128
        wgl = area(o, 512); o += 512
        o_qa = o; qa_sb = area(o, 2, 512); o += 1024
        kk = area(o_qa, 2, 512)
        kva = area(o, 2, 256); o += 512
        glrT = area(o, SEQ)
        vb = area(o, 2, 1024); o += 2048
        rrow2 = area(o, SEQ)
        rb = area(o, 2, 1024); o += 2048
        gab = area(o, 2, 2, 1024); o += 4096
        qbT = area(o, 4, SEQ); o += 1024
        kbT = area(o, 4, SEQ); o += 1024
        o_l = o
        qT2 = area(o, 4, SEQ); kT2 = area(o + 1024, 2, SEQ); vpad2 = area(o + 1536, 2, 2, 2, P)
        probsT2 = area(o + 2560, 2, 8, P); kdup2 = area(o + 2560, 2, 2, P)
        scr2 = area(o + 4608, 1024)
        gb_ = area(o + 4608, 4, SEQ)
        qqT = area(o, 4, SEQ)
        state = area(o + 1024, 3, 4, SEQ)
        am = area(o + 4608, 2, 4, P)
        probs2 = xn[:, :, :].rearrange("p a (h s) -> p (a h) s", s=SEQ)
        etmp = xn[:, 0, :].rearrange("p (a b) -> p a b", b=SEQ)
        kuT = xn[:, 1, :].rearrange("p (a b) -> p a b", b=SEQ)
        h_full2 = area(o, KB, SEQ)
        sil2 = area(o + 2048, 2, 512)
        hid2 = area(o + 3072, 2, 512)

        done = {s: semaphore(s) for s in SIGNALS}
        bank_filled = [semaphore(f"bank_filled{b}") for b in range(8)]
        bank_freed = [semaphore(f"bank_freed{b}") for b in range(8)]
        weights_loaded = [semaphore(f"weights_loaded{i}") for i in range(RAW)]
        hi_split = semaphore("hi_split")
        lo_split = semaphore("lo_split")
        unit_used = semaphore("unit_used")
        x_loaded = semaphore("x_loaded")
        mem_loaded = semaphore("mem_loaded")
        const_loaded = semaphore("const_loaded")
        rows_loaded = semaphore("rows_loaded")
        par_loaded = semaphore("par_loaded")
        b_loaded = semaphore("b_loaded")
        c_loaded = semaphore("c_loaded")
        pos_loaded = semaphore("pos_loaded")
        zeroed = semaphore("zeroed")
        block2_loaded = semaphore("block2_loaded")
        wgl_loaded = semaphore("wgl_loaded")
        stored = semaphore("stored")
        vector_step = semaphore("vector_step")
        scalar_step = semaphore("scalar_step")
        pool_step = semaphore("pool_step")
        pe_step = semaphore("pe_step")

        class Engine:

            def __init__(self, counts_steps=False):
                self.regs, self.cursor = {}, 0
                self.step = Tally() if counts_steps else None

            def nth(self, signal, event):
                return marks[signal].number(event, self.regs) + 1

            def fills(self, name):
                return banks[bank_of[name]].number(name, self.regs) + 1

            def psum(self, name):
                return ps[:, bank_of[name], :]

            def slot(self, name):
                return units.at[name][0] % 3

            def view(self, buf, name, rows=None):
                nk, w = unit_shape[name]
                return buf[:, self.slot(name), 0:nk * w].rearrange("p (k n) -> p k n", n=w)

            def unit_value(self, name, div=1, scale=1):
                n, loops = units.at[name]
                v = (n // div) * scale
                for x in loops:
                    v = self.regs[x] * (units.per[x] // div * scale) + v
                return v

        x_dram = A["x"].rearrange("a (t p) d -> p (a t) d", p=P)
        out_dram = out.rearrange("a (t p) d -> p (a t) d", p=P)

        def unit_source(name, regs):
            nk, w = unit_shape[name]

            def rows(m, kh, c0):
                return m[kh * nk * P:(kh + 1) * nk * P, c0:c0 + w].rearrange("(k p) n -> p k n", p=P)
            n0, n1 = name[0], name[1]
            if n0 in ("km", "vm"):
                return rows(A["w_mem_kv"][0], n1, 512 * (n0 == "vm"))
            if n0 in IN1 and len(name) == 2:
                return rows(A["w_in"][0], n1, IN1[n0][0])
            if n0 == "glu":
                return rows(A["w_glu"][0], 0, 0)
            if n0 == "up":
                return rows(A["w_up_" + n1][0], 0, 512 * name[2])
            if n0 in ("g", "u", "d"):
                (tag, which), part = name[1], name[2]
                shift = {"first": 0, "loop": 0, "last": FULL_CHUNKS - 1, "end": FULL_CHUNKS}[which]
                if tag == "moe":
                    e = EXPERTS - 1 if which == "end" else 0 if which == "first" else regs["moe"]
                    if n0 == "g" and which == "loop":
                        e = e + 1
                    m = A[{"g": "w_gate", "u": "w_up", "d": "w_down"}[n0]][0, e]
                    return rows(m, 0, 512 * part) if n0 == "d" else rows(m, part, 0)
                l = regs["layer"]
                m = A["ffn" + tag[2] + {"g": "_w_gate_2", "u": "_w_up_2", "d": "_w_down_2"}[n0]][l]
                c = shift if which in ("last", "end") else 0 if which == "first" else regs[tag]
                if n0 == "g" and which in ("loop", "last"):
                    c = c + 1
                if n0 == "d":
                    if which == "loop":
                        return m[bass.ds(c * 512, nk * P), 512 * part:512 * part + 512].rearrange("(k p) n -> p k n", p=P)
                    return m[c * 512:c * 512 + nk * P, 512 * part:512 * part + 512].rearrange("(k p) n -> p k n", p=P)
                if which == "loop":
                    return m[part * nk * P:(part + 1) * nk * P, bass.ds(c * 512, w)].rearrange("(k p) n -> p k n", p=P)
                return rows(m, part, c * 512)
            if isinstance(n0, tuple):
                kind, c = n0
                if kind == "gate":
                    return rows(A["w_in"][0], n1, IN1["gate"][0] + 512 * c)
                if kind == "wo":
                    return rows(A["w_out"][0], n1, 512 * c)
                if kind == "wo2":
                    return rows(A["w_out_2"][regs["layer"]], n1, 512 * c)
                if kind == "pb":
                    return rows(A["w_proj_b_2"][regs["layer"]], n1, 512 * c)
                return rows(A["w_in_2"][regs["layer"]], n1, IN2[kind][0] + 512 * c)
            if n0 == "pa":
                return rows(A["w_proj_a_2"][regs["layer"]], 0, 512 * n1)
            return rows(A["w_in_2"][regs["layer"]], n1, IN2[n0][0])

        def straight(lo_name, hi_name):
            i, j = unit_names.index(lo_name), unit_names.index(hi_name)
            return unit_names[i:j + 1]

        def in_trip(tag):
            return [n for n in unit_names if n[0] in ("g", "u", "d") and n[1] == (tag, "loop")]

        def after_trips(tag):
            return [n for n in unit_names if n[0] in ("g", "u", "d") and n[1] in ((tag, "last"), (tag, "end"))]

        FIRST = ("g", ("moe", "first"), 1)
        stretch1 = straight(("u", 0), FIRST)
        stretch_l1 = straight(("g", ("ff1", "first"), 0), ("g", ("ff1", "first"), 1))
        mid = unit_names[unit_names.index(("d", ("ff1", "end"), 1)) + 1:unit_names.index(("g", ("ff2", "first"), 1)) + 1]

        def trips_of(tag):
            return EXPERTS - 1 if tag == "moe" else FULL_CHUNKS - 1

        block = ctx.enter_context(nc.Block())

        @block.sync
        def _(sp):
            E = Engine()
            sp.dma_start(x_sb[:, :, :], x_dram).then_inc(x_loaded, 16)

            def load(name):
                n0 = units.at[name][0]
                if n0 >= RAW or E.regs:
                    sp.wait_ge(lo_split, E.unit_value(name) - (RAW - 1))
                sp.dma_start(E.view(raw, name), unit_source(name, E.regs)).then_inc(weights_loaded[E.slot(name)], 16)

            def load_loop(tag):
                with sp.Fori(0, trips_of(tag)) as i:
                    E.regs[tag] = i
                    for name in in_trip(tag):
                        load(name)
                    del E.regs[tag]
                for name in after_trips(tag):
                    load(name)

            for name in stretch1:
                load(name)
            load_loop("moe")
            with sp.Fori(0, LAYERS) as l:
                E.regs["layer"] = l
                for name in stretch_l1:
                    load(name)
                load_loop("ff1")
                for name in mid:
                    load(name)
                load_loop("ff2")
                del E.regs["layer"]
            sp.wait_ge(done["residual"], marks["residual"].n)
            sp.dma_start(out_dram, x_sb[:, :, :]).then_inc(stored, 16)
            sp.wait_ge(stored, 16)

        @block.tensor
        def _(pe):
            E = Engine(counts_steps=True)
            nth, regs, step = E.nth, E.regs, E.step

            def bank(name):
                b = bank_of[name]
                if banks[b].at[name][0] > 0:
                    pe.wait_ge(bank_freed[b], banks[b].number(name, regs))
                return ps[:, b, :]

            def fill(ins, name):
                ins.then_inc(bank_filled[bank_of[name]], 1)

            def unit(name):
                pe.wait_ge(lo_split, E.unit_value(name) + 1)
                return E.view(w_hi, name), E.view(w_lo, name)

            def split_products(dst, a_h, a_l, b_h, b_l, first, final, **kw):
                pe.matmul(dst, a_h, b_h, start=first, stop=False, **kw)
                pe.matmul(dst, a_h, b_l, start=False, stop=False, **kw)
                return pe.matmul(dst, a_l, b_h, start=False, stop=final, **kw)

            def close(name, dst, row=0, col=0):
                fill(pe.matmul(dst[row:row + 1, col:col + 1], zero_b[:, 0:1], zero_b[:, 0:1], start=False, stop=True,
                               skip_group_check=True, tile_position=(0, row)), name)

            def rows_unit(name, fills, dst, lhs, k0, first, final, fresh=None):
                hi, lo = unit(name)
                nk, w = unit_shape[name]
                for t in range(2):
                    if fresh:
                        pe.wait_ge(done["turned"], nth("turned", (fresh, k0 // 4, t)))
                    for k in range(nk):
                        m = split_products(dst[t][:, 0:w], lhs[0][:, k0 + k, t * P:t * P + P],
                                           lhs[1][:, k0 + k, t * P:t * P + P], hi[:, k, :], lo[:, k, :],
                                           first and k == 0, final and k == nk - 1 and t == 0, skip_group_check=True)
                    if final and t == 0:
                        fill(m, fills[0])
                m.then_inc(unit_used, 1)
                if final:
                    close(fills[1], dst[1])

            def rows_panel(names, fills, lhs=(a_hi, a_lo), fresh=None):
                dst, k0 = [bank(f) for f in fills], 0
                for i, name in enumerate(names):
                    rows_unit(name, fills, dst, lhs, k0, i == 0, i == len(names) - 1, fresh)
                    k0 += unit_shape[name][0]

            def columns_panel(names, fills, rhs=(a_hi, a_lo), m_blocks=4, m_width=P, fresh=None):
                dst, k0 = [bank(f) for f in fills], 0
                for i, name in enumerate(names):
                    hi, lo = unit(name)
                    nk = unit_shape[name][0]
                    if fresh:
                        pe.wait_ge(done["turned"], nth("turned", (fresh, k0 // 4, 1)))
                    for mb in range(m_blocks):
                        o_ = dst[mb // 2][0:m_width, (mb % 2) * SEQ:(mb % 2) * SEQ + SEQ]
                        for k in range(nk):
                            sl = slice(mb * m_width, (mb + 1) * m_width)
                            first = i == 0 and k == 0 and mb % 2 == 0
                            kw = dict(stop=False, skip_group_check=True)
                            pe.matmul(o_, hi[:, k, sl], rhs[0][:, k0 + k, :], start=first, **kw)
                            pe.matmul(o_, lo[:, k, sl], rhs[0][:, k0 + k, :], start=False, **kw)
                            m = pe.matmul(o_, hi[:, k, sl], rhs[1][:, k0 + k, :], start=False, **kw)
                    k0 += nk
                    m.then_inc(unit_used, 1)
                for f, d in zip(fills, dst):
                    close(f, d)

            def half_rows(names, lhs_of, rhs_of):
                dst = [bank(name) for name in names]
                for j in range(2):
                    for p, name in enumerate(names):
                        if j == 1:
                            pe.wait_ge(pe_step, step.value(p + 1 - len(names)))
                        m = pe.matmul(dst[p][:, j * SEQ:j * SEQ + SEQ], lhs_of(j, p), rhs_of(j, p), start=True, stop=True)
                        if j == 0:
                            m.then_inc(pe_step, 1)
                            step.n += 1
                        else:
                            fill(m, name)

            def halves(n):
                return [(n, 0), (n, 1)]

            def turn_blocks(name, sources):
                dst = bank(name)
                for j, src in enumerate(sources):
                    m = pe.transpose(dst[:, j * P:j * P + P], src, ident)
                fill(m, name)

            def turn_part(tag, hh, t, src):
                turn_blocks((tag + "T", hh, t), [src[:, t, (4 * hh + j) * P:(4 * hh + j + 1) * P] for j in range(4)])

            def turn_rows(tag, src=xn):
                for hh in range(2):
                    for t in range(2):
                        pe.wait_ge(done["rows"], nth("rows", (tag, hh, t)))
                        turn_part(tag, hh, t, src)

            def turn_residual(tag, event):
                for hh in range(2):
                    for t in range(2):
                        pe.wait_ge(done["residual"], nth("residual", (event, hh, t)))
                        turn_part(tag, hh, t, x_sb)

            def roots_as_row(tag):
                dst = bank(("rrow", tag))
                pe.wait_ge(done["rstd"], nth("rstd", tag))
                for t in range(2):
                    m = pe.matmul(dst[:, t * P:t * P + P], r_of[tag][:, t:t + 1].broadcast_to([P, P]), ident,
                                  start=True, stop=True)
                fill(m, ("rrow", tag))

            pe.wait_ge(const_loaded, 16)
            pe.wait_ge(zeroed, 1)
            pe.wait_ge(x_loaded, 16)
            for hh in range(2):
                for t in range(2):
                    turn_part("x", hh, t, x_sb)
            columns_panel(halves("u"), [("uT", 0), ("uT", 1)], fresh="x")
            roots_as_row("x")
            pe.wait_ge(done["ssm_params"], nth("ssm_params", "b"))
            for i in range(2):
                turn_blocks(("ssmT", i), [bsc[:, i, 4 * j:4 * j + 4, :].rearrange("p a b -> p (a b)") for j in range(4)])
            pe.wait_ge(mem_loaded, 16)
            for hh in range(2):
                for t in range(2):
                    turn_part("mem", hh, t, xn)
            pe.wait_ge(done["ssm_weights"], nth("ssm_weights", 1))
            pe.wait_ge(done["u_rows"], nth("u_rows", 1))
            y_dst = [bank(("y", h)) for h in range(2)]

            def read_out(T):
                pe.wait_ge(done["rotated"], nth("rotated", T))
                r, j = 32 * (T % 4), T // 4
                o_ = y_dst[j // 2][r:r + 32, (j % 2) * SEQ:(j % 2) * SEQ + SEQ]
                pe.matmul(o_, cc[:, 0, T, :], s_out[:, 0, :], start=True, stop=False, skip_group_check=True,
                          tile_position=(0, r))
                pe.matmul(o_, cc[:, 1, T, :], s_out[:, 1, :], start=False, stop=True, skip_group_check=True,
                          tile_position=(0, r)).then_inc(done["mixed"], 1)

            def drive(T):
                r, j = 32 * (T % 4), T // 4
                dst = bank(("bu", T))
                for i in range(2):
                    m = pe.matmul(dst[:, i * SEQ:i * SEQ + SEQ], bb[r:r + 32, i, j, :], u_f[r:r + 32, j, :],
                                  start=True, stop=True, tile_position=(r, 0))
                fill(m, ("bu", T))

            for T in range(3):
                drive(T)
            for T in range(SSM_TILES):
                if T + 3 < SSM_TILES:
                    drive(T + 3)
                if T % 3 == 0 and T // 3 < len(SCAN_PANELS):
                    n = SCAN_PANELS[T // 3]
                    rows_panel(halves(n), [(n, t) for t in range(2)], (m_hi, m_lo) if n in ("km", "vm") else (a_hi, a_lo),
                               "mem" if n == "km" else None)
                if T >= 2:
                    read_out(T - 2)
            read_out(SSM_TILES - 2)
            read_out(SSM_TILES - 1)
            for h in range(2):
                close(("y", h), y_dst[h], 96, SEQ)

            def gate(c):
                rows_panel(halves(("gate", c)), [("gate", c, t) for t in range(2)])

            gate(0)
            pe.wait_ge(done["gelu_split"], nth("gelu_split", 1))
            columns_panel([("glu", 0)], [("glu", 0), ("glu", 1)], (y_hi[:, 1], y_lo[:, 1]))
            gate(1)
            gate(2)
            for t in range(2):
                pe.wait_ge(done["heads"], nth("heads", "dq"))
                turn_blocks(("dqT", t), [q_sb[:, t, j * P:j * P + P] for j in range(4)])
                pe.wait_ge(done["heads"], nth("heads", "dk"))
                turn_blocks(("dkT", t), [kdup[:, 0, t, :], kdup[:, 1, t, :], kvi[:, t, 128:256], kvi[:, t, 256:384]])
            pe.wait_ge(done["heads_turned"], nth("heads_turned", ("dkT", 1)))
            for t in range(2):
                half_rows([("isc", t, p) for p in range(2)],
                          lambda j, p: kT[64 * j:64 * j + 64, 2 + p, t * P:t * P + P],
                          lambda j, p: kT[64 * j:64 * j + 64, 1, :])
            gate(3)

            def attention(tag, pairs, q_of, k_of, v_of, pT, p_src, meanwhile):
                for t in range(2):
                    half_rows([(tag, "S", t, p) for p in range(pairs)],
                              lambda j, p: q_of(2 * p + j, t), lambda j, p: k_of(2 * p + j))
                    meanwhile(t)
                    pe.wait_ge(done["probs"], nth("probs", (tag, t)))
                    for p in range(pairs):
                        turn_blocks((tag, "PT", t, p), [p_src[:, 2 * p + j, s_ * P:s_ * P + P]
                                                        for j in range(2) for s_ in range(2)])
                    dst = bank((tag, "O", t))
                    for i in range(4):
                        heads = [i] if pairs == 2 else [2 * i, 2 * i + 1]
                        pe.wait_ge(done["probs_turned"], nth("probs_turned", (tag, t, heads[-1] // 2)))
                        terms = [(h, s_) for h in heads for s_ in range(2)]
                        for n, (h, s_) in enumerate(terms):
                            m = pe.matmul(dst[:, i * P:i * P + P], v_of(h, s_), pT[:, s_, h, :],
                                          start=n == 0, stop=n == len(terms) - 1)
                    fill(m, (tag, "O", t))

            pe.wait_ge(done["values"], nth("values", "dsa"))
            attention("dsa", 4, lambda h, t: qT[64 * (h % 2):64 * (h % 2) + 64, h // 2, t * P:t * P + P],
                      lambda h: kT[64 * (h % 2):64 * (h % 2) + 64, 0, :], lambda h, s_: vpad[:, s_, h % 2, :],
                      probsT, probs, lambda t: gate(4 + t))
            pe.wait_ge(done["heads"], nth("heads", "mk"))
            for t in range(2):
                turn_blocks(("mqT", t), [qm_sb[:, t, j * P:j * P + P] for j in range(4)])
                turn_blocks(("mkT", t), [km_sb[:, t, j * P:j * P + P] for j in range(4)])
            pe.wait_ge(done["heads_turned"], nth("heads_turned", ("mkT", 1)))
            def up_ssm(c):
                pe.wait_ge(done["branch"], nth("branch", "ssm"))
                rows_panel([("up", "ssm", c)], [("up", "ssm", c, t) for t in range(2)], (y_hi[:, 0], y_lo[:, 0]))
            attention("mem", 2, lambda h, t: qT[:, h, t * P:t * P + P], lambda h: kT[:, h, :],
                      lambda h, s_: vm_sb[:, s_, h * P:h * P + P], probsT, probs, up_ssm)
            for i, br in ((1, "dsa"), (2, "mem")):
                pe.wait_ge(done["branch"], nth("branch", (br, 1)))
                for c in range(2):
                    rows_panel([("up", br, c)], [("up", br, c, t) for t in range(2)], (y_hi[:, i], y_lo[:, i]))
            turn_rows("m")
            for c in range(2):
                rows_panel(halves(("wo", c)), [("wo", c, t) for t in range(2)], fresh="m")
            turn_residual("f", "wo")
            def turn_hidden(k, src, nb):
                for t in range(2):
                    pe.wait_ge(done["hidden"], nth("hidden", (*k, t)))
                    turn_blocks((*k, "hT", t), [src[:, t, j * P:j * P + P] for j in range(nb)])

            def down(k, acc, nb):
                pe.wait_ge(done["hidden_turned"], nth("hidden_turned", (*k, 1)))
                for c in range(2):
                    hi, lo = unit(("d", k, c))
                    for t in range(2):
                        for j in range(nb):
                            m = split_products(acc[t][c], y_hi[:, 0, j, t * P:t * P + P], y_lo[:, 0, j, t * P:t * P + P],
                                               hi[:, j, :], lo[:, j, :], False, False, skip_group_check=True)
                    m.then_inc(unit_used, 1)

            def glu_trip(tag, which, acc, src, w_next):
                k = (tag, which)
                rows_panel([("u", k, 0), ("u", k, 1)], [(*k, "u", t) for t in range(2)])
                fills = [(*k, "g", t) for t in range(2)]
                dst = [bank(f) for f in fills]
                if w_next == 512:
                    rows_unit(("g", k, 0), fills, dst, (a_hi, a_lo), 0, True, False)
                    turn_hidden(k, src, 4)
                    rows_unit(("g", k, 1), fills, dst, (a_hi, a_lo), 4, False, True)
                else:
                    rows_unit(("g", k, 0), fills, dst, (a_hi, a_lo), 0, True, True)
                    turn_hidden(k, src, 4)
                down(k, acc, 4)

            def route():
                for t in range(2):
                    dst = bank(("rt", t))
                    for k in range(KB):
                        m = pe.matmul(dst[:, 0:36], h_full[:, k, t * P:t * P + P], w_route[:, k, :],
                                      start=k == 0, stop=k == KB - 1)
                    fill(m, ("rt", t))

            def glu(tag, src, tail, fresh):
                rows_panel([("g", (tag, "first"), 0), ("g", (tag, "first"), 1)],
                           [(tag, "first", "g", t) for t in range(2)], fresh=fresh)
                if tag == "moe":
                    route()
                acc = [[bank((tag, "acc", c, t)) for c in range(2)] for t in range(2)]
                for t in range(2):
                    for c in range(2):
                        for q in range(4):
                            pe.matmul(acc[t][c][:, q * P:q * P + P], zero_b[:, :], zero_b[:, :], start=q == 0,
                                      stop=False, skip_group_check=True)
                with pe.Fori(0, trips_of(tag)) as i:
                    regs[tag] = i
                    glu_trip(tag, "loop", acc, src, 512)
                    del regs[tag]
                if tail:
                    glu_trip(tag, "last", acc, src, tail)
                k = (tag, "end")
                w = tail or 512
                rows_panel([("u", k, 0), ("u", k, 1)] if w == 512 else [("u", k, 0)], [(*k, "u", t) for t in range(2)])
                turn_hidden(k, src, w // P)
                down(k, acc, w // P)
                for c in range(2):
                    for t in range(2):
                        close((tag, "acc", c, t), acc[t][c])

            glu("moe", hid, 0, "f")

            with pe.Fori(0, LAYERS) as l:
                regs["layer"] = l
                step.begin(l, 8)
                for hh in range(2):
                    for t in range(2):
                        pe.wait_ge(done["residual"], nth("residual", ("ff1", hh, t)) - 4)
                        turn_part("n1", hh, t, x_sb)
                glu("ff1", hid2, TAIL_FF, "n1")
                turn_residual("n2", "ff1")
                rows_panel(halves("qa"), [("qa", t) for t in range(2)], fresh="n2")
                rows_panel([("kva", 0)], [("kva", t) for t in range(2)])
                roots_as_row("n2")
                columns_panel(halves("qb"), [("qbT", 0), ("qbT", 1)])
                columns_panel(halves("kb"), [("kbT", 0), ("kbT", 1)])
                pe.wait_ge(done["heads"], nth("heads", "sq"))
                for t in range(2):
                    turn_blocks(("sqT", t), [qa_sb[:, t, j * P:j * P + P] for j in range(4)])
                pe.wait_ge(done["heads"], nth("heads", "sk"))
                turn_blocks(("skT", 0), [kdup2[:, g, t, :] for g in range(2) for t in range(2)])
                columns_panel([("glr", 0)], [("glrT", 0)], m_blocks=1, m_width=16)
                pe.wait_ge(done["columns"], nth("columns", "glrT"))
                pe.wait_ge(wgl_loaded, l * 16 + 16)
                for i in range(2):
                    dst = bank(("lgT", i))
                    for j in range(2):
                        mb = 2 * i + j
                        m = pe.matmul(dst[:, j * SEQ:j * SEQ + SEQ], wgl[0:16, mb * P:mb * P + P], glrT[0:16, :],
                                      start=True, stop=True)
                    fill(m, ("lgT", i))

                def wide(n, c):
                    rows_panel(halves((n, c)), [(n, c, t) for t in range(2)])

                pe.wait_ge(done["heads_turned"], nth("heads_turned", ("skT", 0)))
                pe.wait_ge(done["values"], nth("values", "swa"))
                attention("swa", 4, lambda h, t: qT2[64 * (h % 2):64 * (h % 2) + 64, h // 2, t * P:t * P + P],
                          lambda h: kT2[64 * (h % 2):64 * (h % 2) + 64, h // 4, :],
                          lambda h, s_: vpad2[:, s_, h // 4, h % 2, :], probsT2, probs2, lambda t: wide("vb", t))
                wide("rb", 0)
                wide("rb", 1)
                wide("ga", 0)
                pe.wait_ge(done["decayed"], nth("decayed", "ku"))
                for t in range(2):
                    turn_blocks(("gkT", t), [kuT[:, j, t * P:t * P + P] for j in range(4)])
                pe.wait_ge(done["decayed"], nth("decayed", "k"))
                for t in range(2):
                    dst = bank(("A", t))
                    for h in range(4):
                        m = pe.matmul(dst[:, h * P:h * P + P], kbT[:, h, t * P:t * P + P], qbT[:, h, t * P:t * P + P],
                                      start=True, stop=True)
                    fill(m, ("A", t))
                pe.wait_ge(done["evacuated"], nth("evacuated", ("vb", 1, 1)))
                pe.wait_ge(done["gk_turned"], nth("gk_turned", 1))
                for c in range(3):
                    r = 64 * (c % 2)
                    for hp in range(2):
                        dst = bank(("kv", c, hp))
                        for j in range(2):
                            h = 2 * hp + j
                            m = pe.matmul(dst[:, j * SEQ:j * SEQ + SEQ], kk[r:r + 64, c // 2, h * P:h * P + P],
                                          vb[r:r + 64, c // 2, h * SEQ:h * SEQ + SEQ], start=True, stop=True)
                        fill(m, ("kv", c, hp))
                wide("ga", 1)
                wide("gb", 0)
                pe.wait_ge(done["decayed"], nth("decayed", "qq"))
                pe.wait_ge(done["masked"], nth("masked", 1))
                pe.wait_ge(done["state"], nth("state", 2))
                for t in range(2):
                    for hp in range(2):
                        dst = bank(("ob", t, hp))
                        for j in range(2):
                            h = 2 * hp + j
                            o_ = slice(j * SEQ, j * SEQ + SEQ)
                            pe.matmul(dst[:, o_], am[:, t, h, :], vb[:, t, h * SEQ:h * SEQ + SEQ], start=True,
                                      stop=False, skip_group_check=True)
                            for c in (1,) if t == 0 else (2, 3):
                                r = 64 * (c % 2)
                                pe.matmul(dst[r:r + 64, o_], qqT[:, h, c * 64:c * 64 + 64], state[:, c - 1, h, :],
                                          start=False, stop=False, skip_group_check=True, tile_position=(0, r))
                        close(("ob", t, hp), dst, 0, SEQ)
                wide("gb", 1)
                pe.wait_ge(done["branch"], nth("branch", ("swa", 1)))
                for c in range(2):
                    rows_panel([("pa", c)], [("pa", c, t) for t in range(2)], (y_hi[:, 0], y_lo[:, 0]))
                turn_rows("o")
                for c in range(2):
                    rows_panel(halves(("pb", c)), [("pb", c, t) for t in range(2)], fresh="o")
                turn_rows("m2", rb)
                for c in range(2):
                    rows_panel(halves(("wo2", c)), [("wo2", c, t) for t in range(2)], fresh="m2")
                turn_residual("n3", "wo2")
                glu("ff2", hid2, TAIL_FF, "n3")
                step.end(LAYERS)
                del regs["layer"]

        def split_ahead(E, names, emit, name, extra):
            stop = min(names.index(name) + extra + 1, len(names))
            while E.cursor < stop:
                emit(names[E.cursor])
                E.cursor += 1

        @block.scalar
        def _(act):
            E = Engine(counts_steps=True)
            nth, regs, step, fills, psum = E.nth, E.regs, E.step, E.fills, E.psum

            act.dma_start(C[:, 0:packed], A["packed"]).then_inc(const_loaded, 16)
            act.dma_start(par[:, 0:3], A["ssm_params"].rearrange("p (a t) -> p a t", a=3)).then_inc(par_loaded, 16)
            act.dma_start(head_rows, A["head_rows"].partition_broadcast(P)).then_inc(rows_loaded, 16)
            with nc.allow_non_contiguous_dma(reason="positions as a column"):
                act.dma_start(posi[:, :], A["positions"].rearrange("a (t p) -> p (a t)", p=P)).then_inc(pos_loaded, 16)
            act.dma_start(pos_row_i, A["positions"][0].partition_broadcast(P)).then_inc(pos_loaded, 16)
            act.dma_start(bn.rearrange("p a t c -> p (a t c)"), A["ssm_b"]).then_inc(b_loaded, 16)
            act.dma_start(xn[:, :, :], A["mem"].rearrange("a (t p) d -> p (a t) d", p=P)).then_inc(mem_loaded, 16)
            act.dma_start(cc.rearrange("p a t c -> p (a t c)"), A["ssm_c"]).then_inc(c_loaded, 16)

            def hi(name, ahead=0):
                n0 = units.at[name][0] + ahead
                if n0 >= SPLIT or regs:
                    act.wait_ge(unit_used, E.unit_value(name) + (ahead - (SPLIT - 1)))
                act.wait_ge(weights_loaded[E.slot(name)], 16 + E.unit_value(name, 3, 16) + ahead // 3 * 16)
                act.activation(E.view(w_hi, name), E.view(raw, name), ACT.Copy).then_inc(hi_split, 1)

            def copy_out(name, signal_event, dst, src=None, func=ACT.Copy, scale=1.0, signal="evacuated"):
                act.wait_ge(bank_filled[bank_of[name]], fills(name))
                p_ = psum(name)
                if src is not None:
                    p_ = src(p_)
                act.activation(dst, p_, func, scale=scale).then_inc(bank_freed[bank_of[name]], 1)
                act.wait_ge(bank_freed[bank_of[name]], fills(name))
                if signal_event is not None:
                    act.sem_inc(done[signal], 1)

            def inverse_root(event, sums, r, n):
                act.activation(r, sums, ACT.Ln, scale=1.0 / n, bias=eps).then_inc(scalar_step, 1)
                act.wait_ge(scalar_step, step.next())
                act.activation(r, r, ACT.Exp, scale=-0.5).then_inc(done["rstd"], 1)
                act.wait_ge(done["rstd"], nth("rstd", event))

            def stats(tag, src, junk):
                for t in range(2):
                    act.activation(junk, src[:, t, :], ACT.Square, accum_out=st_ss[:, t:t + 1]).then_inc(scalar_step, 1)
                    act.wait_ge(scalar_step, step.next())
                inverse_root(tag, st_ss, r_of[tag], D)

            def turned_hi(tag, full=None, to=a_hi):
                for hh in range(2):
                    for t in range(2):
                        at = (slice(None), slice(4 * hh, 4 * hh + 4), slice(t * P, t * P + P))
                        if full is not None:
                            act.wait_ge(done["gained"], nth("gained", (tag, hh, t)))
                            src = full[at]
                        else:
                            name = (tag + "T", hh, t)
                            act.wait_ge(bank_filled[bank_of[name]], fills(name))
                            src = psum(name).rearrange("p (k s) -> p k s", s=P)
                        act.activation(to[at], src, ACT.Copy).then_inc(done["turned_hi"], 1)
                        act.wait_ge(done["turned_hi"], nth("turned_hi", (tag, hh, t)))

            def ahead(name, extra=1):
                split_ahead(E, stretch, hi, name, extra)

            stretch = stretch1
            act.wait_ge(const_loaded, 16)
            ahead(("u", 0), 0)
            turned_hi("x", full1)
            ahead(("u", 1), 0)
            act.wait_ge(par_loaded, 16)
            act.activation(par[:, 3], par[:, 0], ACT.Exp).then_inc(done["ssm_act"], 1)
            act.wait_ge(done["ssm_act"], nth("ssm_act", 0))
            act.wait_ge(done["ssm_vec"], nth("ssm_vec", 0))
            act.activation(par[:, 9], par[:, 4], ACT.Exp).then_inc(scalar_step, 1)
            act.wait_ge(scalar_step, step.next())
            act.activation(par[:, 10], par[:, 6], ACT.Abs).then_inc(scalar_step, 1)
            act.wait_ge(scalar_step, step.next())
            act.activation(par[:, 10], par[:, 10], ACT.Sin, scale=-6.283185, bias=half_pi).then_inc(scalar_step, 1)
            act.wait_ge(scalar_step, step.next())
            act.activation(par[:, 11], par[:, 6], ACT.Sin, scale=6.283185).then_inc(done["ssm_act"], 1)
            act.wait_ge(done["ssm_act"], nth("ssm_act", 1))
            act.wait_ge(x_loaded, 16)
            stats("x", x_sb, u_flat)

            def tables(g):
                act.wait_ge(done["angle"], nth("angle", g))
                s_ = slice(4 * g, 4 * g + 4)
                act.activation(cos_t[:, s_], sin_t[:, s_], ACT.Abs).then_inc(scalar_step, 1)
                act.wait_ge(scalar_step, step.next())
                act.activation(cos_t[:, s_], cos_t[:, s_], ACT.Sin, scale=-6.283185, bias=half_pi).then_inc(scalar_step, 1)
                act.wait_ge(scalar_step, step.next())
                act.activation(sin_t[:, s_], sin_t[:, s_], ACT.Sin, scale=6.283185).then_inc(done["trig"], 1)
                act.wait_ge(done["trig"], nth("trig", g))
            ahead(("km", 0), 0)
            act.wait_ge(c_loaded, 16)
            act.activation(cc[:, 1], cc[:, 1], ACT.Copy, scale=-1.0).then_inc(scalar_step, 1)
            act.wait_ge(scalar_step, step.next())
            tables(0)
            act.wait_ge(mem_loaded, 16)
            stats("mem", xn, junk_mem)
            for i in range(2):
                copy_out(("ssmT", i), i, bb[:, i].rearrange("p j s -> p (j s)"), signal="ssm_weights")
            turned_hi("mem", full1, m_hi)
            ahead(("km", 1), 1)
            for i, (n, dst, w) in enumerate((("km", km_sb, 512), ("vm", vm_sb, 512), ("kvi", kvi, 452), ("q", q_sb, 512),
                                             ("qm", qm_sb, 512))):
                ahead((n, 1), 2)
                for t in range(2):
                    copy_out((n, t), (n, t), dst[:, t, 0:w], lambda p_: p_[:, 0:w],
                             scale=r_of["mem" if n in ("km", "vm") else "x"][:, t:t + 1])
                if i < 3:
                    tables(1 + i)
            act.wait_ge(done["rope_angle"], nth("rope_angle", 0))
            act.activation(rope_tmp[:, 1], rope_tmp[:, 0], ACT.Abs).then_inc(scalar_step, 1)
            act.wait_ge(scalar_step, step.next())
            r32 = lambda i: rope_tmp[:, i].rearrange("p (t d) -> p t d", d=32)
            act.activation(rope1[:, 0, :, 0:32], r32(1), ACT.Sin, scale=-1.0, bias=half_pi).then_inc(scalar_step, 1)
            act.wait_ge(scalar_step, step.next())
            act.activation(rope1[:, 0, :, 32:64], r32(1), ACT.Sin, scale=-1.0, bias=half_pi).then_inc(scalar_step, 1)
            act.wait_ge(scalar_step, step.next())
            act.activation(rope1[:, 1, :, 0:32], r32(0), ACT.Sin, scale=-1.0).then_inc(scalar_step, 1)
            act.wait_ge(scalar_step, step.next())
            act.activation(rope1[:, 1, :, 32:64], r32(0), ACT.Sin).then_inc(done["rope_trig"], 1)
            act.wait_ge(done["rope_trig"], nth("rope_trig", 0))

            def gate(c, extra=1):
                ahead((("gate", c), 1), extra)
                for t in range(2):
                    copy_out(("gate", c, t), None, gates1[:, t, c, :], scale=r_of["x"][:, t:t + 1])

            for h in range(2):
                act.wait_ge(done["gelu_in"], nth("gelu_in", h))
                act.activation(y_g[:, 2 * h:2 * h + 2], y_g[:, 2 * h:2 * h + 2], ACT.Gelu_apprx_tanh).then_inc(done["gelu"], 1)
                act.wait_ge(done["gelu"], nth("gelu", h))
            gate(0)
            ahead(("glu", 0), 1)
            for h in range(2):
                act.wait_ge(bank_filled[bank_of[("glu", h)]], fills(("glu", h)))
                p_ = psum(("glu", h)).rearrange("p (m s) -> p m s", s=SEQ)
                act.activation(u_f[:, 2 * h:2 * h + 2], p_, ACT.Sigmoid).then_inc(bank_freed[bank_of[("glu", h)]], 1)
                act.wait_ge(bank_freed[bank_of[("glu", h)]], fills(("glu", h)))
                act.sem_inc(done["evacuated"], 1)
            ahead((("gate", 2), 1), 0)
            act.wait_ge(done["meansq"], nth("meansq", "heads1"))
            act.activation(hr[:, 18:34], hs[:, 18:34], ACT.Ln, scale=1.0 / P, bias=eps).then_inc(scalar_step, 1)
            act.wait_ge(scalar_step, step.next())
            act.activation(hr[:, 18:34], hr[:, 18:34], ACT.Exp, scale=-0.5).then_inc(scalar_step, 1)
            act.wait_ge(scalar_step, step.next())
            inverse_root("heads1", hs[:, 0:18], hr[:, 0:18], 64)
            gate(1)
            gate(2)

            def turned_out(name, dst):
                copy_out(name, name, dst, lambda p_: p_.rearrange("p (j s) -> p j s", s=P), signal="heads_turned")

            for t in range(2):
                ts_ = slice(t * P, t * P + P)
                turned_out(("dqT", t), qT[:, :, ts_])
                turned_out(("dkT", t), kT[:, :, ts_])
            for t in range(2):
                for p in range(2):
                    act.wait_ge(bank_filled[bank_of[("isc", t, p)]], fills(("isc", t, p)))
                    p_ = psum(("isc", t, p)).rearrange("p (j s) -> p j s", s=SEQ)
                    act.activation(relu[:, 2 * t + p], p_, ACT.Relu).then_inc(bank_freed[bank_of[("isc", t, p)]], 1)
                    act.wait_ge(bank_freed[bank_of[("isc", t, p)]], fills(("isc", t, p)))
                    act.sem_inc(done["relued"], 1)
            gate(3)

            def attention(tag, pairs, pr, pT, meanwhile):
                for t in range(2):
                    meanwhile(t, 0)
                    act.wait_ge(done["maxed"], nth("maxed", (tag, t)))
                    if tag == "swa":
                        act.activation(snk, snk, ACT.Exp).then_inc(scalar_step, 1)
                        act.wait_ge(scalar_step, step.next())
                    for h in range(2 * pairs):
                        ins = act.activation(pr[:, h, :], pr[:, h, :], ACT.Exp, bias=mx[:, h:h + 1],
                                             accum_out=rs[:, h:h + 1])
                        if h == 2 * pairs - 1:
                            ins.then_inc(done["exped"], 1)
                            act.wait_ge(done["exped"], nth("exped", (tag, t)))
                        else:
                            ins.then_inc(scalar_step, 1)
                            act.wait_ge(scalar_step, step.next())
                    meanwhile(t, 1)
                    for p in range(pairs):
                        act.wait_ge(bank_filled[bank_of[(tag, "PT", t, p)]], fills((tag, "PT", t, p)))
                        p_ = psum((tag, "PT", t, p)).rearrange("p (h s q) -> p s h q", h=2, s=2)
                        act.activation(pT[:, :, 2 * p:2 * p + 2, :], p_, ACT.Copy).then_inc(bank_freed[bank_of[(tag, "PT", t, p)]], 1)
                        act.wait_ge(bank_freed[bank_of[(tag, "PT", t, p)]], fills((tag, "PT", t, p)))
                        act.sem_inc(done["probs_turned"], 1)

            def with_gate(t, when):
                if when == 0:
                    ahead((("gate", 4 + t), 1), 1)
                else:
                    gate(4 + t)

            def with_up(t, when):
                if when == 0:
                    ahead(("up", "ssm", t), 1)
            attention("dsa", 4, probs, probsT, with_gate)
            for t in range(2):
                ts_ = slice(t * P, t * P + P)
                turned_out(("mqT", t), qT[:, :, ts_])
                turned_out(("mkT", t), kT[:, :, ts_])
            attention("mem", 2, probs, probsT, with_up)
            for i, br in enumerate(("ssm", "dsa", "mem")):
                ahead(("up", "dsa", 1), i)
                act.activation(gates1[:, :, 2 * i:2 * i + 2, :], gates1[:, :, 2 * i:2 * i + 2, :], ACT.Sigmoid).then_inc(done["gates"], 1)
                act.wait_ge(done["gates"], nth("gates", br))
            ahead(("up", "mem", 1), 2)
            turned_hi("m")
            ahead((("wo", 1), 1), 1)
            ahead(FIRST, 0)
            turned_hi("f", h_full)
            act.wait_ge(done["residual"], nth("residual", ("wo", 1, 1)))
            stats("f", x_sb, hid[:, :, :].rearrange("p a b -> p (a b)"))
            def silu(k, dst, w, prior, r):
                for t in range(2):
                    if prior is not None:
                        act.wait_ge(done["hidden"], nth("hidden", (*prior, t)))
                    act.wait_ge(bank_filled[bank_of[(*k, "g", t)]], fills((*k, "g", t)))
                    p_ = psum((*k, "g", t))[:, 0:w]
                    act.activation(dst[:, t, 0:w], p_, ACT.Silu, scale=r[:, t:t + 1]).then_inc(bank_freed[bank_of[(*k, "g", t)]], 1)
                    act.wait_ge(bank_freed[bank_of[(*k, "g", t)]], fills((*k, "g", t)))
                    act.sem_inc(done["silu"], 1)

            def route():
                act.wait_ge(done["route_in"], nth("route_in", 0))
                act.activation(rts(0, 4), rts(0, 4), ACT.Exp).then_inc(done["route"], 1)
                act.wait_ge(done["route"], nth("route", "exp"))
                act.wait_ge(done["route_in"], nth("route_in", 1))
                act.activation(rts(5, 1), rts(5, 1), ACT.Exp).then_inc(done["route"], 1)
                act.wait_ge(done["route"], nth("route", "expert"))

            def glu(tag, dst, tail, r):
                L = (tag, "loop")
                regs[tag] = 0
                hi(("u", L, 0))
                hi(("u", L, 1))
                del regs[tag]
                silu((tag, "first"), dst, 512, None, r)
                if tag == "moe":
                    route()
                with act.Fori(0, trips_of(tag)) as i:
                    regs[tag] = i
                    for part in range(2):
                        hi(("g", L, part))
                    hi(("d", L, 0))
                    hi(("d", L, 1))
                    silu(L, dst, 512, L, r)
                    for part in range(2):
                        hi(("u", L, part), units.per[tag])
                    del regs[tag]
                if tail:
                    K, Z = (tag, "last"), (tag, "end")
                    hi(("g", K, 0))
                    hi(("d", K, 0))
                    hi(("d", K, 1))
                    silu(K, dst, tail, K, r)
                    hi(("u", Z, 0))
                    hi(("d", Z, 0))
                    hi(("d", Z, 1))
                else:
                    hi(("d", (tag, "end"), 0))
                    hi(("d", (tag, "end"), 1))

            glu("moe", sil, 0, r_of["f"])
            hid2_flat = hid2[:, :, :].rearrange("p a b -> p (a b)")
            with act.Fori(0, LAYERS) as l:
                regs["layer"] = l
                step.begin(l, SCALAR_STEPS_LAYER)
                stretch, E.cursor = stretch_l1, 0
                ahead(("g", ("ff1", "first"), 1), 0)
                turned_hi("n1", h_full2)
                act.wait_ge(done["residual"], nth("residual", ("ff1", 1, 1)) - 4)
                stats("n1", x_sb, hid2_flat)
                glu("ff1", sil2, TAIL_FF, r_of["n1"])
                stretch, E.cursor = mid, 0
                ahead(mid[0], 1)
                turned_hi("n2", h_full2)
                act.wait_ge(done["residual"], nth("residual", ("ff1", 1, 1)))
                stats("n2", x_sb, hid2_flat)
                act.dma_start(wgl[0:16, :], A["gla_w_gate_2"][l]).then_inc(wgl_loaded, 16)
                ahead(("qa", 1), 1)
                for t in range(2):
                    copy_out(("qa", t), ("qa", t), qa_sb[:, t, :], scale=r_of["n2"][:, t:t + 1])
                ahead(("kva", 0), 1)
                for t in range(2):
                    copy_out(("kva", t), ("kva", t), kva[:, t, :], lambda p_: p_[:, 0:256], scale=r_of["n2"][:, t:t + 1])
                ahead(("qb", 1), 1)
                act.wait_ge(done["meansq"], nth("meansq", "heads2"))
                inverse_root("heads2", hs[:, 0:20], hr[:, 0:20], 64)

                ahead(("kb", 1), 1)
                ahead(("glr", 0), 1)
                for t in range(2):
                    turned_out(("sqT", t), qT2[:, :, t * P:t * P + P])
                copy_out(("skT", 0), ("skT", 0), kT2[:, :, :].rearrange("p g s -> p (g s)"), signal="heads_turned")
                for i in range(2):
                    act.wait_ge(bank_filled[bank_of[("lgT", i)]], fills(("lgT", i)))
                    p_ = psum(("lgT", i))
                    for j in range(2):
                        ins = act.activation(gb_[:, 2 * i + j, :], p_[:, j * SEQ:j * SEQ + SEQ], ACT.Identity,
                                             bias=gate_bias[:, bass.ds(l, 1), 2 * i + j])
                        if j == 1:
                            ins.then_inc(bank_freed[bank_of[("lgT", i)]], 1)
                            act.wait_ge(bank_freed[bank_of[("lgT", i)]], fills(("lgT", i)))
                        else:
                            ins.then_inc(scalar_step, 1)
                            act.wait_ge(scalar_step, step.next())

                def wide(n, c, dst, extra=1):
                    ahead(((n, c), 1), extra)
                    for t in range(2):
                        copy_out((n, c, t), (n, c, t) if n == "vb" else None, dst[:, t, c * 512:c * 512 + 512],
                                 scale=r_of["n2"][:, t:t + 1])

                def with_v(t, when):
                    if when == 0:
                        ahead((("vb", t), 1), 1)
                    else:
                        wide("vb", t, vb)
                attention("swa", 4, probs2, probsT2, with_v)
                ahead((("rb", 0), 1), 0)
                act.wait_ge(done["branch"], nth("branch", ("swa", 1)))
                flat = lambda v: v.rearrange("p a b -> p (a b)")
                act.activation(flat(etmp), flat(gb_), ACT.Abs).then_inc(scalar_step, 1)
                act.wait_ge(scalar_step, step.next())
                act.activation(flat(etmp), flat(etmp), ACT.Exp, scale=-1.0).then_inc(scalar_step, 1)
                act.wait_ge(scalar_step, step.next())
                act.activation(flat(etmp), flat(etmp), ACT.Ln, bias=1.0).then_inc(done["gate_ln"], 1)
                act.wait_ge(done["gate_ln"], nth("gate_ln", 0))
                ahead((("rb", 1), 0), 0)
                act.wait_ge(done["decay"], nth("decay", 0))
                act.activation(flat(gb_), flat(gb_), ACT.Exp, scale=-1.0).then_inc(scalar_step, 1)
                act.wait_ge(scalar_step, step.next())
                ends = etmp[:, :, GLA_CHUNK - 1:SEQ:GLA_CHUNK]
                act.activation(comb4, ends, ACT.Exp).then_inc(done["decay_exp"], 1)
                act.wait_ge(done["decay_exp"], nth("decay_exp", 0))
                wide("rb", 0, rb, 2)
                act.wait_ge(done["decayed"], nth("decayed", "ku"))
                act.activation(flat(gb_), flat(etmp), ACT.Exp).then_inc(done["decay_exp"], 1)
                act.wait_ge(done["decay_exp"], nth("decay_exp", 1))
                act.wait_ge(done["decay"], nth("decay", 1))
                act.activation(flat(gb_), flat(gb_), ACT.Exp).then_inc(done["decay_exp"], 1)
                act.wait_ge(done["decay_exp"], nth("decay_exp", 2))
                ahead((("ga", 0), 0), 0)
                act.wait_ge(done["decay"], nth("decay", 2))
                act.activation(flat(gb_), flat(gb_), ACT.Exp, scale=-1.0).then_inc(done["decay_exp"], 1)
                act.wait_ge(done["decay_exp"], nth("decay_exp", 3))
                wide("rb", 1, rb, 2)
                wide("ga", 0, gab[:, :, 0], 2)
                for t in range(2):
                    copy_out(("gkT", t), t, kk[:, t, :], signal="gk_turned")
                wide("ga", 1, gab[:, :, 0])
                wide("gb", 0, gab[:, :, 1])
                ahead((("gb", 1), 1), 0)
                for t in range(2):
                    for hp in range(2):
                        copy_out(("ob", t, hp), ("ob", t, hp), xn[:, t, hp * 512:hp * 512 + 512])
                ahead(("pa", 0), 0)
                for t in range(2):
                    for h in range(4):
                        ins = act.activation(glrT, xn[:, t, h * SEQ:h * SEQ + SEQ], ACT.Square,
                                             accum_out=hs[:, 4 * t + h:4 * t + h + 1])
                        ins.then_inc(scalar_step, 1)
                        act.wait_ge(scalar_step, step.next())
                inverse_root("o", hs[:, 0:8], hr[:, 0:8], SEQ)
                ahead(("pa", 1), 0)
                act.activation(rb[:, :, :], rb[:, :, :], ACT.Silu).then_inc(done["gates"], 1)
                act.wait_ge(done["gates"], nth("gates", "rb"))
                wide("gb", 1, gab[:, :, 1])
                act.activation(gab[:, :, 0], gab[:, :, 0], ACT.Sigmoid).then_inc(done["gates"], 1)
                act.wait_ge(done["gates"], nth("gates", "ga"))
                act.activation(gab[:, :, 1], gab[:, :, 1], ACT.Sigmoid).then_inc(done["gates"], 1)
                act.wait_ge(done["gates"], nth("gates", "gb"))
                ahead(("pa", 1), 1)
                ahead((("pb", 0), 1), 0)
                turned_hi("o", h_full2)
                ahead((("pb", 1), 1), 2)
                turned_hi("m2")
                ahead((("wo2", 1), 1), 1)
                ahead(mid[-1], 0)
                turned_hi("n3", h_full2)
                act.wait_ge(done["residual"], nth("residual", ("wo2", 1, 1)))
                stats("n3", x_sb, hid2_flat)
                glu("ff2", sil2, TAIL_FF, r_of["n3"])
                step.end(LAYERS)
                del regs["layer"]

        @block.vector
        def _(dve):
            E = Engine(counts_steps=True)
            nth, regs, step, fills, psum = E.nth, E.regs, E.step, E.fills, E.psum
            tt, ts, stt = dve.tensor_tensor, dve.tensor_scalar, dve.scalar_tensor_tensor

            def lo(name, ahead=0):
                dve.wait_ge(hi_split, E.unit_value(name) + 1 + ahead)
                tt(E.view(w_lo, name), E.view(raw, name), E.view(w_hi, name).bitcast(F32), ALU.subtract)\
                    .then_inc(lo_split, 1)

            def ahead(name, extra=1):
                split_ahead(E, stretch, lo, name, extra)

            def split_out(src, hi_, lo_):
                dve.tensor_copy(hi_, src).then_inc(vector_step, 1)
                dve.wait_ge(vector_step, step.next())
                return tt(lo_, src, hi_.bitcast(F32), ALU.subtract)

            def turned(tag, g=None, full=None, to=(a_hi, a_lo), between=None):
                parts = [(hh, t) for hh in range(2) for t in range(2)]
                at = lambda hh, t: (slice(None), slice(4 * hh, 4 * hh + 4), slice(t * P, t * P + P))

                def rest(hh, t):
                    dve.wait_ge(done["turned_hi"], nth("turned_hi", (tag, hh, t)))
                    tt(to[1][at(hh, t)], full[at(hh, t)], to[0][at(hh, t)].bitcast(F32), ALU.subtract)\
                        .then_inc(done["turned"], 1)
                    dve.wait_ge(done["turned"], nth("turned", (tag, hh, t)))
                for i, (hh, t) in enumerate(parts):
                    name = (tag + "T", hh, t)
                    dve.wait_ge(bank_filled[bank_of[name]], fills(name))
                    p_ = psum(name).rearrange("p (k s) -> p k s", s=P)
                    if g is not None:
                        tt(full[at(hh, t)], p_, g[:, 4 * hh:4 * hh + 4].unsqueeze(2).broadcast_to([P, 4, P]), ALU.mult)\
                            .then_inc(bank_freed[bank_of[name]], 1)
                        dve.wait_ge(bank_freed[bank_of[name]], fills(name))
                        dve.sem_inc(done["gained"], 1)
                        if i > 0:
                            rest(*parts[i - 1])
                        if i == 2 and between:
                            ahead(between, 0)
                    else:
                        dve.wait_ge(done["turned_hi"], nth("turned_hi", (tag, hh, t)))
                        tt(to[1][at(hh, t)], p_, to[0][at(hh, t)].bitcast(F32), ALU.subtract)\
                            .then_inc(bank_freed[bank_of[name]], 1)
                        dve.wait_ge(bank_freed[bank_of[name]], fills(name))
                        dve.sem_inc(done["turned"], 1)
                if g is not None:
                    rest(*parts[3])

            stretch = stretch1
            dve.wait_ge(const_loaded, 16)
            turned("x", gain["x"], full1, between=("u", 0))
            ahead(("u", 1), 0)
            dve.wait_ge(par_loaded, 16)
            dve.wait_ge(rows_loaded, 16)
            dve.wait_ge(done["ssm_act"], nth("ssm_act", 0))
            tt(par[:, 4], par[:, 1], par[:, 3], ALU.mult).then_inc(vector_step, 1)
            dve.wait_ge(vector_step, step.next())
            tt(par[:, 5], par[:, 2], par[:, 3], ALU.mult).then_inc(vector_step, 1)
            dve.wait_ge(vector_step, step.next())
            ts(par[:, 6], par[:, 5], 1.0 / TWO_PI, None, ALU.mult).then_inc(vector_step, 1)
            dve.wait_ge(vector_step, step.next())
            ts(par[:, 7], par[:, 6], ROUND, -ROUND, ALU.add, ALU.add).then_inc(vector_step, 1)
            dve.wait_ge(vector_step, step.next())
            tt(par[:, 6], par[:, 6], par[:, 7], ALU.subtract).then_inc(vector_step, 1)
            dve.wait_ge(vector_step, step.next())
            ts(par[:, 7], par[:, 6], COARSE, -COARSE, ALU.add, ALU.add).then_inc(vector_step, 1)
            dve.wait_ge(vector_step, step.next())
            tt(par[:, 8], par[:, 6], par[:, 7], ALU.subtract).then_inc(done["ssm_vec"], 1)
            dve.wait_ge(done["ssm_vec"], nth("ssm_vec", 0))

            def angles(g):
                s_ = slice(4 * g, 4 * g + 4)
                t_b = t_row.unsqueeze(1).broadcast_to([P, 4, SEQ])
                c_, s__ = cos_t[:, s_], sin_t[:, s_]
                per = lambda i: par[:, i, s_].unsqueeze(2).broadcast_to([P, 4, SEQ])
                tt(c_, t_b, per(7), ALU.mult).then_inc(vector_step, 1)
                dve.wait_ge(vector_step, step.next())
                ts(s__, c_, ROUND, -ROUND, ALU.add, ALU.add).then_inc(vector_step, 1)
                dve.wait_ge(vector_step, step.next())
                tt(c_, c_, s__, ALU.subtract).then_inc(vector_step, 1)
                dve.wait_ge(vector_step, step.next())
                tt(s__, t_b, per(8), ALU.mult).then_inc(vector_step, 1)
                dve.wait_ge(vector_step, step.next())
                tt(c_, c_, s__, ALU.add).then_inc(vector_step, 1)
                dve.wait_ge(vector_step, step.next())
                ts(s__, c_, ROUND, -ROUND, ALU.add, ALU.add).then_inc(vector_step, 1)
                dve.wait_ge(vector_step, step.next())
                tt(s__, c_, s__, ALU.subtract).then_inc(done["angle"], 1)
                dve.wait_ge(done["angle"], nth("angle", g))

            angles(0)
            dve.wait_ge(done["ssm_act"], nth("ssm_act", 1))
            tt(par[:, 10], par[:, 10], par[:, 9], ALU.mult).then_inc(vector_step, 1)
            dve.wait_ge(vector_step, step.next())
            ts(par[:, 10], par[:, 10], -1.0, None, ALU.add).then_inc(vector_step, 1)
            dve.wait_ge(vector_step, step.next())
            tt(par[:, 11], par[:, 11], par[:, 9], ALU.mult).then_inc(vector_step, 1)
            dve.wait_ge(vector_step, step.next())
            tt(par[:, 0], par[:, 1], par[:, 1], ALU.mult).then_inc(vector_step, 1)
            dve.wait_ge(vector_step, step.next())
            tt(par[:, 3], par[:, 2], par[:, 2], ALU.mult).then_inc(vector_step, 1)
            dve.wait_ge(vector_step, step.next())
            tt(par[:, 0], par[:, 0], par[:, 3], ALU.add).then_inc(vector_step, 1)
            dve.wait_ge(vector_step, step.next())
            dve.reciprocal(par[:, 0], par[:, 0]).then_inc(vector_step, 1)
            dve.wait_ge(vector_step, step.next())
            tt(par[:, 3], par[:, 10], par[:, 1], ALU.mult).then_inc(vector_step, 1)
            dve.wait_ge(vector_step, step.next())
            tt(par[:, 4], par[:, 11], par[:, 2], ALU.mult).then_inc(vector_step, 1)
            dve.wait_ge(vector_step, step.next())
            tt(par[:, 4], par[:, 3], par[:, 4], ALU.add).then_inc(vector_step, 1)
            dve.wait_ge(vector_step, step.next())
            tt(par[:, 4], par[:, 4], par[:, 0], ALU.mult).then_inc(vector_step, 1)
            dve.wait_ge(vector_step, step.next())
            tt(par[:, 3], par[:, 11], par[:, 1], ALU.mult).then_inc(vector_step, 1)
            dve.wait_ge(vector_step, step.next())
            tt(par[:, 5], par[:, 10], par[:, 2], ALU.mult).then_inc(vector_step, 1)
            dve.wait_ge(vector_step, step.next())
            tt(par[:, 5], par[:, 3], par[:, 5], ALU.subtract).then_inc(vector_step, 1)
            dve.wait_ge(vector_step, step.next())
            tt(par[:, 5], par[:, 5], par[:, 0], ALU.mult).then_inc(done["ssm_vec"], 1)
            dve.wait_ge(done["ssm_vec"], nth("ssm_vec", 1))
            ahead(("km", 0), 0)
            dve.wait_ge(bank_filled[bank_of[("rrow", "x")]], fills(("rrow", "x")))
            dve.tensor_copy(rrow1, psum(("rrow", "x"))[:, 0:SEQ]).then_inc(bank_freed[bank_of[("rrow", "x")]], 1)
            dve.wait_ge(bank_freed[bank_of[("rrow", "x")]], fills(("rrow", "x")))
            for h in range(2):
                dve.wait_ge(bank_filled[bank_of[("uT", h)]], fills(("uT", h)))
                p_ = psum(("uT", h)).rearrange("p (m s) -> p m s", s=SEQ)
                tt(u_f[:, 2 * h:2 * h + 2], p_, rrow1.unsqueeze(1).broadcast_to([P, 2, SEQ]), ALU.mult)\
                    .then_inc(bank_freed[bank_of[("uT", h)]], 1)
                dve.wait_ge(bank_freed[bank_of[("uT", h)]], fills(("uT", h)))
                dve.sem_inc(done["u_rows"], 1)
            turned("mem", gain["mem"], full1, (m_hi, m_lo))
            ahead(("km", 1), 0)
            dve.wait_ge(pos_loaded, 32)
            dve.tensor_copy(pos_row, pos_row_i).then_inc(vector_step, 1)
            dve.wait_ge(vector_step, step.next())
            dve.tensor_copy(pos_col, posi[:, :]).then_inc(vector_step, 1)
            dve.wait_ge(vector_step, step.next())
            ra, rb_ = rope_tmp[:, 0], rope_tmp[:, 1]
            for t in range(2):
                ts(ra[:, 32 * t:32 * t + 32], inv_freq, pos_col[:, t:t + 1], None, ALU.mult).then_inc(vector_step, 1)
                dve.wait_ge(vector_step, step.next())
            ts(rb_, ra, 1.0 / TWO_PI, None, ALU.mult).then_inc(vector_step, 1)
            dve.wait_ge(vector_step, step.next())
            ts(rb_, rb_, ROUND, -ROUND, ALU.add, ALU.add).then_inc(vector_step, 1)
            dve.wait_ge(vector_step, step.next())
            stt(out=ra, in0=rb_, scalar=-6.28125, in1=ra, op0=ALU.mult, op1=ALU.add).then_inc(vector_step, 1)
            dve.wait_ge(vector_step, step.next())
            stt(out=ra, in0=rb_, scalar=-(TWO_PI - 6.28125), in1=ra, op0=ALU.mult, op1=ALU.add).then_inc(vector_step, 1)
            dve.wait_ge(vector_step, step.next())
            ts(ra, ra, 3.1415925, -3.1415925, ALU.min, ALU.max).then_inc(done["rope_angle"], 1)
            dve.wait_ge(done["rope_angle"], nth("rope_angle", 0))
            dve.wait_ge(done["rstd"], nth("rstd", "mem"))
            for T in range(SSM_TILES):
                if T % 4 == 1 and T < 12:
                    angles(1 + T // 4)
                if T % 3 == 0 and T // 3 < len(SCAN_PANELS):
                    ahead((SCAN_PANELS[T // 3], 1), 0 if T == 0 else 1)
                if T % 4 == 0:
                    dve.wait_ge(done["trig"], nth("trig", T // 4))
                dve.wait_ge(bank_filled[bank_of[("bu", T)]], fills(("bu", T)))
                v = psum(("bu", T)).rearrange("p (a s) -> p a s", s=SEQ)
                cosb, sinb = (x_[:, T:T + 1, :].broadcast_to([P, 2, SEQ]) for x_ in (cos_t, sin_t))
                tt(sc_a, v, cosb, ALU.mult).then_inc(vector_step, 1)
                dve.wait_ge(vector_step, step.next())
                tt(sc_b, v, sinb, ALU.mult).then_inc(bank_freed[bank_of[("bu", T)]], 1)
                dve.wait_ge(bank_freed[bank_of[("bu", T)]], fills(("bu", T)))
                tt(sc_a[:, 0], sc_a[:, 0], sc_b[:, 1], ALU.add).then_inc(vector_step, 1)
                dve.wait_ge(vector_step, step.next())
                tt(sc_a[:, 1], sc_a[:, 1], sc_b[:, 0], ALU.subtract).then_inc(vector_step, 1)
                dve.wait_ge(vector_step, step.next())
                if T >= 2:
                    dve.wait_ge(done["rotated"], nth("rotated", T - 2))
                r_ = par[:, 9, T:T + 1].broadcast_to([P, SEQ])
                dve.tensor_tensor_scan(s_rot[:, T % 2, 0], r_, sc_a[:, 0], 0.0, ALU.mult, ALU.add).then_inc(vector_step, 1)
                dve.wait_ge(vector_step, step.next())
                dve.tensor_tensor_scan(s_rot[:, T % 2, 1], r_, sc_a[:, 1], 0.0, ALU.mult, ALU.add).then_inc(done["scanned"], 1)
                dve.wait_ge(done["scanned"], nth("scanned", T))
            ahead((("gate", 0), 1), 0)
            for h in range(2):
                dve.wait_ge(bank_filled[bank_of[("y", h)]], fills(("y", h)))
                p_ = psum(("y", h))
                for j in range(2):
                    ins = stt(out=y_g[:, 2 * h + j], in0=u_f[:, 2 * h + j], scalar=d_skip[:, 2 * h + j:2 * h + j + 1],
                              in1=p_[:, j * SEQ:j * SEQ + SEQ], op0=ALU.mult, op1=ALU.add)
                    if j == 1:
                        ins.then_inc(bank_freed[bank_of[("y", h)]], 1)
                        dve.wait_ge(bank_freed[bank_of[("y", h)]], fills(("y", h)))
                        dve.sem_inc(done["gelu_in"], 1)
                    else:
                        ins.then_inc(vector_step, 1)
                        dve.wait_ge(vector_step, step.next())
            for h in range(2):
                dve.wait_ge(done["gelu"], nth("gelu", h))
                at = (slice(None), slice(2 * h, 2 * h + 2))
                split_out(y_g[at], y_hi[:, 1][at], y_lo[:, 1][at]).then_inc(done["gelu_split"], 1)
                dve.wait_ge(done["gelu_split"], nth("gelu_split", h))
            ahead(("glu", 0), 0)
            dve.wait_ge(done["evacuated"], nth("evacuated", ("glu", 1)))
            tt(y_g[:, :, :], y_g[:, :, :], u_f[:, :, :], ALU.mult).then_inc(vector_step, 1)
            dve.wait_ge(vector_step, step.next())
            split_out(y_g[:, :, :], y_hi[:, 0], y_lo[:, 0]).then_inc(done["branch"], 1)
            dve.wait_ge(done["branch"], nth("branch", "ssm"))

            def rms_heads(src, n, d, at):
                tmp = scr[:, 0:n * d].rearrange("p (h d) -> p h d", d=d)
                if src.ndim == 4:
                    tmp4 = scr[:, 0:n * d].rearrange("p (a h d) -> p a h d", d=d, a=src.shape[1])
                    tt(tmp4, src, src, ALU.mult).then_inc(vector_step, 1)
                    dve.wait_ge(vector_step, step.next())
                else:
                    tt(tmp, src, src, ALU.mult).then_inc(vector_step, 1)
                    dve.wait_ge(vector_step, step.next())
                dve.tensor_reduce(hs[:, at:at + n], tmp, AX, ALU.add).then_inc(vector_step, 1)
                dve.wait_ge(vector_step, step.next())

            def scaled(src, n, d, at, g, last=None):
                ins = tt(src, src, hr[:, at:at + n].unsqueeze(2).broadcast_to([P, n, d]), ALU.mult)
                ins.then_inc(vector_step, 1)
                dve.wait_ge(vector_step, step.next())
                return tt(src, src, g.broadcast_to([P, n, d]), ALU.mult)

            def rope(x4, heads, table):
                n = 2 * heads * 64
                t1 = scr[:, 0:n].rearrange("p (t h d) -> p t h d", t=2, d=64)
                t2 = scrb[:, 0:n].rearrange("p (t h d) -> p t h d", t=2, d=64)
                tab = lambda i, a, b: table[:, i, :, a:b].unsqueeze(2).broadcast_to([P, 2, heads, b - a])
                tt(t1, x4, tab(0, 0, 64), ALU.mult).then_inc(vector_step, 1)
                dve.wait_ge(vector_step, step.next())
                tt(t2[:, :, :, 0:32], x4[:, :, :, 32:64], tab(1, 0, 32), ALU.mult).then_inc(vector_step, 1)
                dve.wait_ge(vector_step, step.next())
                tt(t2[:, :, :, 32:64], x4[:, :, :, 0:32], tab(1, 32, 64), ALU.mult).then_inc(vector_step, 1)
                dve.wait_ge(vector_step, step.next())
                return tt(x4, t1, t2, ALU.add)

            scr, scrb = scr1, area(o_P + 1024, 1024)
            dve.wait_ge(done["evacuated"], nth("evacuated", ("qm", 1)))
            k3 = kvi[:, :, 0:64]
            q3 = q_sb[:, :, :].rearrange("p t (h d) -> p (t h) d", d=64)
            qm3 = qm_sb[:, :, :].rearrange("p t (h d) -> p (t h) d", d=P)
            km3 = km_sb[:, :, :].rearrange("p t (h d) -> p (t h) d", d=P)
            rms_heads(q3, 16, 64, 0)
            rms_heads(k3, 2, 64, 16)
            rms_heads(qm3, 8, P, 18)
            rms_heads(km3, 8, P, 26)
            dve.sem_inc(done["meansq"], 1)
            dve.wait_ge(done["rstd"], nth("rstd", "heads1"))
            dve.wait_ge(done["rope_trig"], nth("rope_trig", 0))
            scaled(q3, 16, 64, 0, g_q1.unsqueeze(1)).then_inc(vector_step, 1)
            dve.wait_ge(vector_step, step.next())
            rope(q_sb[:, :, :].rearrange("p t (h d) -> p t h d", d=64), 8, rope1).then_inc(done["heads"], 1)
            dve.wait_ge(done["heads"], nth("heads", "dq"))
            scaled(k3, 2, 64, 16, g_k1.unsqueeze(1)).then_inc(vector_step, 1)
            dve.wait_ge(vector_step, step.next())
            rope(k3.unsqueeze(2), 1, rope1).then_inc(vector_step, 1)
            dve.wait_ge(vector_step, step.next())
            rope(kvi[:, :, 128:448].rearrange("p t (h d) -> p t h d", d=64), 5, rope1).then_inc(vector_step, 1)
            dve.wait_ge(vector_step, step.next())
            for j in range(2):
                dve.tensor_copy(kdup[:, 0, :, 64 * j:64 * j + 64], k3).then_inc(vector_step, 1)
                dve.wait_ge(vector_step, step.next())
                ins = dve.tensor_copy(kdup[:, 1, :, 64 * j:64 * j + 64], kvi[:, :, 384:448])
                if j == 0:
                    ins.then_inc(vector_step, 1)
                    dve.wait_ge(vector_step, step.next())
            ins.then_inc(done["heads"], 1)
            dve.wait_ge(done["heads"], nth("heads", "dk"))
            scaled(qm3, 8, P, 18, g_qm1.unsqueeze(1)).then_inc(vector_step, 1)
            dve.wait_ge(vector_step, step.next())
            dve.sem_inc(done["heads"], 1)
            scaled(km3, 8, P, 26, g_km1.unsqueeze(1)).then_inc(done["heads"], 1)
            dve.wait_ge(done["heads"], nth("heads", "mk"))
            dve.wait_ge(bank_filled[bank_of[("dqT", 1)]], fills(("dqT", 1)))
            dve.memset(vpad[:, :, :, :], 0.0).then_inc(vector_step, 1)
            dve.wait_ge(vector_step, step.next())
            dve.tensor_copy(vpad[:, :, 0, 0:64], kvi[:, :, 64:128]).then_inc(vector_step, 1)
            dve.wait_ge(vector_step, step.next())
            dve.tensor_copy(vpad[:, :, 1, 64:128], kvi[:, :, 64:128]).then_inc(done["values"], 1)
            dve.wait_ge(done["values"], nth("values", "dsa"))
            for t in range(2):
                ts(allow[:, t], pos_row, pos_col[:, t:t + 1], None, ALU.is_le).then_inc(vector_step, 1)
                dve.wait_ge(vector_step, step.next())
                ts(key_bias[:, t], allow[:, t], -NEG, NEG, ALU.mult, ALU.add).then_inc(vector_step, 1)
                dve.wait_ge(vector_step, step.next())
                for h in range(4):
                    dve.wait_ge(done["relued"], nth("relued", (t, h // 2)))
                    w = kvi[:, t, 448 + h:449 + h]
                    r_ = relu[:, 2 * t + h // 2, h % 2]
                    if h == 0:
                        ts(isc[:, t], r_, w, None, ALU.mult).then_inc(vector_step, 1)
                        dve.wait_ge(vector_step, step.next())
                    else:
                        stt(out=isc[:, t], in0=r_, scalar=w, in1=isc[:, t], op0=ALU.mult, op1=ALU.add).then_inc(vector_step, 1)
                        dve.wait_ge(vector_step, step.next())
                tt(isc[:, t], isc[:, t], key_bias[:, t], ALU.add).then_inc(vector_step, 1)
                dve.wait_ge(vector_step, step.next())
                for r in range(TOPK // 8):
                    dve.max(top8, isc[:, t]).then_inc(vector_step, 1)
                    dve.wait_ge(vector_step, step.next())
                    dve.match_replace(isc[:, t], top8, isc[:, t], GONE).then_inc(vector_step, 1)
                    dve.wait_ge(vector_step, step.next())
                stt(out=key_bias[:, t], in0=isc[:, t], scalar=GONE / 2, in1=allow[:, t], op0=ALU.is_le, op1=ALU.mult).then_inc(vector_step, 1)
                dve.wait_ge(vector_step, step.next())
                ts(key_bias[:, t], key_bias[:, t], -NEG, NEG, ALU.mult, ALU.add).then_inc(vector_step, 1)
                dve.wait_ge(vector_step, step.next())

            def attention(tag, pairs, scale, bias, pr, slot):
                n = 2 * pairs
                for t in range(2):
                    for p in range(pairs):
                        dve.wait_ge(bank_filled[bank_of[(tag, "S", t, p)]], fills((tag, "S", t, p)))
                        p_ = psum((tag, "S", t, p)).rearrange("p (j s) -> p j s", s=SEQ)
                        dst = pr[:, 2 * p:2 * p + 2, :]
                        if bias is None:
                            ts(dst, p_, scale, None, ALU.mult).then_inc(bank_freed[bank_of[(tag, "S", t, p)]], 1)
                            dve.wait_ge(bank_freed[bank_of[(tag, "S", t, p)]], fills((tag, "S", t, p)))
                        else:
                            stt(out=dst, in0=p_, scalar=scale, in1=bias[:, t:t + 1, :].broadcast_to([P, 2, SEQ]),
                                op0=ALU.mult, op1=ALU.add).then_inc(bank_freed[bank_of[(tag, "S", t, p)]], 1)
                            dve.wait_ge(bank_freed[bank_of[(tag, "S", t, p)]], fills((tag, "S", t, p)))
                    dve.tensor_reduce(mx[:, 0:n], pr[:, 0:n, :], AX, ALU.max).then_inc(vector_step, 1)
                    dve.wait_ge(vector_step, step.next())
                    if tag == "swa":
                        sink = sinks[:, bass.ds(regs["layer"], 1), :].rearrange("p a h -> p (a h)")
                        tt(mx, mx, sink, ALU.max).then_inc(vector_step, 1)
                        dve.wait_ge(vector_step, step.next())
                        tt(snk, sink, mx, ALU.subtract).then_inc(vector_step, 1)
                        dve.wait_ge(vector_step, step.next())
                    ts(mx[:, 0:n], mx[:, 0:n], -1.0, None, ALU.mult).then_inc(done["maxed"], 1)
                    dve.wait_ge(done["maxed"], nth("maxed", (tag, t)))
                    dve.wait_ge(done["exped"], nth("exped", (tag, t)))
                    if tag == "swa":
                        tt(rs, rs, snk, ALU.add).then_inc(vector_step, 1)
                        dve.wait_ge(vector_step, step.next())
                    dve.reciprocal(rs[:, 0:n], rs[:, 0:n]).then_inc(vector_step, 1)
                    dve.wait_ge(vector_step, step.next())
                    tt(pr[:, 0:n, :], pr[:, 0:n, :], rs[:, 0:n].unsqueeze(2).broadcast_to([P, n, SEQ]), ALU.mult).then_inc(done["probs"], 1)
                    dve.wait_ge(done["probs"], nth("probs", (tag, t)))
                    dve.wait_ge(bank_filled[bank_of[(tag, "O", t)]], fills((tag, "O", t)))
                    p_ = psum((tag, "O", t)).rearrange("p (i s) -> p i s", s=P)
                    at = (slice(None), slot, slice(0, 4), slice(t * P, t * P + P))
                    split_out(p_, y_hi[at], y_lo[at]).then_inc(bank_freed[bank_of[(tag, "O", t)]], 1)
                    dve.wait_ge(bank_freed[bank_of[(tag, "O", t)]], fills((tag, "O", t)))
                    dve.sem_inc(done["branch"], 1)

            attention("dsa", 4, 0.125, key_bias, probs, 1)
            attention("mem", 2, float(P) ** -0.5, None, probs, 2)
            for i, br in enumerate(("ssm", "dsa", "mem")):
                for c in range(2):
                    dve.wait_ge(done["gates"], nth("gates", br))
                    for t in range(2):
                        dve.wait_ge(bank_filled[bank_of[("up", br, c, t)]], fills(("up", br, c, t)))
                        p_ = psum(("up", br, c, t))
                        dst, g_ = xn[:, t, c * 512:c * 512 + 512], gates1[:, t, 2 * i + c, :]
                        if i == 0:
                            tt(dst, p_, g_, ALU.mult).then_inc(bank_freed[bank_of[("up", br, c, t)]], 1)
                            dve.wait_ge(bank_freed[bank_of[("up", br, c, t)]], fills(("up", br, c, t)))
                        else:
                            tt(gated, p_, g_, ALU.mult).then_inc(bank_freed[bank_of[("up", br, c, t)]], 1)
                            dve.wait_ge(bank_freed[bank_of[("up", br, c, t)]], fills(("up", br, c, t)))
                            ins = tt(dst, dst, gated, ALU.add)
                            if i == 2:
                                ins.then_inc(done["rows"], 1)
                                dve.wait_ge(done["rows"], nth("rows", ("m", c, t)))
                            else:
                                ins.then_inc(vector_step, 1)
                                dve.wait_ge(vector_step, step.next())
            turned("m")

            def residual(tag_of, event, scale=None):
                for c in range(2):
                    for t in range(2):
                        name = tag_of(c, t)
                        dve.wait_ge(bank_filled[bank_of[name]], fills(name))
                        p_, dst = psum(name), x_sb[:, t, c * 512:c * 512 + 512]
                        if scale is None:
                            tt(dst, dst, p_, ALU.add).then_inc(bank_freed[bank_of[name]], 1)
                            dve.wait_ge(bank_freed[bank_of[name]], fills(name))
                        else:
                            stt(out=dst, in0=p_, scalar=scale, in1=dst, op0=ALU.mult, op1=ALU.add).then_inc(bank_freed[bank_of[name]], 1)
                            dve.wait_ge(bank_freed[bank_of[name]], fills(name))
                        dve.sem_inc(done["residual"], 1)
            residual(lambda c, t: ("wo", c, t), "wo")
            turned("f", gain["f"], h_full)
            def hidden(k, dst, gate_, w, weight):
                for t in range(2):
                    dve.wait_ge(bank_filled[bank_of[(*k, "u", t)]], fills((*k, "u", t)))
                    p_ = psum((*k, "u", t))[:, 0:w]
                    dve.wait_ge(done["silu"], marks["hidden"].number((*k, t), regs) + 1)
                    ins = stt(out=dst[:, t, 0:w], in0=p_, scalar=weight(t), in1=gate_[:, t, 0:w], op0=ALU.mult, op1=ALU.mult)
                    ins.then_inc(bank_freed[bank_of[(*k, "u", t)]], 1)
                    dve.wait_ge(bank_freed[bank_of[(*k, "u", t)]], fills((*k, "u", t)))
                    dve.sem_inc(done["hidden"], 1)

            def hidden_turned(k, nb):
                for t in range(2):
                    dve.wait_ge(bank_filled[bank_of[(*k, "hT", t)]], fills((*k, "hT", t)))
                    p_ = psum((*k, "hT", t)).rearrange("p (i s) -> p i s", s=P)[:, 0:nb]
                    at = (slice(None), 0, slice(0, nb), slice(t * P, t * P + P))
                    split_out(p_, y_hi[at], y_lo[at]).then_inc(bank_freed[bank_of[(*k, "hT", t)]], 1)
                    dve.wait_ge(bank_freed[bank_of[(*k, "hT", t)]], fills((*k, "hT", t)))
                    dve.sem_inc(done["hidden_turned"], 1)

            def route():
                dve.wait_ge(done["rstd"], nth("rstd", "f"))
                for t in range(2):
                    dve.wait_ge(bank_filled[bank_of[("rt", t)]], fills(("rt", t)))
                    stt(out=rt[:, t], in0=psum(("rt", t))[:, 0:36], scalar=r_of["f"][:, t:t + 1], in1=b_route, op0=ALU.mult,
                        op1=ALU.add).then_inc(bank_freed[bank_of[("rt", t)]], 1)
                    dve.wait_ge(bank_freed[bank_of[("rt", t)]], fills(("rt", t)))
                bc = lambda v, n: v.broadcast_to([P, 2, n])
                G, Lx = rt[:, :, 0:4], rt[:, :, 4:36]
                dve.tensor_reduce(rts(1, 1), G, AX, ALU.max).then_inc(vector_step, 1)
                dve.wait_ge(vector_step, step.next())
                tt(rts(0, 4), G, bc(rts(1, 1), 4), ALU.subtract).then_inc(done["route_in"], 1)
                dve.wait_ge(done["route_in"], nth("route_in", 0))
                tt(rts(2, 4), G, bc(rts(1, 1), 4), ALU.is_equal).then_inc(vector_step, 1)
                dve.wait_ge(vector_step, step.next())
                tt(rts(2, 4), rts(2, 4), first_key[:, 32:36].unsqueeze(1).broadcast_to([P, 2, 4]), ALU.mult).then_inc(vector_step, 1)
                dve.wait_ge(vector_step, step.next())
                dve.tensor_reduce(rts(1, 1), rts(2, 4), AX, ALU.max).then_inc(vector_step, 1)
                dve.wait_ge(vector_step, step.next())
                tt(rts(2, 4), rts(2, 4), bc(rts(1, 1), 4), ALU.is_equal).then_inc(vector_step, 1)
                dve.wait_ge(vector_step, step.next())
                ts(rts(2, 4), rts(2, 4), -NEG, NEG, ALU.mult, ALU.add).then_inc(vector_step, 1)
                dve.wait_ge(vector_step, step.next())
                tt(rts(3, 32).rearrange("p t (g e) -> p t g e", e=8), Lx.rearrange("p t (g e) -> p t g e", e=8),
                   rts(2, 4).unsqueeze(3).broadcast_to([P, 2, 4, 8]), ALU.add).then_inc(vector_step, 1)
                dve.wait_ge(vector_step, step.next())
                keys = first_key[:, 0:32].unsqueeze(1).broadcast_to([P, 2, 32])

                def best(src, top, sel):
                    dve.tensor_reduce(top, src, AX, ALU.max).then_inc(vector_step, 1)
                    dve.wait_ge(vector_step, step.next())
                    tt(sel, src, bc(top, 32), ALU.is_equal).then_inc(vector_step, 1)
                    dve.wait_ge(vector_step, step.next())
                    tt(sel, sel, keys, ALU.mult).then_inc(vector_step, 1)
                    dve.wait_ge(vector_step, step.next())
                    dve.tensor_reduce(rts(7, 1), sel, AX, ALU.max).then_inc(vector_step, 1)
                    dve.wait_ge(vector_step, step.next())
                    tt(sel, sel, bc(rts(7, 1), 32), ALU.is_equal).then_inc(vector_step, 1)
                    dve.wait_ge(vector_step, step.next())
                best(rts(3, 32), rts(4, 1), rts(8, 32))
                stt(out=rts(3, 32), in0=rts(8, 32), scalar=2 * NEG, in1=rts(3, 32), op0=ALU.mult, op1=ALU.add).then_inc(vector_step, 1)
                dve.wait_ge(vector_step, step.next())
                best(rts(3, 32), rts(5, 1), rts(9, 32))
                tt(rts(5, 1), rts(5, 1), rts(4, 1), ALU.subtract).then_inc(done["route_in"], 1)
                dve.wait_ge(done["route_in"], nth("route_in", 1))
                dve.wait_ge(done["route"], nth("route", "exp"))
                dve.tensor_reduce(rts(6, 1), rts(0, 4), AX, ALU.add).then_inc(vector_step, 1)
                dve.wait_ge(vector_step, step.next())
                dve.wait_ge(done["route"], nth("route", "expert"))
                ts(rts(7, 1), rts(5, 1), 1.0, None, ALU.add).then_inc(vector_step, 1)
                dve.wait_ge(vector_step, step.next())
                tt(rts(6, 1), rts(6, 1), rts(7, 1), ALU.mult).then_inc(vector_step, 1)
                dve.wait_ge(vector_step, step.next())
                dve.reciprocal(rts(6, 1), rts(6, 1)).then_inc(vector_step, 1)
                dve.wait_ge(vector_step, step.next())
                tt(rts(7, 1), rts(6, 1), rts(5, 1), ALU.mult).then_inc(vector_step, 1)
                dve.wait_ge(vector_step, step.next())
                tt(rts(8, 32), rts(8, 32), bc(rts(6, 1), 32), ALU.mult).then_inc(vector_step, 1)
                dve.wait_ge(vector_step, step.next())
                tt(rts(9, 32), rts(9, 32), bc(rts(7, 1), 32), ALU.mult).then_inc(vector_step, 1)
                dve.wait_ge(vector_step, step.next())
                tt(comb, rts(8, 32), rts(9, 32), ALU.add).then_inc(vector_step, 1)
                dve.wait_ge(vector_step, step.next())
                tt(comb, comb, r_of["f"].unsqueeze(2).broadcast_to([P, 2, EXPERTS]), ALU.mult).then_inc(vector_step, 1)
                dve.wait_ge(vector_step, step.next())

            def glu(tag, dst, gate_, tail, steps, weight):
                L = (tag, "loop")
                regs[tag] = 0
                dve.wait_ge(lo_split, E.unit_value(("u", L, 0)))
                lo(("u", L, 0))
                lo(("u", L, 1))
                del regs[tag]
                if tag == "moe":
                    route()
                with dve.Fori(0, trips_of(tag)) as i:
                    regs[tag] = i
                    step.begin(i, steps)
                    lo(("g", L, 0))
                    lo(("g", L, 1))
                    hidden(L, dst, gate_, 512, lambda t: weight(i, t))
                    lo(("d", L, 0))
                    hidden_turned(L, 4)
                    lo(("d", L, 1))
                    lo(("u", L, 0), units.per[tag])
                    lo(("u", L, 1), units.per[tag])
                    step.end(trips_of(tag))
                    del regs[tag]
                Z = (tag, "end")
                if tail:
                    K = (tag, "last")
                    lo(("g", K, 0))
                    hidden(K, dst, gate_, 512, lambda t: weight(0, t))
                    lo(("d", K, 0))
                    hidden_turned(K, 4)
                    lo(("d", K, 1))
                    lo(("u", Z, 0))
                    lo(("d", Z, 0))
                    hidden(Z, dst, gate_, tail, lambda t: weight(0, t))
                    hidden_turned(Z, tail // P)
                    lo(("d", Z, 1))
                else:
                    lo(("d", Z, 0))
                    hidden(Z, dst, gate_, 512, lambda t: weight(EXPERTS - 1, t))
                    hidden_turned(Z, 4)
                    lo(("d", Z, 1))

            glu("moe", hid, sil, 0, 2, lambda e, t: comb[:, t, bass.ds(e, 1)])
            residual(lambda c, t: ("moe", "acc", c, t), "moe")

            with dve.Fori(0, LAYERS) as l:
                regs["layer"] = l
                step.begin(l, VECTOR_STEPS_LAYER)
                g2 = lambda n: gain2[n][:, bass.ds(l, 1), :].rearrange("p a k -> p (a k)")
                turned("n1", g2("n1"), h_full2)
                dve.wait_ge(done["rstd"], nth("rstd", "n1"))
                glu("ff1", hid2, sil2, TAIL_FF, 2, lambda _, t: r_of["n1"][:, t:t + 1])
                lo(("qa", 0))
                lo(("qa", 1))
                residual(lambda c, t: ("ff1", "acc", c, t), "ff1", 0.5)
                turned("n2", g2("n2"), h_full2)
                dve.wait_ge(done["evacuated"], nth("evacuated", ("qa", 1)))
                scr, scrb = scr2, xn[:, 1, :]
                q3 = qa_sb[:, :, :].rearrange("p t (h d) -> p (t h) d", d=64)
                k4 = kva[:, :, 0:128].rearrange("p t (g d) -> p t g d", d=64)
                v4 = kva[:, :, 128:256].rearrange("p t (g d) -> p t g d", d=64)
                rms_heads(q3, 16, 64, 0)
                dve.wait_ge(done["evacuated"], nth("evacuated", ("kva", 1)))
                rms_heads(k4, 4, 64, 16)
                dve.sem_inc(done["meansq"], 1)
                dve.wait_ge(bank_filled[bank_of[("rrow", "n2")]], fills(("rrow", "n2")))
                dve.tensor_copy(rrow2, psum(("rrow", "n2"))[:, 0:SEQ]).then_inc(bank_freed[bank_of[("rrow", "n2")]], 1)
                dve.wait_ge(bank_freed[bank_of[("rrow", "n2")]], fills(("rrow", "n2")))
                gn = lambda i: swa_gain[:, bass.ds(l, 1), i, :]
                dve.wait_ge(done["rstd"], nth("rstd", "heads2"))
                dve.wait_ge(block2_loaded, 64)
                scaled(q3, 16, 64, 0, gn(0)).then_inc(vector_step, 1)
                dve.wait_ge(vector_step, step.next())
                rope(qa_sb[:, :, :].rearrange("p t (h d) -> p t h d", d=64), 8, rope2.rearrange("p t a d -> p a t d")).then_inc(done["heads"], 1)
                dve.wait_ge(done["heads"], nth("heads", "sq"))
                for t in range(2):
                    kt_ = kva[:, t, 0:128].rearrange("p (g d) -> p g d", d=64)
                    tt(kt_, kt_, hr[:, 16 + 2 * t:18 + 2 * t].unsqueeze(2).broadcast_to([P, 2, 64]), ALU.mult).then_inc(vector_step, 1)
                    dve.wait_ge(vector_step, step.next())
                    tt(kt_, kt_, gn(1).broadcast_to([P, 2, 64]), ALU.mult).then_inc(vector_step, 1)
                    dve.wait_ge(vector_step, step.next())
                rope(k4, 2, rope2.rearrange("p t a d -> p a t d")).then_inc(vector_step, 1)
                dve.wait_ge(vector_step, step.next())
                for j in range(2):
                    ins = dve.tensor_copy(kdup2[:, :, :, 64 * j:64 * j + 64], k4.rearrange("p t g d -> p g t d"))
                    if j == 0:
                        ins.then_inc(vector_step, 1)
                        dve.wait_ge(vector_step, step.next())
                ins.then_inc(done["heads"], 1)
                dve.wait_ge(done["heads"], nth("heads", "sk"))
                dve.memset(vpad2[:, :, :, :, :], 0.0).then_inc(vector_step, 1)
                dve.wait_ge(vector_step, step.next())
                dve.tensor_copy(vpad2[:, :, :, 0, 0:64], v4).then_inc(vector_step, 1)
                dve.wait_ge(vector_step, step.next())
                dve.tensor_copy(vpad2[:, :, :, 1, 64:128], v4).then_inc(done["values"], 1)
                dve.wait_ge(done["values"], nth("values", "swa"))
                for n, dst in (("qbT", qbT), ("kbT", kbT)):
                    for h in range(2):
                        dve.wait_ge(bank_filled[bank_of[(n, h)]], fills((n, h)))
                        p_ = psum((n, h)).rearrange("p (m s) -> p m s", s=SEQ)
                        tt(dst[:, 2 * h:2 * h + 2], p_, rrow2.unsqueeze(1).broadcast_to([P, 2, SEQ]), ALU.mult)\
                            .then_inc(bank_freed[bank_of[(n, h)]], 1)
                        dve.wait_ge(bank_freed[bank_of[(n, h)]], fills((n, h)))
                    dve.sem_inc(done["columns"], 1)
                dve.wait_ge(bank_filled[bank_of[("glrT", 0)]], fills(("glrT", 0)))
                tt(glrT[0:16, :], psum(("glrT", 0))[0:16, 0:SEQ], rrow2[0:16, :], ALU.mult)\
                    .then_inc(bank_freed[bank_of[("glrT", 0)]], 1)
                dve.wait_ge(bank_freed[bank_of[("glrT", 0)]], fills(("glrT", 0)))
                dve.sem_inc(done["columns"], 1)
                attention("swa", 4, 0.125, swa_bias, probs2, 0)
                flat = lambda v: v.rearrange("p a b -> p (a b)")
                dve.wait_ge(done["gate_ln"], nth("gate_ln", 0))
                stt(out=flat(gb_), in0=flat(gb_), scalar=0.0, in1=flat(etmp), op0=ALU.min, op1=ALU.subtract).then_inc(vector_step, 1)
                dve.wait_ge(vector_step, step.next())
                ts(flat(gb_), flat(gb_), 1.0 / 16, None, ALU.mult).then_inc(vector_step, 1)
                dve.wait_ge(vector_step, step.next())
                for h in range(4):
                    dve.tensor_tensor_scan(etmp[:, h, :], reset, gb_[:, h, :], 0.0, ALU.mult, ALU.add).then_inc(vector_step, 1)
                    dve.wait_ge(vector_step, step.next())
                chunks = lambda v: v.rearrange("p m (c s) -> p (m c) s", s=GLA_CHUNK)
                ref = lambda i: chunks(etmp)[:, :, i:i + 1].broadcast_to([P, 16, GLA_CHUNK])
                tt(chunks(gb_), chunks(etmp), ref(GLA_CHUNK - 1), ALU.subtract).then_inc(done["decay"], 1)
                dve.wait_ge(done["decay"], nth("decay", 0))
                dve.wait_ge(done["decay_exp"], nth("decay_exp", 0))
                tt(kuT, kbT, gb_, ALU.mult).then_inc(done["decayed"], 1)
                dve.wait_ge(done["decayed"], nth("decayed", "ku"))
                scale = float(P) ** -0.5
                dve.wait_ge(done["decay_exp"], nth("decay_exp", 1))
                stt(out=flat(qqT), in0=flat(qbT), scalar=scale, in1=flat(gb_), op0=ALU.mult, op1=ALU.mult).then_inc(done["decayed"], 1)
                dve.wait_ge(done["decayed"], nth("decayed", "qq"))
                tt(chunks(gb_), chunks(etmp), ref(GLA_CHUNK // 2 - 1), ALU.subtract).then_inc(done["decay"], 1)
                dve.wait_ge(done["decay"], nth("decay", 1))
                dve.wait_ge(done["decay_exp"], nth("decay_exp", 2))
                stt(out=flat(qbT), in0=flat(qbT), scalar=scale, in1=flat(gb_), op0=ALU.mult, op1=ALU.mult).then_inc(done["decayed"], 1)
                dve.wait_ge(done["decayed"], nth("decayed", "q"))
                tt(chunks(gb_), chunks(etmp), ref(GLA_CHUNK // 2 - 1), ALU.subtract).then_inc(done["decay"], 1)
                dve.wait_ge(done["decay"], nth("decay", 2))
                dve.wait_ge(done["decay_exp"], nth("decay_exp", 3))
                tt(flat(kbT), flat(kbT), flat(gb_), ALU.mult).then_inc(done["decayed"], 1)
                dve.wait_ge(done["decayed"], nth("decayed", "k"))
                for t in range(2):
                    dve.wait_ge(bank_filled[bank_of[("A", t)]], fills(("A", t)))
                    p_ = psum(("A", t)).rearrange("p (h s) -> p h s", s=P)
                    tt(am[:, t], p_, gla_mask.unsqueeze(1).broadcast_to([P, 4, P]), ALU.mult).then_inc(bank_freed[bank_of[("A", t)]], 1)
                    dve.wait_ge(bank_freed[bank_of[("A", t)]], fills(("A", t)))
                    dve.sem_inc(done["masked"], 1)
                for c in range(3):
                    for hp in range(2):
                        dve.wait_ge(bank_filled[bank_of[("kv", c, hp)]], fills(("kv", c, hp)))
                        p_ = psum(("kv", c, hp)).rearrange("p (j s) -> p j s", s=SEQ)
                        if c == 0:
                            dve.tensor_copy(state[:, 0, 2 * hp:2 * hp + 2, :], p_).then_inc(bank_freed[bank_of[("kv", c, hp)]], 1)
                            dve.wait_ge(bank_freed[bank_of[("kv", c, hp)]], fills(("kv", c, hp)))
                        else:
                            for j in range(2):
                                h = 2 * hp + j
                                ins = stt(out=state[:, c, h, :], in0=state[:, c - 1, h, :],
                                          scalar=comb4[:, h, c:c + 1], in1=p_[:, j, :], op0=ALU.mult, op1=ALU.add)
                                if j == 0:
                                    ins.then_inc(vector_step, 1)
                                    dve.wait_ge(vector_step, step.next())
                            ins.then_inc(bank_freed[bank_of[("kv", c, hp)]], 1)
                            dve.wait_ge(bank_freed[bank_of[("kv", c, hp)]], fills(("kv", c, hp)))
                    dve.sem_inc(done["state"], 1)
                dve.wait_ge(done["rstd"], nth("rstd", "o"))
                dve.wait_ge(done["gates"], nth("gates", "rb"))
                for hh in range(2):
                    for t in range(2):
                        for h in (2 * hh, 2 * hh + 1):
                            o_h = xn[:, t, h * SEQ:h * SEQ + SEQ]
                            ins = stt(out=o_h, in0=o_h, scalar=hr[:, 4 * t + h:4 * t + h + 1],
                                      in1=rb[:, t, h * SEQ:h * SEQ + SEQ], op0=ALU.mult, op1=ALU.mult)
                            if h % 2 == 0:
                                ins.then_inc(vector_step, 1)
                                dve.wait_ge(vector_step, step.next())
                        ins.then_inc(done["rows"], 1)
                        dve.wait_ge(done["rows"], nth("rows", ("o", hh, t)))
                turned("o", g2("o"), h_full2)
                for i, n in enumerate(("pa", "pb")):
                    for c in range(2):
                        dve.wait_ge(done["gates"], nth("gates", ("ga", "gb")[i]))
                        for t in range(2):
                            dve.wait_ge(bank_filled[bank_of[(n, c, t)]], fills((n, c, t)))
                            p_ = psum((n, c, t))
                            dst, g_ = rb[:, t, c * 512:c * 512 + 512], gab[:, t, i, c * 512:c * 512 + 512]
                            if i == 0:
                                tt(dst, p_, g_, ALU.mult).then_inc(bank_freed[bank_of[(n, c, t)]], 1)
                                dve.wait_ge(bank_freed[bank_of[(n, c, t)]], fills((n, c, t)))
                            else:
                                tt(scr2[:, 0:512], p_, g_, ALU.mult).then_inc(bank_freed[bank_of[(n, c, t)]], 1)
                                dve.wait_ge(bank_freed[bank_of[(n, c, t)]], fills((n, c, t)))
                                ins = tt(dst, dst, scr2[:, 0:512], ALU.add)
                                ins.then_inc(done["rows"], 1)
                                dve.wait_ge(done["rows"], nth("rows", ("m2", c, t)))
                turned("m2")
                residual(lambda c, t: ("wo2", c, t), "wo2")
                turned("n3", g2("n3"), h_full2)
                dve.wait_ge(done["rstd"], nth("rstd", "n3"))
                glu("ff2", hid2, sil2, TAIL_FF, 2, lambda _, t: r_of["n3"][:, t:t + 1])
                residual(lambda c, t: ("ff2", "acc", c, t), "ff2", 0.5)
                step.end(LAYERS)
                del regs["layer"]

        @block.gpsimd
        def _(pool):
            E = Engine(counts_steps=True)
            nth, step = E.nth, E.step
            pool.memset(zero_b[:, :], 0.0).then_inc(zeroed, 1)
            pool.wait_ge(done["ssm_vec"], nth("ssm_vec", 1))
            pool.wait_ge(b_loaded, 16)
            f_re, f_im = (par[:, i].unsqueeze(2).broadcast_to([P, SSM_TILES, 32]) for i in (4, 5))
            b_t = area(o_scan + 1024, SSM_TILES, 32)
            pool.tensor_tensor(bsc[:, 0], bn[:, 0], f_re, ALU.mult).then_inc(pool_step, 1)
            pool.wait_ge(pool_step, step.next())
            pool.tensor_tensor(b_t, bn[:, 1], f_im, ALU.mult).then_inc(pool_step, 1)
            pool.wait_ge(pool_step, step.next())
            pool.tensor_tensor(bsc[:, 0], bsc[:, 0], b_t, ALU.subtract).then_inc(pool_step, 1)
            pool.wait_ge(pool_step, step.next())
            pool.tensor_tensor(bsc[:, 1], bn[:, 1], f_re, ALU.mult).then_inc(pool_step, 1)
            pool.wait_ge(pool_step, step.next())
            pool.tensor_tensor(b_t, bn[:, 0], f_im, ALU.mult).then_inc(pool_step, 1)
            pool.wait_ge(pool_step, step.next())
            pool.tensor_tensor(bsc[:, 1], bsc[:, 1], b_t, ALU.add).then_inc(done["ssm_params"], 1)
            pool.wait_ge(done["ssm_params"], nth("ssm_params", "b"))

            def lo(name):
                pool.wait_ge(hi_split, E.unit_value(name) + 1)
                pool.tensor_tensor(E.view(w_lo, name), E.view(raw, name), E.view(w_hi, name).bitcast(F32), ALU.subtract)\
                    .then_inc(lo_split, 1)

            for T in range(SSM_TILES):
                pool.wait_ge(done["scanned"], nth("scanned", T))
                s_ = s_rot[:, T % 2]
                cosb, sinb = (x_[:, T:T + 1, :].broadcast_to([P, 2, SEQ]) for x_ in (cos_t, sin_t))
                pool.tensor_tensor(sc_p, s_, sinb, ALU.mult).then_inc(pool_step, 1)
                pool.wait_ge(pool_step, step.next())
                pool.tensor_tensor(s_, s_, cosb, ALU.mult).then_inc(pool_step, 1)
                pool.wait_ge(pool_step, step.next())
                if T >= 1:
                    pool.wait_ge(done["mixed"], nth("mixed", T - 1))
                pool.tensor_tensor(s_out[:, 0], s_[:, 0], sc_p[:, 1], ALU.subtract).then_inc(pool_step, 1)
                pool.wait_ge(pool_step, step.next())
                pool.tensor_tensor(s_out[:, 1], s_[:, 1], sc_p[:, 0], ALU.add).then_inc(done["rotated"], 1)
                pool.wait_ge(done["rotated"], nth("rotated", T))
            first = (("gate", 1), 0)
            pool.wait_ge(lo_split, E.unit_value(first))
            for name in stretch1[stretch1.index(first):]:
                lo(name)
            pool.wait_ge(done["residual"], nth("residual", ("wo", 1, 1)))
            pool.dma_start(rope2, A["rope2"].rearrange("(t p) (a d) -> p t a d", p=P, d=64)).then_inc(block2_loaded, 16)
            pool.dma_start(swa_bias, A["swa_bias"].rearrange("(t p) s -> p t s", p=P)).then_inc(block2_loaded, 16)
            pool.dma_start(reset, A["reset"].partition_broadcast(P)).then_inc(block2_loaded, 16)
            pool.dma_start(gla_mask, A["gla_mask"]).then_inc(block2_loaded, 16)
            with pool.Fori(0, LAYERS) as l:
                E.regs["layer"] = l
                pool.wait_ge(lo_split, E.unit_value(stretch_l1[0]))
                for name in stretch_l1:
                    lo(name)
                pool.wait_ge(lo_split, E.unit_value(("kva", 0)))
                for name in mid[2:]:
                    lo(name)
                del E.regs["layer"]


_PACKED = ("g_mem", "g_mix", "g_ffn", "ffn1_norm_2", "mix_norm_2", "ffn2_norm_2", "gla_out_norm_2", "swa_q_norm_2",
           "swa_k_norm_2", "swa_sinks_2", "gla_gate_bias_2", "d_skip", "w_group", "w_expert", "b_group", "b_expert",
           "g_q", "g_k", "g_qm", "g_km", "log_dt", "lam_re", "lam_im", "b_re", "b_im", "c_re", "c_im")


def shape_constants():
    pos = np.arange(SEQ, dtype=np.float32)
    ang = (pos[:, None] * _inv_freq()[None, :]).astype(np.float32)
    cos, sin = np.cos(ang), np.sin(ang)
    q, k = np.arange(SEQ)[:, None], np.arange(SEQ)[None, :]
    s, t = np.arange(P)[:, None], np.arange(P)[None, :]
    return {
        "rope2": np.concatenate([cos, cos, -sin, sin], axis=1).astype(np.float32),
        "swa_bias": np.where((k <= q) & (k > q - 128), 0.0, NEG).astype(np.float32),
        "reset": (np.arange(SEQ) % GLA_CHUNK != 0).astype(np.float32),
        "gla_mask": ((s <= t) & (s // GLA_CHUNK == t // GLA_CHUNK)).astype(np.float32),
    }


def _inv_freq():
    return (1.0 / (10000.0 ** (np.arange(0, 64, 2, dtype=np.float32) / 64))).astype(np.float32)


def packed_inputs(a):
    def columns(v):
        return v.reshape(-1, P).T

    def rows(v):
        return np.tile(v.reshape(1, -1), (P, 1))

    def route(w):
        return w[0].reshape(KB, P, -1).transpose(1, 0, 2)

    def states(v):
        return v[0].reshape(SSM_TILES, 2, 64).transpose(1, 2, 0).reshape(P, SSM_TILES)

    def state_rows(v):
        out = np.zeros((2, 64, SSM_TILES, 2, 16), np.float32)
        for g in range(2):
            out[g, :, :, g, :] = v[0, g::2].transpose(1, 0, 2)
        return out.reshape(P, SSM_TILES * 32)

    key = np.concatenate([np.arange(32, 0, -1), np.arange(8, 0, -1) - 4])
    packed = [np.eye(P), *(columns(a[n]) for n in ("g_mem", "g_mix", "g_ffn", "ffn1_norm_2", "mix_norm_2",
                                                   "ffn2_norm_2", "gla_out_norm_2")),
              rows(np.stack([a["swa_q_norm_2"], a["swa_k_norm_2"]], axis=1)), rows(a["swa_sinks_2"]),
              columns(a["gla_gate_bias_2"]), columns(a["d_skip"]),
              np.concatenate([route(a["w_group"]), route(a["w_expert"])], axis=2).reshape(P, -1),
              rows(np.concatenate([a["b_group"].reshape(-1), a["b_expert"].reshape(-1)])), rows(key),
              np.full((P, 1), 1.5707963), np.full((P, 1), EPS)]
    dt = np.repeat(a["log_dt"][:, :, None], 64, axis=2)
    return {
        "packed": np.concatenate(packed, axis=1).astype(np.float32),
        "ssm_params": np.concatenate([states(dt), states(a["lam_re"]), states(a["lam_im"])], axis=1),
        "ssm_b": np.concatenate([state_rows(a["b_re"]), state_rows(a["b_im"])], axis=1),
        "ssm_c": np.concatenate([state_rows(a[n].transpose(0, 1, 3, 2)) for n in ("c_re", "c_im")], axis=1),
        "head_rows": np.concatenate([np.arange(SEQ, dtype=np.float32), a["g_q"][0], a["g_k"][0], a["g_qm"][0],
                                     a["g_km"][0], _inv_freq()]),
    }


def kernel(**inputs):
    import concourse.bacc as _bacc
    from concourse.bass_utils import run_bass_kernel_spmd as _run

    nc = _bacc.Bacc("TRN2", target_bir_lowering=False, num_devices=1)
    arrays, aps = {}, {}
    inputs = {n: np.asarray(v) for n, v in inputs.items()}
    left = {n: v for n, v in inputs.items() if n not in _PACKED}
    for name, a in {**left, **packed_inputs(inputs), **shape_constants()}.items():
        a = np.ascontiguousarray(a)
        arrays[f"in_{name}"] = a
        aps[name] = nc.dram_tensor(f"in_{name}", a.shape, mybir.dt.from_np(a.dtype), kind="ExternalInput").ap()
    out = nc.dram_tensor("out_x", (1, SEQ, D), F32, kind="ExternalOutput").ap()
    bass_hybrid_moe_then_swa_gla(nc, aps, out)
    r = _run(nc, [arrays], core_ids=[0])
    return r.results[0]["out_x"]
```
